# Optimizing a Trainium2 kernel written in Bass

```python
import jax, jax.numpy as jnp
from jax import lax
import numpy as np

D_MODEL = 1024
BATCH = 1
SEQ = 256
DEPTH = 2

CHUNK = 64
Q_BLOCK = 128
CONV_WIDTH = 1024
CONV_GROUPS = 16
CONV_K = 3
MLA_HEADS = 16
QK_NOPE = 64
QK_ROPE = 32
V_DIM = 64
Q_LORA = 256
KV_LORA = 128
ROPE_THETA = 10000.0
N_BRANCH = 2
D_FF_DENSE = 2816
N_EXPERTS = 8
TOP_K = 2
D_FF_EXPERT = 1792
N_DENSE = (DEPTH + 1) // 2
N_MOE = DEPTH // 2
EPS = 1e-6
IN_SIZES = (CONV_WIDTH, CONV_WIDTH, CONV_WIDTH, Q_LORA, KV_LORA + QK_ROPE, N_BRANCH * D_MODEL)
IN_COLS = sum(IN_SIZES)

kernel_name = "hybrid_shortconv_mla_moe_trunk"

def rmsnorm(x, g):
    xf = x.astype(jnp.float32)
    inv = lax.rsqrt(jnp.mean(xf * xf, axis=-1, keepdims=True) + EPS)
    return (xf * inv).astype(x.dtype) * g

def rope_tables(positions):
    inv_freq = ROPE_THETA ** (-jnp.arange(0, QK_ROPE, 2, dtype=jnp.float32) / QK_ROPE)
    ang = positions.astype(jnp.float32)[..., None] * inv_freq
    return jnp.cos(ang), jnp.sin(ang)

def apply_rope(t, cos, sin):
    t1, t2 = jnp.split(t, 2, axis=-1)
    cos = cos.astype(t.dtype)
    sin = sin.astype(t.dtype)
    return jnp.concatenate([t1 * cos - t2 * sin, t1 * sin + t2 * cos], axis=-1)

def short_conv_mixer(gate_b, gate_c, u, conv_w, w_out):
    z = gate_c * u
    z = lax.conv_general_dilated(
        z, conv_w.astype(z.dtype), window_strides=(1,), padding=[(CONV_K - 1, 0)],
        dimension_numbers=("NWC", "WIO", "NWC"), feature_group_count=CONV_WIDTH)
    return (gate_b * z) @ w_out

def chunk_causal_attention(q_nope, q_rope, k_nope, k_rope, v):
    B, S, H, _ = q_nope.shape
    n_blk = S // Q_BLOCK
    scale = (QK_NOPE + QK_ROPE) ** -0.5
    k_chunk = jnp.arange(S) // CHUNK

    def to_blocks(t):
        return jnp.moveaxis(t.reshape((B, n_blk, Q_BLOCK) + t.shape[2:]), 1, 0)

    def one_block(args):
        blk, qn, qr = args
        s = (jnp.einsum("bqhd,bkhd->bhqk", qn, k_nope).astype(jnp.float32)
             + jnp.einsum("bqhr,bkr->bhqk", qr, k_rope).astype(jnp.float32)) * scale
        q_chunk = (blk * Q_BLOCK + jnp.arange(Q_BLOCK)) // CHUNK
        mask = k_chunk[None, :] <= q_chunk[:, None]
        s = jnp.where(mask[None, None], s, -jnp.inf)
        p = jax.nn.softmax(s, axis=-1).astype(v.dtype)
        return jnp.einsum("bhqk,bkhd->bqhd", p, v)

    o = lax.map(one_block, (jnp.arange(n_blk), to_blocks(q_nope), to_blocks(q_rope)))
    return jnp.moveaxis(o, 0, 1).reshape(B, S, H, V_DIM)

def mla_mixer(c_q, c_kv_full, cos, sin, g_q, g_kv, w_uq, w_ukv, w_o):
    B, S, _ = c_q.shape
    c_q = rmsnorm(c_q, g_q)
    q = (c_q @ w_uq).reshape(B, S, MLA_HEADS, QK_NOPE + QK_ROPE)
    q_nope = q[..., :QK_NOPE]
    q_rope = apply_rope(q[..., QK_NOPE:], cos[:, :, None, :], sin[:, :, None, :])
    c_kv = rmsnorm(c_kv_full[..., :KV_LORA], g_kv)
    k_rope = apply_rope(c_kv_full[..., KV_LORA:], cos, sin)
    kv = (c_kv @ w_ukv).reshape(B, S, MLA_HEADS, QK_NOPE + V_DIM)
    k_nope = kv[..., :QK_NOPE]
    v = kv[..., QK_NOPE:]
    o = chunk_causal_attention(q_nope, q_rope, k_nope, k_rope, v)
    return o.reshape(B, S, MLA_HEADS * V_DIM) @ w_o

def swiglu(t, w_gate, w_up, w_down):
    return (jax.nn.silu(t @ w_gate) * (t @ w_up)) @ w_down

def moe_swiglu(x, w_router, w_gate, w_up, w_down):
    B, S, D = x.shape
    t = x.reshape(B * S, D)
    logits = (t @ w_router).astype(jnp.float32)
    top_vals, top_idx = lax.top_k(logits, TOP_K)
    top_w = jax.nn.softmax(top_vals, axis=-1)
    gates = jnp.sum(jax.nn.one_hot(top_idx, N_EXPERTS, dtype=jnp.float32) * top_w[..., None], axis=1)
    out = jnp.zeros_like(t)
    for e in range(N_EXPERTS):
        out = out + gates[:, e:e + 1].astype(t.dtype) * swiglu(t, w_gate[e], w_up[e], w_down[e])
    return out.reshape(B, S, D)

def setup_inputs(seed: int = 0) -> dict:
    key = jax.random.key(seed)
    ks = jax.random.split(key, 32)

    def nrm(k, shape, fan_in):
        return jax.random.normal(k, shape, jnp.float32) * (fan_in ** -0.5)

    def gain(k, shape):
        return 1.0 + 0.05 * jax.random.normal(k, shape, jnp.float32)

    x = jax.random.normal(ks[0], (BATCH, SEQ, D_MODEL), jnp.float32)
    offset = jax.random.randint(ks[1], (BATCH,), 0, 64, dtype=jnp.int32) * CHUNK
    positions = offset[:, None] + jnp.arange(SEQ, dtype=jnp.int32)[None, :]
    H = MLA_HEADS
    return {
        "x": x,
        "positions": positions,
        "norm_mix": gain(ks[2], (DEPTH, D_MODEL)),
        "w_in": nrm(ks[3], (DEPTH, D_MODEL, IN_COLS), D_MODEL),
        "b_gate": 0.02 * jax.random.normal(ks[4], (DEPTH, N_BRANCH * D_MODEL), jnp.float32),
        "conv_w": nrm(ks[5], (DEPTH, CONV_K, 1, CONV_WIDTH), CONV_K),
        "w_conv_out": nrm(ks[6], (DEPTH, CONV_WIDTH, D_MODEL), CONV_WIDTH),
        "norm_q": gain(ks[7], (DEPTH, Q_LORA)),
        "norm_kv": gain(ks[8], (DEPTH, KV_LORA)),
        "w_uq": nrm(ks[9], (DEPTH, Q_LORA, H * (QK_NOPE + QK_ROPE)), Q_LORA),
        "w_ukv": nrm(ks[10], (DEPTH, KV_LORA, H * (QK_NOPE + V_DIM)), KV_LORA),
        "w_attn_out": nrm(ks[11], (DEPTH, H * V_DIM, D_MODEL), H * V_DIM),
        "w_mix_out": nrm(ks[12], (DEPTH, D_MODEL, D_MODEL), D_MODEL),
        "norm_ffn": gain(ks[13], (DEPTH, D_MODEL)),
        "dense_w_gate": nrm(ks[14], (N_DENSE, D_MODEL, D_FF_DENSE), D_MODEL),
        "dense_w_up": nrm(ks[15], (N_DENSE, D_MODEL, D_FF_DENSE), D_MODEL),
        "dense_w_down": nrm(ks[16], (N_DENSE, D_FF_DENSE, D_MODEL), D_FF_DENSE),
        "router_w": nrm(ks[17], (N_MOE, D_MODEL, N_EXPERTS), D_MODEL),
        "moe_w_gate": nrm(ks[18], (N_MOE, N_EXPERTS, D_MODEL, D_FF_EXPERT), D_MODEL),
        "moe_w_up": nrm(ks[19], (N_MOE, N_EXPERTS, D_MODEL, D_FF_EXPERT), D_MODEL),
        "moe_w_down": nrm(ks[20], (N_MOE, N_EXPERTS, D_FF_EXPERT, D_MODEL), D_FF_EXPERT),
        "norm_final": gain(ks[21], (D_MODEL,)),
    }

def reference(x, positions, norm_mix, w_in, b_gate, conv_w, w_conv_out, norm_q, norm_kv,
              w_uq, w_ukv, w_attn_out, w_mix_out, norm_ffn, dense_w_gate, dense_w_up,
              dense_w_down, router_w, moe_w_gate, moe_w_up, moe_w_down, norm_final):
    cos, sin = rope_tables(positions)
    split_at = [int(v) for v in np.cumsum(IN_SIZES)[:-1]]
    h = x
    for layer in range(DEPTH):
        xn = rmsnorm(h, norm_mix[layer])
        proj = xn @ w_in[layer]
        gate_b, gate_c, u, c_q, c_kv_full, gate_logits = jnp.split(proj, split_at, axis=-1)
        y_a = short_conv_mixer(gate_b, gate_c, u, conv_w[layer], w_conv_out[layer])
        y_b = mla_mixer(c_q, c_kv_full, cos, sin, norm_q[layer], norm_kv[layer],
                        w_uq[layer], w_ukv[layer], w_attn_out[layer])
        g_a, g_b = jnp.split(jax.nn.sigmoid(gate_logits + b_gate[layer]), N_BRANCH, axis=-1)
        h = h + (g_a * y_a + g_b * y_b) @ w_mix_out[layer]
        xn = rmsnorm(h, norm_ffn[layer])
        i = layer // 2
        if layer % 2 == 0:
            f = swiglu(xn, dense_w_gate[i], dense_w_up[i], dense_w_down[i])
        else:
            f = moe_swiglu(xn, router_w[i], moe_w_gate[i], moe_w_up[i], moe_w_down[i])
        h = h + f
    return rmsnorm(h, norm_final)


_drawn_inputs = setup_inputs


def setup_inputs(seed=0):
    import zlib

    import numpy as np

    out = dict(_drawn_inputs(seed))
    spreads = {}
    factors = {'norm_q': 2.828, 'norm_kv': 3.466}
    for name, (base, spread) in spreads.items():
        noise = np.random.default_rng([zlib.crc32(name.encode()), seed]).standard_normal(out[name].shape)
        drawn = base * np.exp(spread * noise) if base else spread * noise
        out[name] = __import__('jax').numpy.asarray(drawn.astype(out[name].dtype))
    for name, factor in factors.items():
        out[name] = (out[name] * factor).astype(out[name].dtype)
    return out
```

```python
from contextlib import ExitStack

import concourse.bass as bass
import numpy as np
from concourse import mybir

F32 = mybir.dt.float32
F32R = mybir.dt.float32r
I32 = mybir.dt.int32
U32 = mybir.dt.uint32
ACT = mybir.ActivationFunctionType
ALU = mybir.AluOpType
AX = mybir.AxisListType.X
ds = bass.ds

P = 128
D = 1024
KC = D // P
S = 256
NT = S // P
DEPTH = 2
CHUNK = 64
CONV_K = 3
HEADS, NOPE, ROPE, VD = 16, 64, 32, 64
QK = NOPE + ROPE
RH = ROPE // 2
Q_LORA, KV_LORA = 256, 128
LAT = Q_LORA + KV_LORA + ROPE
LC = (Q_LORA + KV_LORA) // P
F_DENSE, F_EXPERT, EXPERTS = 2816, 1792, 8
EPS = 1e-6
THETA = 10000.0
SCALE = float(QK) ** -0.5
MASKED = -1e30
NB = 512
HB = 256
HC = HB // P
SLOT = 2048
G_CHUNKS = ((0, 3), (3, 3), (6, 2))
COL_B, COL_C, COL_U, COL_LAT, COL_G = 0, D, 2 * D, 3 * D, 3 * D + LAT

BLK_LAT, BLK_CU, BLK_B, BLK_CONV, BLK_UQ, BLK_UKV, BLK_GATE, BLK_ATT, BLK_MIX, MIXER = 0, 1, 5, 7, 9, 10, 11, 15, 17, 19
DENSE, EXPERT = F_DENSE // HB, F_EXPERT // HB
MIX = (0, MIXER + DENSE)
FFN = (MIXER, 2 * MIXER + DENSE)

SLAB_SIZES = tuple(n * NB for _, n in G_CHUNKS)
LAT_SIZES = tuple(n * LAT for _, n in G_CHUNKS)
UQ_SIZES = (2 * NB,) * 3
UKV_SIZES = (2 * NB, NB, NB)
FFN_SIZES = (SLOT,) * 3


def mixer_sizes(b):
    return {BLK_LAT: LAT_SIZES, BLK_UQ: UQ_SIZES, BLK_UKV: UKV_SIZES, MIXER: FFN_SIZES}.get(b, SLAB_SIZES)


def raw_value(block, j, first):
    if j == 2:
        return 16 * (block + 1)
    doubled = {MIX[0]: 0, FFN[0]: 0, MIX[1]: DENSE, FFN[1]: DENSE}[first]
    return 16 * (first + doubled) + (32 if first in FFN else 16) * (block - first + 1)


PAIR_CU, PAIR_B, PAIR_CONV, PAIR_UQ, PAIR_UKV, PAIR_GATE, PAIR_ATT, PAIR_MIX, PAIRS = 0, 4, 6, 8, 11, 15, 19, 21, 23


def build_trunk(nc, x, positions, norm_mix, w_in, b_gate, conv_w, w_conv_out, norm_q, norm_kv, w_uq, w_ukv,
                w_attn_out, w_mix_out, norm_ffn, dense_w_gate, dense_w_up, dense_w_down, router_w,
                moe_w_gate, moe_w_up, moe_w_down, norm_final, out):
    ctx = ExitStack()
    with ctx:
        sizeof = 4
        at = [(nc.sbuf_base + 31) // 32 * 32]

        def place(name, shape, dt=F32):
            t = nc.alloc_sbuf_tensor_at(name, shape, dt, offset=at[0])
            at[0] += (int(np.prod(shape[1:])) * sizeof + 31) // 32 * 32
            return t

        def regions(*groups):
            start, end, got = at[0], at[0], []
            for group in groups:
                at[0] = start
                got += [place(*t) for t in group]
                end = max(end, at[0])
            at[0] = end
            return got

        def sem(name):
            return ctx.enter_context(nc.semaphore(name))

        raw = place("raw", [P, 2, 3, SLOT])
        w_hi = place("w_hi", [P, 3, SLOT], F32R)
        w_lo = place("w_lo", [P, 3, SLOT], F32R)
        h = place("h", [P, NT, D])
        aT_hi = place("aT_hi", [P, KC, S], F32R)
        aT_lo = place("aT_lo", [P, KC, S], F32R)
        ident = place("ident", [P, P])
        mask = place("mask", [P, 3 * P])
        cos = place("cos", [P, NT, RH])
        sin = place("sin", [P, NT, RH])
        NCOL = DEPTH * (CONV_K * KC + LC)
        cols = place("cols", [P, NCOL])
        rwt = place("rwt", [P, KC * EXPERTS])
        rw_hi = place("rw_hi", [P, KC * EXPERTS], F32R)
        rw_lo = place("rw_lo", [P, KC * EXPERTS], F32R)
        expert_gate = place("expert_gate", [P, NT, EXPERTS])
        rope_k = place("rope_k", [P, 4, NT, RH])
        k_rope = place("k_rope", [P, NT, ROPE])
        small = place("small", [P, 64])
        sq_sum, var, rstd = small[:, 0:2], small[:, 2:4], small[:, 4:6]
        lat_sq, lat_var, lat_rstd = small[:, 6:10], small[:, 10:14], small[:, 14:18]
        minus_half = small[:, 18:22]
        neg_max = small[:, 22:24]
        row_sum = small[:, 24:26]
        row_inv = (small[:, 26:28], small[:, 32:34])
        lat_scale = small[:, 28:32]
        mixed = place("mixed", [P, NT, D])
        gates = place("gates", [P, NT, 2 * D])
        xs, lT_hi, lT_lo = regions(
            [("xs", [P, NT, D])],
            [("lT_hi", [P, LC, S], F32R), ("lT_lo", [P, LC, S], F32R)])
        (proj, zT, q, k, v, sg, hid, hT_hi, hT_lo, rt, gain, ang, turns, rowc, pos_i, posf, freq) = regions(
            [("proj", [P, 3, NT, D]), ("zT", [P, KC, S])],
            [("q", [P, NT, HEADS * QK]), ("k", [P, NT, HEADS * QK]), ("v", [P, NT, HEADS * VD])],
            [("sg", [P, NT, HB]), ("hid", [P, NT, HB]),
             ("hT_hi", [P, HC, S], F32R), ("hT_lo", [P, HC, S], F32R),
             ("rt", [P, NT, 9, EXPERTS]),
             ("gain", [P, D])],
            [("ang", [P, 4, NT, RH]), ("turns", [P, 4, NT, RH]), ("rowc", [NCOL, P]),
             ("pos_i", [P, NT], I32), ("posf", [P, NT]), ("freq", [P, RH])])
        acc = proj[:, 1, :, :].rearrange("p t (c s) -> p (t c) s", s=S)
        bT_hi, bT_lo, qkT, s_buf, p_buf, pT, rope_t = regions(
            [("bT_hi", [P, KC, S], F32R), ("bT_lo", [P, KC, S], F32R)],
            [("qkT", [P, 2 * S]), ("s_buf", [P, 3 * P]), ("p_buf", [P, 3 * P]), ("pT", [P, 3 * P]),
             ("rope_t", [P, 4, HEADS, RH])])
        assert at[0] <= nc.sbuf_usable_end, at[0] - nc.sbuf_usable_end

        bank = [ctx.enter_context(nc.psum_tensor(f"bank{i}", [P, NB], F32)) for i in range(8)]
        B_QK, B_S, B_PT, B_O = 4, 5, 6, 7
        B_T = 4
        B_LAT, B_LT = 4, 6

        raw_in = [sem(f"raw_in{j}") for j in range(3)]
        hi_made = [sem(f"hi_made{j}") for j in range(3)]
        lo_made = [sem(f"lo_made{j}") for j in range(3)]
        used = [sem(f"used{j}") for j in range(3)]
        h_in, rows_in, gain_in, bias_in, router_in, pos_in = (sem(n) for n in (
            "h_in", "rows_in", "gain_in", "bias_in", "router_in", "pos_in"))
        ident_made, consts_made, cols_tr, cols_made = (sem(n) for n in ("ident_made", "consts_made", "cols_tr", "cols_made"))
        sq_act, sq_dve, rstd_made, xs_made = (sem(n) for n in ("sq_act", "sq_dve", "rstd_made", "xs_made"))
        tr_made, tr_hi, tr_lo = (sem(n) for n in ("tr_made", "tr_hi", "tr_lo"))
        out_made, act_out, dve_out = sem("out_made"), [sem("act_out0"), sem("act_out1")], [sem("dve_out0"), sem("dve_out1")]
        lat_squared, lat_rstd_made, lat_scaled, lat_tr, lat_hi, lat_lo = (sem(n) for n in (
            "lat_squared", "lat_rstd_made", "lat_scaled", "lat_tr", "lat_hi", "lat_lo"))
        z_made, z_tr, z_in, b_tr, prod_made, prod_hi, prod_lo = (sem(n) for n in (
            "z_made", "z_tr", "z_in", "b_tr", "prod_made", "prod_hi", "prod_lo"))
        heads_ready, kv_act, qk_tr, qk_in, s_made, max_made, p_made, p_tr, p_in, o_made, o_in = (sem(n) for n in (
            "heads_ready", "kv_act", "qk_tr", "qk_in", "s_made", "max_made", "p_made", "p_tr", "p_in", "o_made", "o_in"))
        s_read, inv_made, gate_made, m_made = (sem(n) for n in (
            "s_read", "inv_made", "gate_made", "m_made"))
        gu_made, silu_made, hid_made, hid_tr, hT_hi_made, hT_lo_made, h_new = (sem(n) for n in (
            "gu_made", "silu_made", "hid_made", "hid_tr", "hT_hi_made", "hT_lo_made", "h_new"))
        logits_made, lmax_made, lexp_made, rw_hi_made, rw_lo_made, angle_made, sines_made = (sem(n) for n in (
            "logits_made", "lmax_made", "lexp_made", "rw_hi_made", "rw_lo_made", "angle_made", "sines_made"))
        dve_link, pool_link, act_link, stored = (sem(n) for n in ("dve_link", "pool_link", "act_link", "stored"))

        B_GU, B_HT = 4, 6
        OUTS = 1 + PAIRS
        def dve_value(L, pair, t):
            first = (PAIR_UKV, PAIR_GATE)[t]
            return (PAIRS - first) * L + pair - first + 1

        def wait_residual(eng, N):
            if N == 0:
                eng.wait_ge(h_in, 16)
            elif N % 2:
                for t in range(NT):
                    eng.wait_ge(dve_out[t], dve_value(N // 2, PAIRS - 1, t))
            else:
                eng.wait_ge(h_new, (4, 4 + 4 * EXPERTS)[N // 2 - 1])

        def wait_out(eng, L, pair, t):
            if pair == PAIR_UKV and t == 1:
                pair, t = pair + 1, 0
            if t == 0:
                eng.wait_ge(out_made, OUTS * L + 1 + pair + 1)
            else:
                b, j = ((BLK_CU + pair, 2) if pair < PAIR_UQ else (BLK_UQ, pair - PAIR_UQ) if pair < PAIR_UKV else
                        (BLK_UKV, pair - PAIR_UKV - 1) if pair < PAIR_GATE else (BLK_GATE + pair - PAIR_GATE, 2))
                eng.wait_ge(used[j], MIX[L] + b + 1)

        def wait_pair_free(eng, L, pair, t):
            p = pair - 2
            if p < 0:
                return
            if p < PAIR_UKV or (p < PAIR_GATE and t == 1):
                eng.wait_ge(act_out[t], (PAIR_UKV, PAIR_GATE)[t] * L + p + 1)
            else:
                eng.wait_ge(dve_out[t], dve_value(L, p, t))

        block = ctx.enter_context(nc.Block())

        @block.sync
        def _(sp):
            loaded_reg = sp.alloc_register("loaded")

            def load(b, j, first, parts, settled=False):
                at_span_start = isinstance(b, int) and b == first
                before = {FFN[0]: MIX[0], MIX[1]: FFN[0], FFN[1]: MIX[1]}.get(first) if at_span_start else first
                loaded = raw_value(b - 1, j, before) if settled or b >= 1 else None
                if not isinstance(b, int):
                    sp.reg_mov(loaded_reg, loaded)
                    loaded = sp.snap(loaded_reg)
                if settled or b >= 2:
                    sp.wait_ge(lo_made[j], b - 1)
                if settled or b >= 1:
                    sp.wait_ge(raw_in[j], loaded)
                for dst, src in parts:
                    sp.dma_start(dst, src).then_inc(raw_in[j], 16)

            def slot(b, j, n, width):
                return raw[:, b % 2, j, 0:n * width].rearrange("p (c n) -> p c n", n=width)

            def slab(b, first, w, col, width=NB):
                for j, (c0, n) in enumerate(G_CHUNKS):
                    load(b, j, first, [(slot(b, j, n, width), w[:, c0:c0 + n, col:col + width])])

            def chunks(w):
                return w.rearrange("(c p) n -> p c n", p=P)

            def gate_up(b, i, first, w_gate, w_up, settled):
                for j in range(2):
                    dst = raw[:, b % 2, j, :].rearrange("p (c w n) -> p c w n", w=2, n=HB)
                    load(b, j, first, [(dst[:, :, n, :], w[:, 4 * j:4 * j + 4, ds(i * HB, HB)])
                                       for n, w in enumerate((w_gate, w_up))], settled)

            def down(b, i, first, w_down):
                load(b, 2, first, [(slot(b, 2, HC, D), w_down[:, ds(i * HC, HC), :])], True)

            def ffn(F, first, n, w_gate, w_up, w_down):
                gate_up(F, 0, first, w_gate, w_up, True)
                with sp.Fori(1, n) as i:
                    gate_up(F + i, i, first, w_gate, w_up, True)
                    down(F + i - 1, i - 1, first, w_down)
                down(F + n - 1, n - 1, first, w_down)

            sp.dma_start(h[:, :, :], x[0].rearrange("(t p) d -> p t d", p=P)).then_inc(h_in, 16)
            for L in range(DEPTH):
                B = MIX[L]
                w_in_c = chunks(w_in[L])
                slab(B + BLK_LAT, B, w_in_c, COL_LAT, LAT)
                for s, col in enumerate((COL_C, COL_C + NB, COL_U, COL_U + NB, COL_B, COL_B + NB)):
                    slab(B + BLK_CU + s, B, w_in_c, col)
                for u in range(2):
                    slab(B + BLK_CONV + u, B, chunks(w_conv_out[L]), u * NB)
                for j in range(3):
                    b = B + BLK_UQ
                    load(b, j, B, [(slot(b, j, 2, NB), chunks(w_uq[L])[:, :, j * NB:(j + 1) * NB])])
                for j, (c0, n) in enumerate(((0, 2), (2, 1), (3, 1))):
                    b = B + BLK_UKV
                    load(b, j, B, [(raw[:, b % 2, j, 0:n * NB], w_ukv[L][:, c0 * NB:(c0 + n) * NB])])
                for g in range(4):
                    slab(B + BLK_GATE + g, B, w_in_c, COL_G + g * NB)
                for u in range(2):
                    slab(B + BLK_ATT + u, B, chunks(w_attn_out[L]), u * NB)
                for u in range(2):
                    slab(B + BLK_MIX + u, B, chunks(w_mix_out[L]), u * NB)
                if L == 0:
                    ffn(FFN[0], FFN[0], DENSE, chunks(dense_w_gate[0]), chunks(dense_w_up[0]), chunks(dense_w_down[0]))
                else:
                    eg = moe_w_gate[0].rearrange("e (c p) n -> p (e c) n", p=P)
                    eu = moe_w_up[0].rearrange("e (c p) n -> p (e c) n", p=P)
                    ed = moe_w_down[0].rearrange("e (c p) n -> p (e c) n", p=P)

                    def expert_gate_up(e, b, i):
                        for j in range(2):
                            dst = raw[:, b % 2, j, :].rearrange("p (c w n) -> p c w n", w=2, n=HB)
                            load(b, j, FFN[1], [(dst[:, :, n, :], w[:, ds(e * KC + 4 * j, 4), ds(i * HB, HB)])
                                                for n, w in enumerate((eg, eu))], True)

                    with sp.Fori(0, EXPERTS) as e:
                        F = FFN[1] + EXPERT * e
                        if True:
                            expert_gate_up(e, F, 0)
                        for i in range(1, EXPERT):
                            expert_gate_up(e, F + i, i)
                            b = F + i - 1
                            load(b, 2, FFN[1], [(slot(b, 2, HC, D), ed[:, ds(e * 2 * EXPERT + HC * (i - 1), HC), :])], True)
                        b = F + EXPERT - 1
                        load(b, 2, FFN[1], [(slot(b, 2, HC, D), ed[:, ds(e * 2 * EXPERT + HC * (EXPERT - 1), HC), :])], True)
            sp.wait_ge(xs_made, 10)
            sp.dma_start(out[0].rearrange("(t p) d -> p t d", p=P), xs[:, :, :]).then_inc(stored, 16)
            sp.wait_ge(stored, 16)

        @block.gpsimd
        def _(pool):
            links = [0]

            def link(ins):
                links[0] += 1
                ins.then_inc(pool_link, 1)
                pool.wait_ge(pool_link, links[0])

            for L in range(DEPTH):
                taps = CONV_K * KC
                pool.dma_start(rowc[L * taps:(L + 1) * taps, :], conv_w[L].rearrange("k o (c p) -> (k o c) p", p=P)).then_inc(rows_in, 16)
                r = DEPTH * taps + L * LC
                pool.dma_start(rowc[r:r + 2, :], norm_q[L].rearrange("(c p) -> c p", p=P)).then_inc(rows_in, 16)
                pool.dma_start(rowc[r + 2:r + 3, :], norm_kv[L].rearrange("(c p) -> c p", p=P)).then_inc(rows_in, 16)
            pool.dma_start(gain[:, :], norm_mix[0].partition_broadcast(P)).then_inc(gain_in, 16)
            for t in range(NT):
                pool.dma_start(pos_i[:, t:t + 1], positions[0, t * P:(t + 1) * P].rearrange("(p o) -> p o", o=1)).then_inc(pos_in, 16)
            link(pool.memset(ident[:, :], 0.0))
            pool.affine_select(out=ident[:, :], in_=ident[:, :], compare_op=ALU.not_equal, fill=1.0, base=0,
                               pattern=[[-1, P]], channel_multiplier=1).then_inc(ident_made, 1)
            link(pool.memset(mask[:, :], 0.0))
            pool.memset(mask[0:CHUNK, CHUNK:P], MASKED)
            pool.memset(mask[0:CHUNK, 2 * P + CHUNK:3 * P], MASKED)
            pool.memset(minus_half, -0.5)
            pool.memset(lat_scale[:, 0:2], 1.0 / Q_LORA)
            pool.memset(lat_scale[:, 2:4], 1.0 / KV_LORA)
            inv_freq = np.float32(THETA) ** (-np.arange(0, ROPE, 2, dtype=np.float32) / np.float32(ROPE))
            for n in range(RH):
                last = pool.memset(freq[:, n:n + 1], float(inv_freq[n]))
            last.then_inc(consts_made, 1)
            pool.dma_start(rwt[:, :].rearrange("p (c e) -> p c e", e=EXPERTS),
                           router_w[0].rearrange("(c p) e -> p c e", p=P)).then_inc(router_in, 16)
            pool.dma_start(gates[:, 0, :], b_gate[0].partition_broadcast(P)).then_inc(bias_in, 16)
            pool.dma_start(gates[:, 1, :], b_gate[0].partition_broadcast(P)).then_inc(bias_in, 16)

            def norm_root(N, next_gain):
                pool.wait_ge(sq_act, N + 1)
                pool.wait_ge(sq_dve, N + 1)
                link(pool.tensor_scalar(var, sq_sum, 1.0 / D, EPS, ALU.mult, ALU.add))
                pool.tensor_tensor(rstd, var, minus_half[:, 0:2], ALU.pow).then_inc(rstd_made, 1)
                if next_gain is not None:
                    pool.wait_ge(xs_made, 2 * N + 2)
                    pool.dma_start(gain[:, :], next_gain.partition_broadcast(P)).then_inc(gain_in, 16)

            for L in range(DEPTH):
                norm_root(2 * L, None)
                pool.wait_ge(lat_squared, 4 * (L + 1))
                link(pool.tensor_tensor(lat_var, lat_sq, lat_scale, ALU.mult))
                link(pool.tensor_scalar(lat_var, lat_var, EPS, None, ALU.add))
                pool.tensor_tensor(lat_rstd, lat_var, minus_half, ALU.pow).then_inc(lat_rstd_made, 1)
                pool.wait_ge(o_made, HEADS * (L + 1))
                pool.dma_start(gain[:, :], norm_ffn[L].partition_broadcast(P)).then_inc(gain_in, 16)
                norm_root(2 * L + 1, norm_mix[1] if L == 0 else norm_final)
                if L == 0:
                    pool.wait_ge(m_made, 4)
                    for t in range(NT):
                        pool.dma_start(gates[:, t, :], b_gate[1].partition_broadcast(P)).then_inc(bias_in, 16)
            norm_root(4, None)

        @block.scalar
        def _(act):
            def hi(b, j, n, first, settled=False):
                act.wait_ge(raw_in[j], raw_value(b, j, first))
                if settled or b >= 1:
                    act.wait_ge(used[j], b)
                act.activation(w_hi[:, j, 0:n], raw[:, b % 2, j, 0:n], ACT.Copy).then_inc(hi_made[j], 1)

            def his(L, b):
                first = MIX[L] if b < MIXER else FFN[L]
                for j in range(3 if b < MIXER else 2):
                    hi(MIX[L] + b, j, mixer_sizes(b)[j], first)

            def square_tile(N):
                wait_residual(act, N)
                act.activation(xs[:, 0, :], h[:, 0, :], ACT.Square, accum_out=sq_sum[:, 0:1]).then_inc(sq_act, 1)

            def transposed_hi(use, dst, banks=range(4)):
                for n in banks:
                    act.wait_ge(tr_made, 4 * use + n + 1)
                    act.activation(dst[:, 2 * n:2 * n + 2, :], bank[B_T + n][:, :].rearrange("p (c s) -> p c s", s=S),
                                   ACT.Copy).then_inc(tr_hi, 1)

            def out_copy(L, pair, dst):
                for t in range(NT):
                    wait_out(act, L, pair, t)
                    act.activation(dst(t), bank[2 * (pair % 2) + t][:, :], ACT.Copy).then_inc(act_out[t], 1)

            act.wait_ge(router_in, 16)
            act.activation(rw_hi[:, :], rwt[:, :], ACT.Copy).then_inc(rw_hi_made, 1)
            his(0, 0)
            act.wait_ge(angle_made, 1)
            act.activation(ang[:, 2:4, :, :], ang[:, 0:2, :, :], ACT.Sin).then_inc(sines_made, 1)

            def mixer(L):
                B = MIX[L]
                square_tile(2 * L)
                transposed_hi(4 * L, aT_hi)
                his(L, BLK_CU)
                for t in range(NT):
                    act.wait_ge((out_made, used[2])[t], (OUTS * L + 1, MIX[L] + BLK_LAT + 1)[t])
                    for n, (a, b) in enumerate(((0, Q_LORA), (Q_LORA, Q_LORA + KV_LORA))):
                        act.activation(mixed[:, t, a:b], bank[B_LAT + t][:, a:b], ACT.Square,
                                       accum_out=lat_sq[:, 2 * n + t:2 * n + t + 1]).then_inc(lat_squared, 1)
                for t in range(NT):
                    act.activation(mixed[:, t, LAT - ROPE:LAT], bank[B_LAT + t][:, LAT - ROPE:LAT], ACT.Copy).then_inc(lat_scaled, 1)
                act.wait_ge(lat_rstd_made, L + 1)
                for t in range(NT):
                    for n, (a, b) in enumerate(((0, Q_LORA), (Q_LORA, Q_LORA + KV_LORA))):
                        act.activation(mixed[:, t, a:b], bank[B_LAT + t][:, a:b], ACT.Copy,
                                       scale=lat_rstd[:, 2 * n + t:2 * n + t + 1]).then_inc(lat_scaled, 1)
                for p in range(6):
                    his(L, BLK_CU + p + 1)
                    out_copy(L, PAIR_CU + p, lambda t: proj[:, p // 2, t, p % 2 * NB:(p % 2 + 1) * NB])
                    if p == 1:
                        for c in range(LC):
                            act.wait_ge(lat_tr, 2 * L + (1 if c < 2 else 2))
                            act.activation(lT_hi[:, c, :], bank[B_LT + c // 2][:, c % 2 * S:(c % 2 + 1) * S], ACT.Copy,
                                           scale=cols[:, DEPTH * CONV_K * KC + L * LC + c:][:, 0:1]).then_inc(lat_hi, 1)
                    if p == 4:
                        for n in range(4):
                            act.wait_ge(z_tr, 4 * L + n + 1)
                            act.activation(zT[:, 2 * n:2 * n + 2, :], bank[B_T + n][:, :].rearrange("p (c s) -> p c s", s=S),
                                           ACT.Copy).then_inc(z_in, 1)
                for n in range(4):
                    act.wait_ge(prod_made, 4 * L + n + 1)
                    act.activation(bT_hi[:, 2 * n:2 * n + 2, :], acc[:, 2 * n:2 * n + 2, :], ACT.Copy).then_inc(prod_hi, 1)
                for u in range(2):
                    his(L, BLK_CONV + u + 1)
                    out_copy(L, PAIR_CONV + u, lambda t: mixed[:, t, u * NB:(u + 1) * NB])
                for j in range(3):
                    hi(B + BLK_UKV, j, UKV_SIZES[j], B)
                    out_copy(L, PAIR_UQ + j, lambda t: q[:, t, j * NB:(j + 1) * NB])
                for c in range(4):
                    if c:
                        j = c - 1
                        hi(B + BLK_GATE, j, SLAB_SIZES[j], B)
                    wait_out(act, L, PAIR_UKV + c, 1)
                    src = bank[2 * ((PAIR_UKV + c) % 2) + 1][:, :].rearrange("p (h d) -> p h d", d=NOPE + VD)
                    act.activation(k[:, 1, :].rearrange("p (h d) -> p h d", d=QK)[:, 4 * c:4 * c + 4, 0:NOPE],
                                   src[:, :, 0:NOPE], ACT.Copy).then_inc(kv_act, 1)
                    act.activation(v[:, 1, :].rearrange("p (h d) -> p h d", d=VD)[:, 4 * c:4 * c + 4, :],
                                   src[:, :, NOPE:], ACT.Copy).then_inc(act_out[1], 1)
                for n in range(HEADS + 3):
                    if n < HEADS:
                        act.wait_ge(qk_tr, HEADS * L + n + 1)
                        if n:
                            act.wait_ge(s_made, HEADS * L + n)
                        act.activation(qkT[0:QK, :], bank[B_QK][0:QK, :], ACT.Copy).then_inc(qk_in, 1)
                    if 1 <= n <= HEADS:
                        act.wait_ge(max_made, 2 * (HEADS * L + n))
                        if n >= 2:
                            act.wait_ge(p_tr, HEADS * L + n - 1)
                            act.wait_ge(inv_made, HEADS * L + n - 1)
                        act.activation(p_buf[:, 0:P], s_buf[:, 0:P], ACT.Exp, bias=neg_max[:, 0:1],
                                       accum_out=row_sum[:, 0:1]).then_inc(p_made, 1)
                        act.activation(p_buf[:, P:3 * P], s_buf[:, P:3 * P], ACT.Exp, bias=neg_max[:, 1:2],
                                       accum_out=row_sum[:, 1:2]).then_inc(p_made, 1)
                    if 2 <= n <= HEADS + 1:
                        act.wait_ge(p_tr, HEADS * L + n - 1)
                        if n >= 3:
                            act.wait_ge(o_made, HEADS * L + n - 2)
                        act.activation(pT[:, :], bank[B_PT][:, 0:3 * P], ACT.Copy).then_inc(p_in, 1)
                    if n < HEADS and n % 4:
                        j = n % 4 - 1
                        hi(B + BLK_GATE + n // 4 + 1, j, SLAB_SIZES[j], B)
                transposed_hi(4 * L + 1, aT_hi)
                for t in range(NT):
                    act.wait_ge(dve_out[t], dve_value(L, PAIR_GATE + 3, t))
                    act.activation(gates[:, t, :], gates[:, t, :], ACT.Sigmoid).then_inc(gate_made, 1)
                his(L, BLK_ATT + 1)
                his(L, BLK_MIX)
                transposed_hi(4 * L + 2, bT_hi)
                his(L, BLK_MIX + 1)
                if L == 0:
                    his(L, MIXER)

            def silu(F, fb):
                for t in range(NT):
                    act.wait_ge((gu_made, used[1])[t], (fb + 1, F + 1)[t])
                    act.activation(sg[:, t, :], bank[B_GU + t][:, 0:HB], ACT.Silu).then_inc(silu_made, 1)

            def hidden_hi(fb):
                act.wait_ge(hid_tr, fb + 1)
                act.activation(hT_hi[:, :, :], bank[B_HT][:, :].rearrange("p (c s) -> p c s", s=S), ACT.Copy).then_inc(hT_hi_made, 1)

            def ffn_step(F, fb, first, ahead):
                silu(F - 1, fb - 1)
                hi(F - 1, 2, SLOT, first, True)
                hidden_hi(fb - 1)
                for j in range(2 if ahead else 0):
                    hi(F + 1, j, SLOT, first, True)

            mixer(0)
            square_tile(1)
            transposed_hi(3, aT_hi)
            F = FFN[0]
            for j in range(2):
                hi(F + 1, j, SLOT, F, True)
            with act.Fori(1, DENSE - 1) as i:
                ffn_step(F + i, i, F, True)
            ffn_step(F + DENSE - 1, DENSE - 1, F, False)
            for j in range(2):
                hi(MIX[1], j, LAT_SIZES[j], MIX[1])
            silu(F + DENSE - 1, DENSE - 1)
            hi(F + DENSE - 1, 2, SLOT, F, True)
            hidden_hi(DENSE - 1)
            hi(MIX[1], 2, LAT_SIZES[2], MIX[1])
            mixer(1)
            square_tile(3)
            transposed_hi(7, aT_hi)
            act.wait_ge(lmax_made, 1)
            act.activation(rt[:, :, 5, 0:1], rt[:, :, 4, 0:1], ACT.Exp).then_inc(lexp_made, 1)
            with act.Fori(0, EXPERTS) as e:
                F = FFN[1] + EXPERT * e
                fb = DENSE + EXPERT * e
                for b in (F, F + 1):
                    for j in range(2):
                        hi(b, j, SLOT, FFN[1], True)
                for i in range(1, EXPERT):
                    ffn_step(F + i, fb + i, FFN[1], i < EXPERT - 1)
                silu(F + EXPERT - 1, fb + EXPERT - 1)
                hi(F + EXPERT - 1, 2, SLOT, FFN[1], True)
                hidden_hi(fb + EXPERT - 1)
            square_tile(4)

        @block.vector
        def _(dve):
            links = [0]

            def link(*ins):
                for i in ins:
                    links[0] += 1
                    i.then_inc(dve_link, 1)
                dve.wait_ge(dve_link, links[0])

            def lo(b, j, n):
                dve.wait_ge(hi_made[j], b + 1)
                dve.tensor_tensor(w_lo[:, j, 0:n], raw[:, b % 2, j, 0:n], w_hi[:, j, 0:n].bitcast(F32),
                                  ALU.subtract).then_inc(lo_made[j], 1)

            def los(L, b):
                for j in range(3 if b < MIXER else 2):
                    lo(MIX[L] + b, j, mixer_sizes(b)[j])

            def square_tile(N):
                wait_residual(dve, N)
                dve.tensor_tensor_reduce(out=xs[:, 1, :], in0=h[:, 1, :], in1=h[:, 1, :], scale=1.0, scalar=0.0,
                                         op0=ALU.mult, op1=ALU.add, accum_out=sq_sum[:, 1:2]).then_inc(sq_dve, 1)

            def scale_tokens(N):
                dve.wait_ge(rstd_made, N + 1)
                dve.wait_ge(gain_in, 16 * (N + 1))
                for t in range(NT):
                    dve.scalar_tensor_tensor(out=xs[:, t, :], in0=h[:, t, :], scalar=rstd[:, t:t + 1], in1=gain[:, :],
                                             op0=ALU.mult, op1=ALU.mult).then_inc(xs_made, 1)

            def transposed_lo(use, dst, dst_hi, banks=range(4)):
                for n in banks:
                    dve.wait_ge(tr_hi, 4 * use + n + 1)
                    dve.tensor_tensor(dst[:, 2 * n:2 * n + 2, :], bank[B_T + n][:, :].rearrange("p (c s) -> p c s", s=S),
                                      dst_hi[:, 2 * n:2 * n + 2, :].bitcast(F32), ALU.subtract).then_inc(tr_lo, 1)

            def heads_of(t, d):
                return t.rearrange("p (h d) -> p h d", d=d)

            dve.wait_ge(cols_tr, 1)
            dve.tensor_copy(cols[:, :], bank[7][:, 0:NCOL]).then_inc(cols_made, 1)
            dve.wait_ge(rw_hi_made, 1)
            dve.tensor_tensor(rw_lo[:, :], rwt[:, :], rw_hi[:, :].bitcast(F32), ALU.subtract).then_inc(rw_lo_made, 1)
            los(0, 0)
            dve.wait_ge(pos_in, 16 * NT)
            dve.wait_ge(consts_made, 1)
            link(dve.tensor_copy(posf[:, :], pos_i[:, :]))
            link(*[dve.tensor_scalar(turns[:, 0, t, :], freq[:, :], posf[:, t:t + 1], None, ALU.mult) for t in range(NT)])
            magic = 1.5 * 2.0 ** 23
            two_pi = 2.0 * np.pi
            part1 = float(np.float32(6.28125))
            part2 = float(np.floor((two_pi - part1) * 2.0 ** 20) / 2.0 ** 20)
            part3 = float(np.float32(two_pi - part1 - part2))
            link(dve.tensor_scalar(turns[:, 1], turns[:, 0], 1.0 / two_pi, magic, ALU.mult, ALU.add))
            link(dve.tensor_scalar(turns[:, 2], turns[:, 1], magic, None, ALU.subtract))
            for part in (part1, part2, part3):
                link(dve.scalar_tensor_tensor(out=turns[:, 0], in0=turns[:, 2], scalar=-part, in1=turns[:, 0],
                                              op0=ALU.mult, op1=ALU.add))
            link(dve.tensor_scalar(ang[:, 0], turns[:, 0], 3.1415925, -3.1415925, ALU.min, ALU.max))
            dve.tensor_scalar(ang[:, 1], ang[:, 0], 0.5, None, ALU.mult).then_inc(angle_made, 1)
            dve.wait_ge(sines_made, 1)
            dve.tensor_copy(sin[:, :, :], ang[:, 2])
            link(dve.tensor_tensor(turns[:, 3], ang[:, 3], ang[:, 3], ALU.mult))
            link(dve.tensor_scalar(cos[:, :, :], turns[:, 3], -2.0, 1.0, ALU.mult, ALU.add))

            def mixer(L):
                B = MIX[L]
                square_tile(2 * L)
                scale_tokens(2 * L)
                transposed_lo(4 * L, aT_lo, aT_hi)
                los(L, BLK_CU)
                dve.wait_ge(lat_scaled, 6 * L + 2)
                k1, k2 = mixed[:, :, LAT - ROPE:LAT - RH], mixed[:, :, LAT - RH:LAT]
                kt = [rope_k[:, n, :, :] for n in range(4)]
                link(dve.tensor_tensor(kt[0], k1, cos[:, :, :], ALU.mult), dve.tensor_tensor(kt[1], k2, sin[:, :, :], ALU.mult),
                     dve.tensor_tensor(kt[2], k1, sin[:, :, :], ALU.mult), dve.tensor_tensor(kt[3], k2, cos[:, :, :], ALU.mult))
                link(dve.tensor_tensor(k_rope[:, :, 0:RH], kt[0], kt[1], ALU.subtract),
                     dve.tensor_tensor(k_rope[:, :, RH:], kt[2], kt[3], ALU.add))
                for p in range(6):
                    los(L, BLK_CU + p + 1)
                    if p == 1:
                        for c in range(LC):
                            dve.wait_ge(lat_hi, LC * L + (2 if c < 2 else 3))
                            dve.scalar_tensor_tensor(out=lT_lo[:, c, :], in0=bank[B_LT + c // 2][:, c % 2 * S:(c % 2 + 1) * S],
                                                     scalar=cols[:, DEPTH * CONV_K * KC + L * LC + c:][:, 0:1],
                                                     in1=lT_hi[:, c, :].bitcast(F32), op0=ALU.mult,
                                                     op1=ALU.subtract).then_inc(lat_lo, 1)
                    if p == 3:
                        for t in range(NT):
                            dve.wait_ge(act_out[t], (PAIR_UKV, PAIR_GATE)[t] * L + 4)
                            dve.tensor_tensor(proj[:, 0, t, :], proj[:, 0, t, :], proj[:, 1, t, :], ALU.mult).then_inc(z_made, 1)
                    if p == 4:
                        dve.wait_ge(z_in, 4 * L + 4)
                        tap = [[cols[:, (L * CONV_K + n) * KC + c:][:, 0:1] for c in range(KC)] for n in range(CONV_K)]
                        link(*[dve.tensor_scalar(acc[:, c, :], zT[:, c, :], tap[2][c], None, ALU.mult) for c in range(KC)])
                        for back in (1, 2):
                            link(*[dve.scalar_tensor_tensor(out=acc[:, c, back:], in0=zT[:, c, 0:S - back], scalar=tap[2 - back][c],
                                                            in1=acc[:, c, back:], op0=ALU.mult, op1=ALU.add) for c in range(KC)])
                for n in range(4):
                    part = acc[:, 2 * n:2 * n + 2, :]
                    dve.wait_ge(b_tr, 4 * L + n + 1)
                    dve.tensor_tensor(part, part, bank[B_T + n][:, :].rearrange("p (c s) -> p c s", s=S), ALU.mult).then_inc(prod_made, 1)
                for n in range(4):
                    part = acc[:, 2 * n:2 * n + 2, :]
                    dve.wait_ge(prod_hi, 4 * L + n + 1)
                    dve.tensor_tensor(bT_lo[:, 2 * n:2 * n + 2, :], part, bT_hi[:, 2 * n:2 * n + 2, :].bitcast(F32),
                                      ALU.subtract).then_inc(prod_lo, 1)
                los(L, BLK_CONV + 1)
                los(L, BLK_UQ)
                for j in range(3):
                    lo(B + BLK_UKV, j, UKV_SIZES[j])
                for c in range(4):
                    if c:
                        lo(B + BLK_GATE, c - 1, SLAB_SIZES[c - 1])
                    wait_out(dve, L, PAIR_UKV + c, 0)
                    src = heads_of(bank[2 * ((PAIR_UKV + c) % 2)][:, :], NOPE + VD)
                    link(dve.tensor_copy(heads_of(k[:, 0, :], QK)[:, 4 * c:4 * c + 4, 0:NOPE], src[:, :, 0:NOPE]))
                    dve.tensor_copy(heads_of(v[:, 0, :], VD)[:, 4 * c:4 * c + 4, :], src[:, :, NOPE:]).then_inc(dve_out[0], 1)
                for t in range(NT):
                    dve.tensor_copy(heads_of(k[:, t, :], QK)[:, :, NOPE:],
                                    k_rope[:, t, :].unsqueeze(1).to_broadcast([P, HEADS, ROPE])).then_inc(heads_ready, 1)
                    dve.wait_ge(act_out[t], (PAIR_UKV, PAIR_GATE)[t] * L + PAIR_UKV)
                    q1, q2 = heads_of(q[:, t, :], QK)[:, :, NOPE:NOPE + RH], heads_of(q[:, t, :], QK)[:, :, NOPE + RH:]
                    c_b, s_b = (m[:, t, :].unsqueeze(1).to_broadcast([P, HEADS, RH]) for m in (cos, sin))
                    r = [rope_t[:, n, :, :] for n in range(4)]
                    if t:
                        dve.wait_ge(heads_ready, 6 * L + 3)
                    link(dve.tensor_tensor(r[0], q1, c_b, ALU.mult), dve.tensor_tensor(r[1], q2, s_b, ALU.mult),
                         dve.tensor_tensor(r[2], q1, s_b, ALU.mult), dve.tensor_tensor(r[3], q2, c_b, ALU.mult))
                    dve.tensor_tensor(q1, r[0], r[1], ALU.subtract).then_inc(heads_ready, 1)
                    dve.tensor_tensor(q2, r[2], r[3], ALU.add).then_inc(heads_ready, 1)
                dve.wait_ge(bias_in, 32 * (L + 1))

                def add_bias(g):
                    for t in range(NT):
                        wait_out(dve, L, PAIR_GATE + g, t)
                        part = gates[:, t, g * NB:(g + 1) * NB]
                        dve.tensor_tensor(part, part, bank[2 * ((PAIR_GATE + g) % 2) + t][:, :], ALU.add).then_inc(dve_out[t], 1)

                for n in range(HEADS + 3):
                    if 2 <= n <= HEADS + 1:
                        dve.wait_ge(p_made, 2 * (HEADS * L + n - 1))
                        if n >= 4:
                            dve.wait_ge(o_in, 2 * (HEADS * L + n - 3))
                        dve.reciprocal(row_inv[n % 2], row_sum).then_inc(inv_made, 1)
                    if 1 <= n <= HEADS:
                        dve.wait_ge(s_made, HEADS * L + n)
                        if n >= 2:
                            dve.wait_ge(p_made, 2 * (HEADS * L + n - 1))
                        link(dve.scalar_tensor_tensor(out=s_buf[:, :], in0=bank[B_S][:, 0:3 * P], scalar=SCALE, in1=mask[:, :],
                                                      op0=ALU.mult, op1=ALU.add))
                        dve.reduce_max(neg_max[:, 0:1], s_buf[:, 0:P], AX, negate=True).then_inc(max_made, 1)
                        dve.reduce_max(neg_max[:, 1:2], s_buf[:, P:3 * P], AX, negate=True).then_inc(max_made, 1)
                    if n >= 3:
                        dve.wait_ge(o_made, HEADS * L + n - 2)
                        dve.wait_ge(inv_made, HEADS * L + n - 2)
                        for t in range(NT):
                            dve.tensor_scalar(xs[:, t, (n - 3) * VD:(n - 2) * VD], bank[B_O][:, t * VD:(t + 1) * VD],
                                              row_inv[(n - 1) % 2][:, t:t + 1], None, ALU.mult).then_inc(o_in, 1)
                    if n < HEADS and n % 4:
                        lo(B + BLK_GATE + n // 4 + 1, n % 4 - 1, SLAB_SIZES[n % 4 - 1])
                    elif n and n <= HEADS:
                        add_bias(n // 4 - 1)
                transposed_lo(4 * L + 1, aT_lo, aT_hi)
                los(L, BLK_ATT + 1)
                for t in range(NT):
                    dve.wait_ge(gate_made, NT * L + t + 1)
                    dve.wait_ge(act_out[t], (PAIR_UKV, PAIR_GATE)[t] * L + PAIR_CONV + 2)
                    link(dve.tensor_tensor(mixed[:, t, :], mixed[:, t, :], gates[:, t, 0:D], ALU.mult))
                for u in range(2):
                    for t in range(NT):
                        wait_out(dve, L, PAIR_ATT + u, t)
                        g_b, m = gates[:, t, D + u * NB:D + (u + 1) * NB], mixed[:, t, u * NB:(u + 1) * NB]
                        dve.tensor_tensor(g_b, g_b, bank[2 * ((PAIR_ATT + u) % 2) + t][:, :], ALU.mult).then_inc(dve_out[t], 1)
                        dve.wait_ge(dve_out[t], dve_value(L, PAIR_ATT + u, t))
                        dve.tensor_tensor(m, m, g_b, ALU.add).then_inc(m_made, 1)
                    if u == 0:
                        los(L, BLK_MIX)
                transposed_lo(4 * L + 2, bT_lo, bT_hi)
                los(L, BLK_MIX + 1)
                for u in range(2):
                    for t in range(NT):
                        wait_out(dve, L, PAIR_MIX + u, t)
                        part = h[:, t, u * NB:(u + 1) * NB]
                        dve.tensor_tensor(part, part, bank[2 * ((PAIR_MIX + u) % 2) + t][:, :], ALU.add).then_inc(dve_out[t], 1)
                    if u == 0 and L == 0:
                        los(L, MIXER)

            def hidden(fb):
                for t in range(NT):
                    dve.wait_ge(silu_made, 2 * fb + t + 1)
                    dve.tensor_tensor(hid[:, t, :], sg[:, t, :], bank[B_GU + t][:, HB:2 * HB], ALU.mult).then_inc(hid_made, 1)

            def hidden_lo(fb):
                dve.wait_ge(hT_hi_made, fb + 1)
                dve.tensor_tensor(hT_lo[:, :, :], bank[B_HT][:, :].rearrange("p (c s) -> p c s", s=S),
                                  hT_hi[:, :, :].bitcast(F32), ALU.subtract).then_inc(hT_lo_made, 1)

            def ffn_step(F, fb, ahead):
                hidden(fb - 1)
                lo(F - 1, 2, SLOT)
                hidden_lo(fb - 1)
                for j in range(2 if ahead else 0):
                    lo(F + 1, j, SLOT)

            mixer(0)
            square_tile(1)
            scale_tokens(1)
            transposed_lo(3, aT_lo, aT_hi)
            F = FFN[0]
            for j in range(2):
                lo(F + 1, j, SLOT)
            with dve.Fori(1, DENSE - 1) as i:
                ffn_step(F + i, i, True)
            ffn_step(F + DENSE - 1, DENSE - 1, False)
            for j in range(2):
                lo(MIX[1], j, LAT_SIZES[j])
            hidden(DENSE - 1)
            lo(F + DENSE - 1, 2, SLOT)
            hidden_lo(DENSE - 1)
            lo(MIX[1], 2, LAT_SIZES[2])
            dve.wait_ge(used[2], F + DENSE)
            for t in range(NT):
                for u in range(2):
                    part = h[:, t, u * NB:(u + 1) * NB]
                    dve.tensor_tensor(part, part, bank[2 * t + u][:, :], ALU.add).then_inc(h_new, 1)
            mixer(1)
            square_tile(3)
            scale_tokens(3)
            transposed_lo(7, aT_lo, aT_hi)
            lg, mx, ix, ixf, df, w1, w2, pick = (rt[:, :, n, :] for n in range(8))
            iota_e = rt[:, :, 8, :]
            dve.wait_ge(logits_made, 1)
            link(*[dve.tensor_copy(lg[:, t, :], bank[t][:, 0:EXPERTS]) for t in range(NT)])
            link(*[dve.memset(iota_e[:, :, n:n + 1], float(n)) for n in range(EXPERTS)])
            link(*[dve.max(mx[:, t, :], lg[:, t, :]) for t in range(NT)])
            link(*[dve.max_index(ix[:, t, :].bitcast(U32), mx[:, t, :], lg[:, t, :]) for t in range(NT)])
            link(dve.tensor_copy(ixf, ix.bitcast(U32)))
            dve.tensor_tensor(df[:, :, 0:1], mx[:, :, 1:2], mx[:, :, 0:1], ALU.subtract).then_inc(lmax_made, 1)
            dve.wait_ge(lexp_made, 1)
            link(dve.tensor_scalar(w1[:, :, 1:2], w1[:, :, 0:1], 1.0, None, ALU.add))
            link(dve.reciprocal(w1[:, :, 2:3], w1[:, :, 1:2]))
            link(dve.tensor_tensor(w1[:, :, 3:4], w1[:, :, 0:1], w1[:, :, 2:3], ALU.mult))
            for t in range(NT):
                link(dve.tensor_scalar(pick[:, t, :], iota_e[:, t, :], ixf[:, t, 0:1], w1[:, t, 2:3], ALU.is_equal, ALU.mult),
                     dve.tensor_scalar(w2[:, t, :], iota_e[:, t, :], ixf[:, t, 1:2], w1[:, t, 3:4], ALU.is_equal, ALU.mult))
                link(dve.tensor_tensor(expert_gate[:, t, :], pick[:, t, :], w2[:, t, :], ALU.add))
            with dve.Fori(0, EXPERTS) as e:
                F = FFN[1] + EXPERT * e
                fb = DENSE + EXPERT * e
                for b in (F, F + 1):
                    for j in range(2):
                        lo(b, j, SLOT)
                for i in range(1, EXPERT):
                    ffn_step(F + i, fb + i, i < EXPERT - 1)
                hidden(fb + EXPERT - 1)
                lo(F + EXPERT - 1, 2, SLOT)
                hidden_lo(fb + EXPERT - 1)
                dve.wait_ge(used[2], F + EXPERT)
                for t in range(NT):
                    for u in range(2):
                        part = h[:, t, u * NB:(u + 1) * NB]
                        dve.scalar_tensor_tensor(out=part, in0=bank[2 * t + u][:, :], scalar=expert_gate[:, t, ds(e, 1)],
                                                 in1=part, op0=ALU.mult, op1=ALU.add).then_inc(h_new, 1)
            square_tile(4)
            scale_tokens(4)

        @block.tensor
        def _(pe):
            def product(dst, x_hi, x_lo, b_hi, b_lo, start, stop):
                pe.matmul(dst, x_hi, b_hi, start=start, stop=False)
                pe.matmul(dst, x_hi, b_lo, start=False, stop=False)
                return pe.matmul(dst, x_lo, b_hi, start=False, stop=stop)

            def tile(m, c, t):
                return m[:, c, t * P:(t + 1) * P]

            def w(j, c, n, width, m):
                return m[:, j, c * width:c * width + n]

            def slab(L, b, pair, x_hi, x_lo, before=None):
                for j, (c0, nc_) in enumerate(G_CHUNKS):
                    pe.wait_ge(lo_made[j], MIX[L] + b + 1)
                    for t in range(NT):
                        if j == 0:
                            wait_pair_free(pe, L, pair, t)
                        dst = bank[2 * (pair % 2) + t][:, :]
                        for c in range(nc_):
                            last = product(dst, tile(x_hi, c0 + c, t), tile(x_lo, c0 + c, t), w(j, c, NB, NB, w_hi),
                                           w(j, c, NB, NB, w_lo), c0 + c == 0, c0 + c == KC - 1)
                        if j == 2 and t == 0:
                            last.then_inc(out_made, 1)
                    last.then_inc(used[j], 1)

            def transpose_tokens(src, use, halves=(0, 1)):
                for u in halves:
                    for n in (2 * u, 2 * u + 1):
                        for c in (2 * n, 2 * n + 1):
                            for t in range(NT):
                                last = pe.transpose(bank[B_T + n][:, (c % 2) * S + t * P:(c % 2) * S + (t + 1) * P],
                                                    src(t)[:, c * P:(c + 1) * P], ident[:, :])
                        last.then_inc(use, 1)

            def mixer(L):
                pe.wait_ge(xs_made, 4 * L + 2)
                transpose_tokens(lambda t: xs[:, t, :], tr_made)
                pe.wait_ge(tr_lo, 16 * L + 4)
                for j, (c0, nc_) in enumerate(G_CHUNKS):
                    pe.wait_ge(lo_made[j], MIX[L] + BLK_LAT + 1)
                    for t in range(NT):
                        for c in range(nc_):
                            last = product(bank[B_LAT + t][:, 0:LAT], tile(aT_hi, c0 + c, t), tile(aT_lo, c0 + c, t),
                                           w(j, c, LAT, LAT, w_hi), w(j, c, LAT, LAT, w_lo), c0 + c == 0, c0 + c == KC - 1)
                        if j == 2 and t == 0:
                            last.then_inc(out_made, 1)
                    last.then_inc(used[j], 1)
                for p in range(6):
                    if p == 5:
                        pe.wait_ge(z_made, NT * (L + 1))
                        pe.wait_ge(lat_scaled, 6 * (L + 1))
                        pe.wait_ge(lat_lo, LC * (L + 1))
                        transpose_tokens(lambda t: proj[:, 0, t, :], z_tr)
                    slab(L, BLK_CU + p, PAIR_CU + p, aT_hi, aT_lo)
                    if p == 1:
                        pe.wait_ge(lat_scaled, 6 * (L + 1))
                        for c in range(LC):
                            for t in range(NT):
                                last = pe.transpose(bank[B_LT + c // 2][:, c % 2 * S + t * P:c % 2 * S + (t + 1) * P],
                                                    mixed[:, t, c * P:(c + 1) * P], ident[:, :])
                            if c:
                                last.then_inc(lat_tr, 1)
                for t in range(NT):
                    pe.wait_ge(act_out[t], (PAIR_UKV, PAIR_GATE)[t] * L + PAIR_CONV)
                pe.wait_ge(z_in, 4 * (L + 1))
                transpose_tokens(lambda t: proj[:, 2, t, :], b_tr)
                pe.wait_ge(prod_lo, 4 * (L + 1))
                for u in range(2):
                    slab(L, BLK_CONV + u, PAIR_CONV + u, bT_hi, bT_lo)
                for j in range(3):
                    pe.wait_ge(lo_made[j], MIX[L] + BLK_UQ + 1)
                    for t in range(NT):
                        wait_pair_free(pe, L, PAIR_UQ + j, t)
                        for c in range(2):
                            last = product(bank[2 * ((PAIR_UQ + j) % 2) + t][:, :], tile(lT_hi, c, t), tile(lT_lo, c, t),
                                           w(j, c, NB, NB, w_hi), w(j, c, NB, NB, w_lo), c == 0, c == 1)
                        if t == 0:
                            last.then_inc(out_made, 1)
                    last.then_inc(used[j], 1)
                for c, (j, n) in enumerate(((0, 0), (0, 1), (1, 0), (2, 0))):
                    pe.wait_ge(lo_made[j], MIX[L] + BLK_UKV + 1)
                    for t in range(NT):
                        wait_pair_free(pe, L, PAIR_UKV + c, t)
                        last = product(bank[2 * ((PAIR_UKV + c) % 2) + t][:, :], tile(lT_hi, 2, t), tile(lT_lo, 2, t),
                                       w(j, n, NB, NB, w_hi), w(j, n, NB, NB, w_lo), True, True)
                        if t == 0:
                            last.then_inc(out_made, 1)
                    if c:
                        last.then_inc(used[j], 1)
                for n in range(HEADS + 3):
                    if n < HEADS:
                        g, b = n // 4, BLK_GATE + n // 4
                        for c in (2 * (n % 4), 2 * (n % 4) + 1):
                            j = c // 3
                            if c % 3 == 0:
                                pe.wait_ge(lo_made[j], MIX[L] + b + 1)
                            for t in range(NT):
                                if c == 0:
                                    wait_pair_free(pe, L, PAIR_GATE + g, t)
                                last = product(bank[2 * ((PAIR_GATE + g) % 2) + t][:, :], tile(aT_hi, c, t), tile(aT_lo, c, t),
                                               w(j, c % 3, NB, NB, w_hi), w(j, c % 3, NB, NB, w_lo), c == 0, c == KC - 1)
                                if c == KC - 1 and t == 0:
                                    last.then_inc(out_made, 1)
                            if c in (2, 5, 7):
                                last.then_inc(used[j], 1)
                        if n == 0:
                            pe.wait_ge(heads_ready, 6 * (L + 1))
                            pe.wait_ge(kv_act, 4 * (L + 1))
                            for t in range(NT):
                                pe.wait_ge((dve_out, act_out)[t][t], dve_value(L, PAIR_UKV + 3, 0) if t == 0 else PAIR_GATE * (L + 1))
                        else:
                            pe.wait_ge(qk_in, HEADS * L + n)
                        for m, src in enumerate((q, k)):
                            for t in range(NT):
                                last = pe.transpose(bank[B_QK][0:QK, m * S + t * P:m * S + (t + 1) * P],
                                                    src[:, t, n * QK:(n + 1) * QK], ident[:, :])
                        last.then_inc(qk_tr, 1)
                    if 1 <= n <= HEADS:
                        pe.wait_ge(qk_in, HEADS * L + n)
                        if n >= 2:
                            pe.wait_ge(max_made, 2 * (HEADS * L + n - 1))
                        for t in range(NT):
                            last = pe.matmul(bank[B_S][:, t * P:(2 * t + 1) * P], qkT[0:QK, t * P:(t + 1) * P],
                                             qkT[0:QK, S:S + (t + 1) * P], start=True, stop=True)
                        last.then_inc(s_made, 1)
                    if 2 <= n <= HEADS + 1:
                        pe.wait_ge(p_made, 2 * (HEADS * L + n - 1))
                        if n >= 3:
                            pe.wait_ge(p_in, HEADS * L + n - 2)
                        for m in range(3):
                            last = pe.transpose(bank[B_PT][:, m * P:(m + 1) * P], p_buf[:, m * P:(m + 1) * P], ident[:, :])
                        last.then_inc(p_tr, 1)
                    if n >= 3:
                        pe.wait_ge(p_in, HEADS * L + n - 2)
                        if n >= 4:
                            pe.wait_ge(o_in, 2 * (HEADS * L + n - 3))
                        for t, (m, kt, start, stop) in zip((0, 1, 1), ((0, 0, True, True), (1, 0, True, False), (2, 1, False, True))):
                            last = pe.matmul(bank[B_O][:, t * VD:(t + 1) * VD], pT[:, m * P:(m + 1) * P],
                                             v[:, kt, (n - 3) * VD:(n - 2) * VD], start=start, stop=stop)
                        last.then_inc(o_made, 1)
                pe.wait_ge(o_in, 2 * HEADS * (L + 1))
                transpose_tokens(lambda t: xs[:, t, :], tr_made)
                pe.wait_ge(tr_lo, 16 * L + 8)
                for u in range(2):
                    slab(L, BLK_ATT + u, PAIR_ATT + u, aT_hi, aT_lo)
                pe.wait_ge(m_made, 4 * L + 4)
                transpose_tokens(lambda t: mixed[:, t, :], tr_made)
                pe.wait_ge(tr_lo, 16 * L + 12)
                for u in range(2):
                    slab(L, BLK_MIX + u, PAIR_MIX + u, bT_hi, bT_lo)

            def gate_up(F, fb, j):
                pe.wait_ge(lo_made[j], F + 1)
                for t in range(NT):
                    if j == 0 and not (isinstance(fb, int) and fb == 0):
                        pe.wait_ge(hid_made, 2 * fb - 1 + t)
                    for c in range(4):
                        last = product(bank[B_GU + t][:, :], tile(aT_hi, 4 * j + c, t), tile(aT_lo, 4 * j + c, t),
                                       w(j, c, NB, NB, w_hi), w(j, c, NB, NB, w_lo), j == 0 and c == 0, j == 1 and c == 3)
                    if j == 1 and t == 0:
                        last.then_inc(gu_made, 1)
                last.then_inc(used[j], 1)

            def hidden_transposes(fb):
                pe.wait_ge(hid_made, 2 * fb + 2)
                for c in range(HC):
                    for t in range(NT):
                        last = pe.transpose(bank[B_HT][:, c * S + t * P:c * S + (t + 1) * P], hid[:, t, c * P:(c + 1) * P], ident[:, :])
                last.then_inc(hid_tr, 1)

            def down(F, fb, start, stop):
                pe.wait_ge(hT_lo_made, fb + 1)
                pe.wait_ge(lo_made[2], F + 1)
                for t in range(NT):
                    for u in range(2):
                        for c in range(HC):
                            last = product(bank[2 * t + u][:, :], tile(hT_hi, c, t), tile(hT_lo, c, t),
                                           w_hi[:, 2, c * D + u * NB:c * D + (u + 1) * NB], w_lo[:, 2, c * D + u * NB:c * D + (u + 1) * NB],
                                           start and c == 0, stop and c == HC - 1)
                last.then_inc(used[2], 1)

            def ffn_step(F, fb, start):
                gate_up(F, fb, 0)
                hidden_transposes(fb - 1)
                gate_up(F, fb, 1)
                down(F - 1, fb - 1, start, False)

            pe.wait_ge(rows_in, 16 * 3 * DEPTH)
            pe.wait_ge(ident_made, 1)
            pe.transpose(bank[7][:, 0:NCOL], rowc[:, :], ident[0:NCOL, 0:NCOL]).then_inc(cols_tr, 1)
            pe.wait_ge(cols_made, 1)
            mixer(0)
            F = FFN[0]
            pe.wait_ge(xs_made, 4)
            transpose_tokens(lambda t: xs[:, t, :], tr_made)
            pe.wait_ge(tr_lo, 16)
            for j in range(2):
                gate_up(F, 0, j)
            ffn_step(F + 1, 1, True)
            with pe.Fori(2, DENSE) as i:
                ffn_step(F + i, i, False)
            hidden_transposes(DENSE - 1)
            down(F + DENSE - 1, DENSE - 1, False, True)
            pe.wait_ge(h_new, 4)
            mixer(1)
            pe.wait_ge(xs_made, 8)
            transpose_tokens(lambda t: xs[:, t, :], tr_made)
            pe.wait_ge(tr_lo, 32)
            pe.wait_ge(rw_lo_made, 1)
            for t in range(NT):
                for c in range(KC):
                    e8 = slice(c * EXPERTS, (c + 1) * EXPERTS)
                    last = product(bank[t][:, 0:EXPERTS], tile(aT_hi, c, t), tile(aT_lo, c, t), rw_hi[:, e8], rw_lo[:, e8],
                                   c == 0, c == KC - 1)
            last.then_inc(logits_made, 1)
            pe.wait_ge(lmax_made, 1)
            with pe.Fori(0, EXPERTS) as e:
                F = FFN[1] + EXPERT * e
                fb = DENSE + EXPERT * e
                for j in range(2):
                    gate_up(F, fb, j)
                for i in range(1, EXPERT):
                    if i == 1:
                        pe.wait_ge(h_new, 4 * e + 4)
                    ffn_step(F + i, fb + i, i == 1)
                hidden_transposes(fb + EXPERT - 1)
                down(F + EXPERT - 1, fb + EXPERT - 1, False, True)


_INS = ["x", "positions", "norm_mix", "w_in", "b_gate", "conv_w", "w_conv_out", "norm_q", "norm_kv", "w_uq", "w_ukv",
        "w_attn_out", "w_mix_out", "norm_ffn", "dense_w_gate", "dense_w_up", "dense_w_down", "router_w",
        "moe_w_gate", "moe_w_up", "moe_w_down", "norm_final"]


def kernel(**inputs):
    import numpy as _np
    import concourse.bacc as _bacc
    from concourse import mybir as _mybir
    from concourse.bass_utils import run_bass_kernel_spmd as _run

    nc = _bacc.Bacc("TRN2", target_bir_lowering=False, num_devices=1)
    arrays, args = {}, []
    for name in _INS:
        a = _np.ascontiguousarray(inputs[name])
        arrays[f"in_{name}"] = a
        args.append(nc.dram_tensor(f"in_{name}", a.shape, _mybir.dt.from_np(a.dtype), kind="ExternalInput").ap())
    args.append(nc.dram_tensor("out_0", (1, S, D), F32, kind="ExternalOutput").ap())
    build_trunk(nc, *args)
    r = _run(nc, [arrays], core_ids=[0])
    return r.results[0]["out_0"]
```

```python
from contextlib import ExitStack

import concourse.bass as bass
import numpy as np
from concourse import mybir

F32 = mybir.dt.float32
F32R = mybir.dt.float32r
I32 = mybir.dt.int32
U32 = mybir.dt.uint32
ACT = mybir.ActivationFunctionType
ALU = mybir.AluOpType
AX = mybir.AxisListType.X
ds = bass.ds

P = 128
D = 1024
KC = D // P
S = 256
NT = S // P
DEPTH = 2
CHUNK = 64
CONV_K = 3
HEADS, NOPE, ROPE, VD = 16, 64, 32, 64
QK = NOPE + ROPE
RH = ROPE // 2
Q_LORA, KV_LORA = 256, 128
LAT = Q_LORA + KV_LORA + ROPE
LC = (Q_LORA + KV_LORA) // P
F_DENSE, F_EXPERT, EXPERTS = 2816, 1792, 8
EPS = 1e-6
THETA = 10000.0
SCALE = float(QK) ** -0.5
MASKED = -1e30
NB = 512
HB = 256
HC = HB // P
SLOT = 2048
G_CHUNKS = ((0, 3), (3, 3), (6, 2))
COL_B, COL_C, COL_U, COL_LAT, COL_G = 0, D, 2 * D, 3 * D, 3 * D + LAT

BLK_LAT, BLK_CU, BLK_B, BLK_CONV, BLK_UQ, BLK_UKV, BLK_GATE, BLK_ATT, BLK_MIX, MIXER = 0, 1, 5, 7, 9, 10, 11, 15, 17, 19
DENSE, EXPERT = F_DENSE // HB, F_EXPERT // HB
MIX = (0, MIXER + DENSE)
FFN = (MIXER, 2 * MIXER + DENSE)

SLAB_SIZES = tuple(n * NB for _, n in G_CHUNKS)
LAT_SIZES = tuple(n * LAT for _, n in G_CHUNKS)
UQ_SIZES = (2 * NB,) * 3
UKV_SIZES = (2 * NB, NB, NB)
FFN_SIZES = (SLOT,) * 3


def mixer_sizes(b):
    return {BLK_LAT: LAT_SIZES, BLK_UQ: UQ_SIZES, BLK_UKV: UKV_SIZES, MIXER: FFN_SIZES}.get(b, SLAB_SIZES)


def raw_value(block, j, first):
    if j == 2:
        return 16 * (block + 1)
    doubled = {MIX[0]: 0, FFN[0]: 0, MIX[1]: DENSE, FFN[1]: DENSE}[first]
    return 16 * (first + doubled) + (32 if first in FFN else 16) * (block - first + 1)


PAIR_CU, PAIR_B, PAIR_CONV, PAIR_UQ, PAIR_UKV, PAIR_GATE, PAIR_ATT, PAIR_MIX, PAIRS = 0, 4, 6, 8, 11, 15, 19, 21, 23


def build_trunk(nc, x, positions, norm_mix, w_in, b_gate, conv_w, w_conv_out, norm_q, norm_kv, w_uq, w_ukv,
                w_attn_out, w_mix_out, norm_ffn, dense_w_gate, dense_w_up, dense_w_down, router_w,
                moe_w_gate, moe_w_up, moe_w_down, norm_final, out):
    ctx = ExitStack()
    with ctx:
        sizeof = 4
        at = [(nc.sbuf_base + 31) // 32 * 32]

        def place(name, shape, dt=F32):
            t = nc.alloc_sbuf_tensor_at(name, shape, dt, offset=at[0])
            at[0] += (int(np.prod(shape[1:])) * sizeof + 31) // 32 * 32
            return t

        def regions(*groups):
            start, end, got = at[0], at[0], []
            for group in groups:
                at[0] = start
                got += [place(*t) for t in group]
                end = max(end, at[0])
            at[0] = end
            return got

        def sem(name):
            return ctx.enter_context(nc.semaphore(name))

        raw = place("raw", [P, 2, 3, SLOT])
        w_hi = place("w_hi", [P, 3, SLOT], F32R)
        w_lo = place("w_lo", [P, 3, SLOT], F32R)
        h = place("h", [P, NT, D])
        aT_hi = place("aT_hi", [P, KC, S], F32R)
        aT_lo = place("aT_lo", [P, KC, S], F32R)
        ident = place("ident", [P, P])
        mask = place("mask", [P, 3 * P])
        cos = place("cos", [P, NT, RH])
        sin = place("sin", [P, NT, RH])
        NCOL = DEPTH * (CONV_K * KC + LC)
        cols = place("cols", [P, NCOL])
        rwt = place("rwt", [P, KC * EXPERTS])
        rw_hi = place("rw_hi", [P, KC * EXPERTS], F32R)
        rw_lo = place("rw_lo", [P, KC * EXPERTS], F32R)
        expert_gate = place("expert_gate", [P, NT, EXPERTS])
        rope_k = place("rope_k", [P, 4, NT, RH])
        k_rope = place("k_rope", [P, NT, ROPE])
        small = place("small", [P, 64])
        sq_sum, var, rstd = small[:, 0:2], small[:, 2:4], small[:, 4:6]
        lat_sq, lat_var, lat_rstd = small[:, 6:10], small[:, 10:14], small[:, 14:18]
        minus_half = small[:, 18:22]
        neg_max = small[:, 22:24]
        row_sum = small[:, 24:26]
        row_inv = (small[:, 26:28], small[:, 32:34])
        lat_scale = small[:, 28:32]
        mixed, y_hi, y_lo = regions(
            [("mixed", [P, NT, D])],
            [("y_hi", [P, D], F32R), ("y_lo", [P, D], F32R)])
        gates, xn_hi, xn_lo = regions(
            [("gates", [P, NT, 2 * D])],
            [("xn_hi", [P, NT, D], F32R), ("xn_lo", [P, NT, D], F32R)])
        xs, lT_hi, lT_lo = regions(
            [("xs", [P, NT, D])],
            [("lT_hi", [P, LC, S], F32R), ("lT_lo", [P, LC, S], F32R)])
        (proj, zT, q, k, v, sg, hid, hT_hi, hT_lo, rt, gain, sel, selT, slot_no, token_slot, chosen, tri, ones, counts, flag, iota_i, ang, turns, rowc, pos_i, posf, freq) = regions(
            [("proj", [P, 3, NT, D]), ("zT", [P, KC, S])],
            [("q", [P, NT, HEADS * QK]), ("k", [P, NT, HEADS * QK]), ("v", [P, NT, HEADS * VD])],
            [("sg", [P, NT, HB]), ("hid", [P, NT, HB]),
             ("hT_hi", [P, HC, S], F32R), ("hT_lo", [P, HC, S], F32R),
             ("rt", [P, NT, 9, EXPERTS]),
             ("gain", [P, D]),
             ("sel", [P, 2, NT, P], F32R),
             ("selT", [P, 2, S], F32R),
             ("slot_no", [P, S]), ("token_slot", [P, NT, EXPERTS]), ("chosen", [P, NT, EXPERTS]),
             ("tri", [P, P]), ("ones", [P, P]), ("counts", [P, 8]), ("flag", [P, 1], I32), ("iota_i", [P, S], I32)],
            [("ang", [P, 4, NT, RH]), ("turns", [P, 4, NT, RH]), ("rowc", [NCOL, P]),
             ("pos_i", [P, NT], I32), ("posf", [P, NT]), ("freq", [P, RH])])
        acc = proj[:, 1, :, :].rearrange("p t (c s) -> p (t c) s", s=S)
        bT_hi, bT_lo, qkT, s_buf, p_buf, pT, rope_t = regions(
            [("bT_hi", [P, KC, S], F32R), ("bT_lo", [P, KC, S], F32R)],
            [("qkT", [P, 2 * S]), ("s_buf", [P, 3 * P]), ("p_buf", [P, 3 * P]), ("pT", [P, 3 * P]),
             ("rope_t", [P, 4, HEADS, RH])])
        assert at[0] <= nc.sbuf_usable_end, at[0] - nc.sbuf_usable_end

        bank = [ctx.enter_context(nc.psum_tensor(f"bank{i}", [P, NB], F32)) for i in range(8)]
        B_QK, B_S, B_PT, B_O = 4, 5, 6, 7
        B_T = 4
        B_LAT, B_LT = 4, 6

        raw_in = [sem(f"raw_in{j}") for j in range(3)]
        hi_made = [sem(f"hi_made{j}") for j in range(3)]
        lo_made = [sem(f"lo_made{j}") for j in range(3)]
        used = [sem(f"used{j}") for j in range(3)]
        h_in, rows_in, gain_in, bias_in, router_in, pos_in = (sem(n) for n in (
            "h_in", "rows_in", "gain_in", "bias_in", "router_in", "pos_in"))
        ident_made, consts_made, cols_tr, cols_made = (sem(n) for n in ("ident_made", "consts_made", "cols_tr", "cols_made"))
        sq_act, sq_dve, rstd_made, xs_made = (sem(n) for n in ("sq_act", "sq_dve", "rstd_made", "xs_made"))
        tr_made, tr_hi, tr_lo = (sem(n) for n in ("tr_made", "tr_hi", "tr_lo"))
        out_made, act_out, dve_out = sem("out_made"), [sem("act_out0"), sem("act_out1")], [sem("dve_out0"), sem("dve_out1")]
        lat_squared, lat_rstd_made, lat_scaled, lat_tr, lat_hi, lat_lo = (sem(n) for n in (
            "lat_squared", "lat_rstd_made", "lat_scaled", "lat_tr", "lat_hi", "lat_lo"))
        z_made, z_tr, z_in, b_tr, prod_made, prod_hi, prod_lo = (sem(n) for n in (
            "z_made", "z_tr", "z_in", "b_tr", "prod_made", "prod_hi", "prod_lo"))
        heads_ready, kv_act, qk_tr, qk_in, s_made, max_made, p_made, p_tr, p_in, o_made, o_in = (sem(n) for n in (
            "heads_ready", "kv_act", "qk_tr", "qk_in", "s_made", "max_made", "p_made", "p_tr", "p_in", "o_made", "o_in"))
        s_read, inv_made, gate_made, m_made = (sem(n) for n in (
            "s_read", "inv_made", "gate_made", "m_made"))
        gu_made, silu_made, hid_made, hid_tr, hT_hi_made, hT_lo_made, h_new = (sem(n) for n in (
            "gu_made", "silu_made", "hid_made", "hid_tr", "hT_hi_made", "hT_lo_made", "h_new"))
        xn_hi_made, xn_lo_made, chosen_made, ranks_made, iota_made, flag_made, sel_made, x_hi_tr, x_lo_tr, x_hi_in, x_lo_in, selT_tr, selT_in, y_hi_made, y_lo_made, back_made, back_added = (
            sem(n) for n in ("xn_hi_made", "xn_lo_made", "chosen_made", "ranks_made", "iota_made", "flag_made", "sel_made", "x_hi_tr", "x_lo_tr",
                             "x_hi_in", "x_lo_in", "selT_tr", "selT_in", "y_hi_made", "y_lo_made", "back_made", "back_added"))
        logits_made, lmax_made, lexp_made, rw_hi_made, rw_lo_made, angle_made, sines_made = (sem(n) for n in (
            "logits_made", "lmax_made", "lexp_made", "rw_hi_made", "rw_lo_made", "angle_made", "sines_made"))
        dve_link, pool_link, act_link, stored = (sem(n) for n in ("dve_link", "pool_link", "act_link", "stored"))

        B_GU, B_HT = 4, 6
        B_XHI, B_XLO, B_SELT = (2, 3), (5, 7), 2
        B_BACK = ((2, 3), (5, 7))
        OUTS = 1 + PAIRS
        def dve_value(L, pair, t):
            first = (PAIR_UKV, PAIR_GATE)[t]
            return (PAIRS - first) * L + pair - first + 1

        def wait_residual(eng, N):
            if N == 0:
                eng.wait_ge(h_in, 16)
            elif N % 2:
                for t in range(NT):
                    eng.wait_ge(dve_out[t], dve_value(N // 2, PAIRS - 1, t))
            else:
                eng.wait_ge(h_new, (4, 4 + 4 * EXPERTS)[N // 2 - 1])

        def wait_out(eng, L, pair, t):
            if pair == PAIR_UKV and t == 1:
                pair, t = pair + 1, 0
            if t == 0:
                eng.wait_ge(out_made, OUTS * L + 1 + pair + 1)
            else:
                b, j = ((BLK_CU + pair, 2) if pair < PAIR_UQ else (BLK_UQ, pair - PAIR_UQ) if pair < PAIR_UKV else
                        (BLK_UKV, pair - PAIR_UKV - 1) if pair < PAIR_GATE else (BLK_GATE + pair - PAIR_GATE, 2))
                eng.wait_ge(used[j], MIX[L] + b + 1)

        def wait_pair_free(eng, L, pair, t):
            p = pair - 2
            if p < 0:
                return
            if p < PAIR_UKV or (p < PAIR_GATE and t == 1):
                eng.wait_ge(act_out[t], (PAIR_UKV, PAIR_GATE)[t] * L + p + 1)
            else:
                eng.wait_ge(dve_out[t], dve_value(L, p, t))

        def expert_round(eng, r, step):
            def turn(p, last):
                for x in range(2):
                    final = last and x == 1
                    for i in range(2, EXPERT):
                        step(2 * p + x, i, x, gather=not final, back=False, ahead=not (final and i == EXPERT - 1))
                    if not final:
                        for i in range(2):
                            step(2 * p + x + 1, i, 1 - x, gather=False, back=i == 1, ahead=True)

            for i in range(2):
                step(0, i, 0, gather=False, back=False, ahead=True)
            with eng.Fori(0, EXPERTS // 2 - 1) as p:
                turn(p, False)
            turn(EXPERTS // 2 - 1, True)

        def second_round(eng, round_of, after=None):
            eng.wait_ge(flag_made, 1)
            over = eng.value_load(flag[0:1, 0:1], min_val=0, max_val=1)
            with eng.If(over > 0):
                round_of(1)
                if after is not None:
                    after()

        block = ctx.enter_context(nc.Block())

        @block.sync
        def _(sp):
            loaded_reg = sp.alloc_register("loaded")

            def load(b, j, first, parts, settled=False):
                at_span_start = isinstance(b, int) and b == first
                before = {FFN[0]: MIX[0], MIX[1]: FFN[0], FFN[1]: MIX[1]}.get(first) if at_span_start else first
                loaded = raw_value(b - 1, j, before) if settled or b >= 1 else None
                if not isinstance(b, int):
                    sp.reg_mov(loaded_reg, loaded)
                    loaded = sp.snap(loaded_reg)
                if settled or b >= 2:
                    sp.wait_ge(lo_made[j], b - 1)
                if settled or b >= 1:
                    sp.wait_ge(raw_in[j], loaded)
                for dst, src in parts:
                    sp.dma_start(dst, src).then_inc(raw_in[j], 16)

            def slot(b, j, n, width):
                return raw[:, b % 2, j, 0:n * width].rearrange("p (c n) -> p c n", n=width)

            def slab(b, first, w, col, width=NB):
                for j, (c0, n) in enumerate(G_CHUNKS):
                    load(b, j, first, [(slot(b, j, n, width), w[:, c0:c0 + n, col:col + width])])

            def chunks(w):
                return w.rearrange("(c p) n -> p c n", p=P)

            def gate_up(b, i, first, w_gate, w_up, settled):
                for j in range(2):
                    dst = raw[:, b % 2, j, :].rearrange("p (c w n) -> p c w n", w=2, n=HB)
                    load(b, j, first, [(dst[:, :, n, :], w[:, 4 * j:4 * j + 4, ds(i * HB, HB)])
                                       for n, w in enumerate((w_gate, w_up))], settled)

            def down(b, i, first, w_down):
                load(b, 2, first, [(slot(b, 2, HC, D), w_down[:, ds(i * HC, HC), :])], True)

            def ffn(F, first, n, w_gate, w_up, w_down):
                gate_up(F, 0, first, w_gate, w_up, True)
                with sp.Fori(1, n) as i:
                    gate_up(F + i, i, first, w_gate, w_up, True)
                    down(F + i - 1, i - 1, first, w_down)
                down(F + n - 1, n - 1, first, w_down)

            sp.dma_start(h[:, :, :], x[0].rearrange("(t p) d -> p t d", p=P)).then_inc(h_in, 16)
            for L in range(DEPTH):
                B = MIX[L]
                w_in_c = chunks(w_in[L])
                slab(B + BLK_LAT, B, w_in_c, COL_LAT, LAT)
                for s, col in enumerate((COL_C, COL_C + NB, COL_U, COL_U + NB, COL_B, COL_B + NB)):
                    slab(B + BLK_CU + s, B, w_in_c, col)
                for u in range(2):
                    slab(B + BLK_CONV + u, B, chunks(w_conv_out[L]), u * NB)
                for j in range(3):
                    b = B + BLK_UQ
                    load(b, j, B, [(slot(b, j, 2, NB), chunks(w_uq[L])[:, :, j * NB:(j + 1) * NB])])
                for j, (c0, n) in enumerate(((0, 2), (2, 1), (3, 1))):
                    b = B + BLK_UKV
                    load(b, j, B, [(raw[:, b % 2, j, 0:n * NB], w_ukv[L][:, c0 * NB:(c0 + n) * NB])])
                for g in range(4):
                    slab(B + BLK_GATE + g, B, w_in_c, COL_G + g * NB)
                for u in range(2):
                    slab(B + BLK_ATT + u, B, chunks(w_attn_out[L]), u * NB)
                for u in range(2):
                    slab(B + BLK_MIX + u, B, chunks(w_mix_out[L]), u * NB)
                if L == 0:
                    ffn(FFN[0], FFN[0], DENSE, chunks(dense_w_gate[0]), chunks(dense_w_up[0]), chunks(dense_w_down[0]))
                else:
                    eg = moe_w_gate[0].rearrange("e (c p) n -> p (e c) n", p=P)
                    eu = moe_w_up[0].rearrange("e (c p) n -> p (e c) n", p=P)
                    ed = moe_w_down[0].rearrange("e (c p) n -> p (e c) n", p=P)

                    def expert_loads(r):
                        def step(e, i, x, gather, back, ahead):
                            b = FFN[1] + EXPERT * (EXPERTS * r + e) + i
                            parity = (FFN[1] + x * EXPERT + i) % 2
                            for j in range(2):
                                dst = raw[:, parity, j, :].rearrange("p (c w n) -> p c w n", w=2, n=HB)
                                load(b, j, FFN[1], [(dst[:, :, n, :], w[:, ds(e * KC + 4 * j, 4), i * HB:(i + 1) * HB])
                                                    for n, w in enumerate((eg, eu))], True)
                            if isinstance(e, int) and e == 0 and i == 0:
                                return
                            expert_down(b - 1, e, i - 1, 1 - parity)
                            if not ahead:
                                expert_down(b, e, i, parity)

                        def expert_down(b, e, i, parity):
                            load(b, 2, FFN[1], [(raw[:, parity, 2, :].rearrange("p (c n) -> p c n", n=D),
                                                 ed[:, ds(e * HC * EXPERT + HC * i, HC), :])], True)

                        expert_round(sp, r, step)

                    expert_loads(0)
                    second_round(sp, expert_loads)
            sp.wait_ge(xs_made, 10)
            sp.dma_start(out[0].rearrange("(t p) d -> p t d", p=P), xs[:, :, :]).then_inc(stored, 16)
            sp.wait_ge(stored, 16)

        @block.gpsimd
        def _(pool):
            links = [0]

            def link(ins):
                links[0] += 1
                ins.then_inc(pool_link, 1)
                pool.wait_ge(pool_link, links[0])

            for L in range(DEPTH):
                taps = CONV_K * KC
                pool.dma_start(rowc[L * taps:(L + 1) * taps, :], conv_w[L].rearrange("k o (c p) -> (k o c) p", p=P)).then_inc(rows_in, 16)
                r = DEPTH * taps + L * LC
                pool.dma_start(rowc[r:r + 2, :], norm_q[L].rearrange("(c p) -> c p", p=P)).then_inc(rows_in, 16)
                pool.dma_start(rowc[r + 2:r + 3, :], norm_kv[L].rearrange("(c p) -> c p", p=P)).then_inc(rows_in, 16)
            pool.dma_start(gain[:, :], norm_mix[0].partition_broadcast(P)).then_inc(gain_in, 16)
            for t in range(NT):
                pool.dma_start(pos_i[:, t:t + 1], positions[0, t * P:(t + 1) * P].rearrange("(p o) -> p o", o=1)).then_inc(pos_in, 16)
            link(pool.memset(ident[:, :], 0.0))
            pool.affine_select(out=ident[:, :], in_=ident[:, :], compare_op=ALU.not_equal, fill=1.0, base=0,
                               pattern=[[-1, P]], channel_multiplier=1).then_inc(ident_made, 1)
            link(pool.memset(mask[:, :], 0.0))
            pool.memset(mask[0:CHUNK, CHUNK:P], MASKED)
            pool.memset(mask[0:CHUNK, 2 * P + CHUNK:3 * P], MASKED)
            pool.memset(minus_half, -0.5)
            pool.memset(lat_scale[:, 0:2], 1.0 / Q_LORA)
            pool.memset(lat_scale[:, 2:4], 1.0 / KV_LORA)
            inv_freq = np.float32(THETA) ** (-np.arange(0, ROPE, 2, dtype=np.float32) / np.float32(ROPE))
            for n in range(RH):
                last = pool.memset(freq[:, n:n + 1], float(inv_freq[n]))
            last.then_inc(consts_made, 1)
            pool.dma_start(rwt[:, :].rearrange("p (c e) -> p c e", e=EXPERTS),
                           router_w[0].rearrange("(c p) e -> p c e", p=P)).then_inc(router_in, 16)
            pool.dma_start(gates[:, 0, :], b_gate[0].partition_broadcast(P)).then_inc(bias_in, 16)
            pool.dma_start(gates[:, 1, :], b_gate[0].partition_broadcast(P)).then_inc(bias_in, 16)

            def norm_root(N, next_gain):
                pool.wait_ge(sq_act, N + 1)
                pool.wait_ge(sq_dve, N + 1)
                link(pool.tensor_scalar(var, sq_sum, 1.0 / D, EPS, ALU.mult, ALU.add))
                pool.tensor_tensor(rstd, var, minus_half[:, 0:2], ALU.pow).then_inc(rstd_made, 1)
                if next_gain is not None:
                    pool.wait_ge(xs_made, 2 * N + 2)
                    pool.dma_start(gain[:, :], next_gain.partition_broadcast(P)).then_inc(gain_in, 16)

            for L in range(DEPTH):
                norm_root(2 * L, None)
                pool.wait_ge(lat_squared, 4 * (L + 1))
                link(pool.tensor_tensor(lat_var, lat_sq, lat_scale, ALU.mult))
                link(pool.tensor_scalar(lat_var, lat_var, EPS, None, ALU.add))
                pool.tensor_tensor(lat_rstd, lat_var, minus_half, ALU.pow).then_inc(lat_rstd_made, 1)
                pool.wait_ge(o_made, HEADS * (L + 1))
                pool.dma_start(gain[:, :], norm_ffn[L].partition_broadcast(P)).then_inc(gain_in, 16)
                if L == 1:
                    pool.iota(iota_i[:, :], pattern=[[1, S]], base=0, channel_multiplier=0).then_inc(iota_made, 1)
                    link(pool.memset(ones[:, :], 1.0))
                    pool.affine_select(out=tri[:, :], in_=ones[:, :], compare_op=ALU.is_ge, fill=0.0, base=0,
                                       pattern=[[1, P]], channel_multiplier=-1).then_inc(iota_made, 1)
                norm_root(2 * L + 1, norm_mix[1] if L == 0 else norm_final)
                if L == 0:
                    pool.wait_ge(m_made, 4)
                    for t in range(NT):
                        pool.dma_start(gates[:, t, :], b_gate[1].partition_broadcast(P)).then_inc(bias_in, 16)
            norm_root(4, None)

        @block.scalar
        def _(act):
            def hi(b, j, n, first, settled=False):
                act.wait_ge(raw_in[j], raw_value(b, j, first))
                if settled or b >= 1:
                    act.wait_ge(used[j], b)
                act.activation(w_hi[:, j, 0:n], raw[:, b % 2, j, 0:n], ACT.Copy).then_inc(hi_made[j], 1)

            def his(L, b):
                first = MIX[L] if b < MIXER else FFN[L]
                for j in range(3 if b < MIXER else 2):
                    hi(MIX[L] + b, j, mixer_sizes(b)[j], first)

            def square_tile(N):
                wait_residual(act, N)
                act.activation(xs[:, 0, :], h[:, 0, :], ACT.Square, accum_out=sq_sum[:, 0:1]).then_inc(sq_act, 1)

            def transposed_hi(use, dst, banks=range(4)):
                for n in banks:
                    act.wait_ge(tr_made, 4 * use + n + 1)
                    act.activation(dst[:, 2 * n:2 * n + 2, :], bank[B_T + n][:, :].rearrange("p (c s) -> p c s", s=S),
                                   ACT.Copy).then_inc(tr_hi, 1)

            def out_copy(L, pair, dst):
                for t in range(NT):
                    wait_out(act, L, pair, t)
                    act.activation(dst(t), bank[2 * (pair % 2) + t][:, :], ACT.Copy).then_inc(act_out[t], 1)

            his(0, 0)
            act.wait_ge(angle_made, 1)
            act.activation(ang[:, 2:4, :, :], ang[:, 0:2, :, :], ACT.Sin).then_inc(sines_made, 1)

            def mixer(L):
                B = MIX[L]
                square_tile(2 * L)
                transposed_hi(4 * L, aT_hi)
                his(L, BLK_CU)
                for t in range(NT):
                    act.wait_ge((out_made, used[2])[t], (OUTS * L + 1, MIX[L] + BLK_LAT + 1)[t])
                    for n, (a, b) in enumerate(((0, Q_LORA), (Q_LORA, Q_LORA + KV_LORA))):
                        act.activation(mixed[:, t, a:b], bank[B_LAT + t][:, a:b], ACT.Square,
                                       accum_out=lat_sq[:, 2 * n + t:2 * n + t + 1]).then_inc(lat_squared, 1)
                for t in range(NT):
                    act.activation(mixed[:, t, LAT - ROPE:LAT], bank[B_LAT + t][:, LAT - ROPE:LAT], ACT.Copy).then_inc(lat_scaled, 1)
                act.wait_ge(lat_rstd_made, L + 1)
                for t in range(NT):
                    for n, (a, b) in enumerate(((0, Q_LORA), (Q_LORA, Q_LORA + KV_LORA))):
                        act.activation(mixed[:, t, a:b], bank[B_LAT + t][:, a:b], ACT.Copy,
                                       scale=lat_rstd[:, 2 * n + t:2 * n + t + 1]).then_inc(lat_scaled, 1)
                for p in range(6):
                    his(L, BLK_CU + p + 1)
                    out_copy(L, PAIR_CU + p, lambda t: proj[:, p // 2, t, p % 2 * NB:(p % 2 + 1) * NB])
                    if p == 1:
                        for c in range(LC):
                            act.wait_ge(lat_tr, 2 * L + (1 if c < 2 else 2))
                            act.activation(lT_hi[:, c, :], bank[B_LT + c // 2][:, c % 2 * S:(c % 2 + 1) * S], ACT.Copy,
                                           scale=cols[:, DEPTH * CONV_K * KC + L * LC + c:][:, 0:1]).then_inc(lat_hi, 1)
                    if p == 4:
                        for n in range(4):
                            act.wait_ge(z_tr, 4 * L + n + 1)
                            act.activation(zT[:, 2 * n:2 * n + 2, :], bank[B_T + n][:, :].rearrange("p (c s) -> p c s", s=S),
                                           ACT.Copy).then_inc(z_in, 1)
                for n in range(4):
                    act.wait_ge(prod_made, 4 * L + n + 1)
                    act.activation(bT_hi[:, 2 * n:2 * n + 2, :], acc[:, 2 * n:2 * n + 2, :], ACT.Copy).then_inc(prod_hi, 1)
                for u in range(2):
                    his(L, BLK_CONV + u + 1)
                    out_copy(L, PAIR_CONV + u, lambda t: mixed[:, t, u * NB:(u + 1) * NB])
                for j in range(3):
                    hi(B + BLK_UKV, j, UKV_SIZES[j], B)
                    out_copy(L, PAIR_UQ + j, lambda t: q[:, t, j * NB:(j + 1) * NB])
                for c in range(4):
                    if c:
                        j = c - 1
                        hi(B + BLK_GATE, j, SLAB_SIZES[j], B)
                    wait_out(act, L, PAIR_UKV + c, 1)
                    src = bank[2 * ((PAIR_UKV + c) % 2) + 1][:, :].rearrange("p (h d) -> p h d", d=NOPE + VD)
                    act.activation(k[:, 1, :].rearrange("p (h d) -> p h d", d=QK)[:, 4 * c:4 * c + 4, 0:NOPE],
                                   src[:, :, 0:NOPE], ACT.Copy).then_inc(kv_act, 1)
                    act.activation(v[:, 1, :].rearrange("p (h d) -> p h d", d=VD)[:, 4 * c:4 * c + 4, :],
                                   src[:, :, NOPE:], ACT.Copy).then_inc(act_out[1], 1)
                for n in range(HEADS + 3):
                    if n < HEADS:
                        act.wait_ge(qk_tr, HEADS * L + n + 1)
                        if n:
                            act.wait_ge(s_made, HEADS * L + n)
                        act.activation(qkT[0:QK, :], bank[B_QK][0:QK, :], ACT.Copy).then_inc(qk_in, 1)
                    if 1 <= n <= HEADS:
                        act.wait_ge(max_made, 2 * (HEADS * L + n))
                        if n >= 2:
                            act.wait_ge(p_tr, HEADS * L + n - 1)
                            act.wait_ge(inv_made, HEADS * L + n - 1)
                        act.activation(p_buf[:, 0:P], s_buf[:, 0:P], ACT.Exp, bias=neg_max[:, 0:1],
                                       accum_out=row_sum[:, 0:1]).then_inc(p_made, 1)
                        act.activation(p_buf[:, P:3 * P], s_buf[:, P:3 * P], ACT.Exp, bias=neg_max[:, 1:2],
                                       accum_out=row_sum[:, 1:2]).then_inc(p_made, 1)
                    if 2 <= n <= HEADS + 1:
                        act.wait_ge(p_tr, HEADS * L + n - 1)
                        if n >= 3:
                            act.wait_ge(o_made, HEADS * L + n - 2)
                        act.activation(pT[:, :], bank[B_PT][:, 0:3 * P], ACT.Copy).then_inc(p_in, 1)
                    if n < HEADS and n % 4:
                        j = n % 4 - 1
                        hi(B + BLK_GATE + n // 4 + 1, j, SLAB_SIZES[j], B)
                transposed_hi(4 * L + 1, aT_hi)
                for t in range(NT):
                    act.wait_ge(dve_out[t], dve_value(L, PAIR_GATE + 3, t))
                    act.activation(gates[:, t, :], gates[:, t, :], ACT.Sigmoid).then_inc(gate_made, 1)
                his(L, BLK_ATT + 1)
                his(L, BLK_MIX)
                transposed_hi(4 * L + 2, bT_hi)
                his(L, BLK_MIX + 1)
                if L == 0:
                    his(L, MIXER)

            def silu(F, fb):
                for t in range(NT):
                    act.wait_ge((gu_made, used[1])[t], (fb + 1, F + 1)[t])
                    act.activation(sg[:, t, :], bank[B_GU + t][:, 0:HB], ACT.Silu).then_inc(silu_made, 1)

            def hidden_hi(fb):
                act.wait_ge(hid_tr, fb + 1)
                act.activation(hT_hi[:, :, :], bank[B_HT][:, :].rearrange("p (c s) -> p c s", s=S), ACT.Copy).then_inc(hT_hi_made, 1)

            def ffn_step(F, fb, first, ahead):
                hi(F - 1, 2, SLOT, first, True)
                hidden_hi(fb - 1)
                if ahead:
                    hi(F + 1, 0, SLOT, first, True)
                    silu(F, fb)
                    hi(F + 1, 1, SLOT, first, True)

            mixer(0)
            act.wait_ge(router_in, 16)
            act.activation(rw_hi[:, :], rwt[:, :], ACT.Copy).then_inc(rw_hi_made, 1)
            square_tile(1)
            transposed_hi(3, aT_hi)
            F = FFN[0]
            hi(F + 1, 0, SLOT, F, True)
            silu(F, 0)
            hi(F + 1, 1, SLOT, F, True)
            with act.Fori(1, DENSE - 1) as i:
                ffn_step(F + i, i, F, True)
            ffn_step(F + DENSE - 1, DENSE - 1, F, False)
            hi(MIX[1], 0, LAT_SIZES[0], MIX[1])
            silu(F + DENSE - 1, DENSE - 1)
            hi(MIX[1], 1, LAT_SIZES[1], MIX[1])
            hi(F + DENSE - 1, 2, SLOT, F, True)
            hidden_hi(DENSE - 1)
            hi(MIX[1], 2, LAT_SIZES[2], MIX[1])
            mixer(1)
            square_tile(3)
            transposed_hi(7, aT_hi)
            for t in range(NT):
                act.activation(xn_hi[:, t, :], xs[:, t, :], ACT.Copy).then_inc(xn_hi_made, 1)
            act.wait_ge(lmax_made, 1)
            act.activation(rt[:, :, 5, 0:1], rt[:, :, 4, 0:1], ACT.Exp).then_inc(lexp_made, 1)

            def gathered_hi(E, x):
                act.wait_ge(x_hi_tr, E + 1)
                for n, b in enumerate(B_XHI):
                    act.activation(aT_hi[:, 4 * n:4 * n + 4, x * P:(x + 1) * P], bank[b][:, :].rearrange("p (c s) -> p c s", s=P),
                                   ACT.Copy).then_inc(x_hi_in, 1)

            def sel_transposed(E, x):
                act.wait_ge(selT_tr, E + 1)
                act.activation(selT[:, x, :], bank[B_SELT][:, 0:S], ACT.Copy).then_inc(selT_in, 1)

            def output_hi(F, E):
                act.wait_ge(used[2], F + EXPERT)
                for u in range(2):
                    act.activation(y_hi[:, u * NB:(u + 1) * NB], bank[u][:, :], ACT.Copy).then_inc(y_hi_made, 1)

            def experts(r):
                F0, E0, fb0 = FFN[1] + EXPERT * EXPERTS * r, EXPERTS * r, DENSE + EXPERT * EXPERTS * r
                gathered_hi(E0, 0)
                sel_transposed(E0, 0)
                for j in range(2):
                    expert_hi(F0, j, 0, 0)

                def step(e, i, x, gather, back, ahead):
                    b, fb = F0 + EXPERT * e + i, fb0 + EXPERT * e + i
                    if not (isinstance(e, int) and e == 0 and i == 0):
                        expert_hi(b - 1, 2, x, i - 1)
                        if back:
                            output_hi(F0 + EXPERT * (e - 1), E0 + e - 1)
                        hidden_hi_1(fb - 1)
                    if gather and i == 4:
                        gathered_hi(E0 + e + 1, 1 - x)
                    if gather and i == 5:
                        sel_transposed(E0 + e + 1, 1 - x)
                    if ahead:
                        expert_hi(b + 1, 0, x, i + 1)
                    expert_silu(b)
                    if ahead:
                        expert_hi(b + 1, 1, x, i + 1)
                    else:
                        expert_hi(b, 2, x, i)
                        hidden_hi_1(fb)
                        output_hi(F0 + EXPERT * e, E0 + e)

                expert_round(act, r, step)

            def expert_hi(b, j, x, i):
                act.wait_ge(raw_in[j], raw_value(b, j, FFN[1]))
                act.wait_ge(used[j], b)
                act.activation(w_hi[:, j, :], raw[:, (FFN[1] + x * EXPERT + i) % 2, j, :], ACT.Copy).then_inc(hi_made[j], 1)

            def expert_silu(b):
                act.wait_ge(used[1], b + 1)
                act.activation(sg[:, 0, :], bank[B_GU][:, 0:HB], ACT.Silu).then_inc(silu_made, 1)

            def hidden_hi_1(fb):
                act.wait_ge(hid_tr, fb + 1)
                act.activation(hT_hi[:, :, 0:P], bank[B_HT][:, 0:HC * P].rearrange("p (c s) -> p c s", s=P), ACT.Copy).then_inc(hT_hi_made, 1)

            experts(0)
            second_round(act, experts, lambda: act.wait_ge(h_new, 4 + 8 * EXPERTS))
            square_tile(4)

        @block.vector
        def _(dve):
            links = [0]

            def link(*ins):
                for i in ins:
                    links[0] += 1
                    i.then_inc(dve_link, 1)
                dve.wait_ge(dve_link, links[0])

            def lo(b, j, n):
                dve.wait_ge(hi_made[j], b + 1)
                dve.tensor_tensor(w_lo[:, j, 0:n], raw[:, b % 2, j, 0:n], w_hi[:, j, 0:n].bitcast(F32),
                                  ALU.subtract).then_inc(lo_made[j], 1)

            def los(L, b):
                for j in range(3 if b < MIXER else 2):
                    lo(MIX[L] + b, j, mixer_sizes(b)[j])

            def square_tile(N):
                wait_residual(dve, N)
                dve.tensor_tensor_reduce(out=xs[:, 1, :], in0=h[:, 1, :], in1=h[:, 1, :], scale=1.0, scalar=0.0,
                                         op0=ALU.mult, op1=ALU.add, accum_out=sq_sum[:, 1:2]).then_inc(sq_dve, 1)

            def scale_tokens(N):
                dve.wait_ge(rstd_made, N + 1)
                dve.wait_ge(gain_in, 16 * (N + 1))
                for t in range(NT):
                    dve.scalar_tensor_tensor(out=xs[:, t, :], in0=h[:, t, :], scalar=rstd[:, t:t + 1], in1=gain[:, :],
                                             op0=ALU.mult, op1=ALU.mult).then_inc(xs_made, 1)

            def transposed_lo(use, dst, dst_hi, banks=range(4)):
                for n in banks:
                    dve.wait_ge(tr_hi, 4 * use + n + 1)
                    dve.tensor_tensor(dst[:, 2 * n:2 * n + 2, :], bank[B_T + n][:, :].rearrange("p (c s) -> p c s", s=S),
                                      dst_hi[:, 2 * n:2 * n + 2, :].bitcast(F32), ALU.subtract).then_inc(tr_lo, 1)

            def heads_of(t, d):
                return t.rearrange("p (h d) -> p h d", d=d)

            dve.wait_ge(cols_tr, 1)
            dve.tensor_copy(cols[:, :], bank[7][:, 0:NCOL]).then_inc(cols_made, 1)
            los(0, 0)
            dve.wait_ge(pos_in, 16 * NT)
            dve.wait_ge(consts_made, 1)
            link(dve.tensor_copy(posf[:, :], pos_i[:, :]))
            link(*[dve.tensor_scalar(turns[:, 0, t, :], freq[:, :], posf[:, t:t + 1], None, ALU.mult) for t in range(NT)])
            magic = 1.5 * 2.0 ** 23
            two_pi = 2.0 * np.pi
            part1 = float(np.float32(6.28125))
            part2 = float(np.floor((two_pi - part1) * 2.0 ** 20) / 2.0 ** 20)
            part3 = float(np.float32(two_pi - part1 - part2))
            link(dve.tensor_scalar(turns[:, 1], turns[:, 0], 1.0 / two_pi, magic, ALU.mult, ALU.add))
            link(dve.tensor_scalar(turns[:, 2], turns[:, 1], magic, None, ALU.subtract))
            for part in (part1, part2, part3):
                link(dve.scalar_tensor_tensor(out=turns[:, 0], in0=turns[:, 2], scalar=-part, in1=turns[:, 0],
                                              op0=ALU.mult, op1=ALU.add))
            link(dve.tensor_scalar(ang[:, 0], turns[:, 0], 3.1415925, -3.1415925, ALU.min, ALU.max))
            dve.tensor_scalar(ang[:, 1], ang[:, 0], 0.5, None, ALU.mult).then_inc(angle_made, 1)
            dve.wait_ge(sines_made, 1)
            dve.tensor_copy(sin[:, :, :], ang[:, 2])
            link(dve.tensor_tensor(turns[:, 3], ang[:, 3], ang[:, 3], ALU.mult))
            link(dve.tensor_scalar(cos[:, :, :], turns[:, 3], -2.0, 1.0, ALU.mult, ALU.add))

            def mixer(L):
                B = MIX[L]
                square_tile(2 * L)
                scale_tokens(2 * L)
                transposed_lo(4 * L, aT_lo, aT_hi)
                los(L, BLK_CU)
                dve.wait_ge(lat_scaled, 6 * L + 2)
                k1, k2 = mixed[:, :, LAT - ROPE:LAT - RH], mixed[:, :, LAT - RH:LAT]
                kt = [rope_k[:, n, :, :] for n in range(4)]
                link(dve.tensor_tensor(kt[0], k1, cos[:, :, :], ALU.mult), dve.tensor_tensor(kt[1], k2, sin[:, :, :], ALU.mult),
                     dve.tensor_tensor(kt[2], k1, sin[:, :, :], ALU.mult), dve.tensor_tensor(kt[3], k2, cos[:, :, :], ALU.mult))
                link(dve.tensor_tensor(k_rope[:, :, 0:RH], kt[0], kt[1], ALU.subtract),
                     dve.tensor_tensor(k_rope[:, :, RH:], kt[2], kt[3], ALU.add))
                for p in range(6):
                    los(L, BLK_CU + p + 1)
                    if p == 1:
                        for c in range(LC):
                            dve.wait_ge(lat_hi, LC * L + (2 if c < 2 else 3))
                            dve.scalar_tensor_tensor(out=lT_lo[:, c, :], in0=bank[B_LT + c // 2][:, c % 2 * S:(c % 2 + 1) * S],
                                                     scalar=cols[:, DEPTH * CONV_K * KC + L * LC + c:][:, 0:1],
                                                     in1=lT_hi[:, c, :].bitcast(F32), op0=ALU.mult,
                                                     op1=ALU.subtract).then_inc(lat_lo, 1)
                    if p == 3:
                        for t in range(NT):
                            dve.wait_ge(act_out[t], (PAIR_UKV, PAIR_GATE)[t] * L + 4)
                            dve.tensor_tensor(proj[:, 0, t, :], proj[:, 0, t, :], proj[:, 1, t, :], ALU.mult).then_inc(z_made, 1)
                    if p == 4:
                        dve.wait_ge(z_in, 4 * L + 4)
                        tap = [[cols[:, (L * CONV_K + n) * KC + c:][:, 0:1] for c in range(KC)] for n in range(CONV_K)]
                        link(*[dve.tensor_scalar(acc[:, c, :], zT[:, c, :], tap[2][c], None, ALU.mult) for c in range(KC)])
                        for back in (1, 2):
                            link(*[dve.scalar_tensor_tensor(out=acc[:, c, back:], in0=zT[:, c, 0:S - back], scalar=tap[2 - back][c],
                                                            in1=acc[:, c, back:], op0=ALU.mult, op1=ALU.add) for c in range(KC)])
                for n in range(4):
                    part = acc[:, 2 * n:2 * n + 2, :]
                    dve.wait_ge(b_tr, 4 * L + n + 1)
                    dve.tensor_tensor(part, part, bank[B_T + n][:, :].rearrange("p (c s) -> p c s", s=S), ALU.mult).then_inc(prod_made, 1)
                for n in range(4):
                    part = acc[:, 2 * n:2 * n + 2, :]
                    dve.wait_ge(prod_hi, 4 * L + n + 1)
                    dve.tensor_tensor(bT_lo[:, 2 * n:2 * n + 2, :], part, bT_hi[:, 2 * n:2 * n + 2, :].bitcast(F32),
                                      ALU.subtract).then_inc(prod_lo, 1)
                los(L, BLK_CONV + 1)
                los(L, BLK_UQ)
                for j in range(3):
                    lo(B + BLK_UKV, j, UKV_SIZES[j])
                for c in range(4):
                    if c:
                        lo(B + BLK_GATE, c - 1, SLAB_SIZES[c - 1])
                    wait_out(dve, L, PAIR_UKV + c, 0)
                    src = heads_of(bank[2 * ((PAIR_UKV + c) % 2)][:, :], NOPE + VD)
                    link(dve.tensor_copy(heads_of(k[:, 0, :], QK)[:, 4 * c:4 * c + 4, 0:NOPE], src[:, :, 0:NOPE]))
                    dve.tensor_copy(heads_of(v[:, 0, :], VD)[:, 4 * c:4 * c + 4, :], src[:, :, NOPE:]).then_inc(dve_out[0], 1)
                for t in range(NT):
                    dve.tensor_copy(heads_of(k[:, t, :], QK)[:, :, NOPE:],
                                    k_rope[:, t, :].unsqueeze(1).to_broadcast([P, HEADS, ROPE])).then_inc(heads_ready, 1)
                    dve.wait_ge(act_out[t], (PAIR_UKV, PAIR_GATE)[t] * L + PAIR_UKV)
                    q1, q2 = heads_of(q[:, t, :], QK)[:, :, NOPE:NOPE + RH], heads_of(q[:, t, :], QK)[:, :, NOPE + RH:]
                    c_b, s_b = (m[:, t, :].unsqueeze(1).to_broadcast([P, HEADS, RH]) for m in (cos, sin))
                    r = [rope_t[:, n, :, :] for n in range(4)]
                    if t:
                        dve.wait_ge(heads_ready, 6 * L + 3)
                    link(dve.tensor_tensor(r[0], q1, c_b, ALU.mult), dve.tensor_tensor(r[1], q2, s_b, ALU.mult),
                         dve.tensor_tensor(r[2], q1, s_b, ALU.mult), dve.tensor_tensor(r[3], q2, c_b, ALU.mult))
                    dve.tensor_tensor(q1, r[0], r[1], ALU.subtract).then_inc(heads_ready, 1)
                    dve.tensor_tensor(q2, r[2], r[3], ALU.add).then_inc(heads_ready, 1)
                dve.wait_ge(bias_in, 32 * (L + 1))

                def add_bias(g):
                    for t in range(NT):
                        wait_out(dve, L, PAIR_GATE + g, t)
                        part = gates[:, t, g * NB:(g + 1) * NB]
                        dve.tensor_tensor(part, part, bank[2 * ((PAIR_GATE + g) % 2) + t][:, :], ALU.add).then_inc(dve_out[t], 1)

                for n in range(HEADS + 3):
                    if 2 <= n <= HEADS + 1:
                        dve.wait_ge(p_made, 2 * (HEADS * L + n - 1))
                        if n >= 4:
                            dve.wait_ge(o_in, 2 * (HEADS * L + n - 3))
                        dve.reciprocal(row_inv[n % 2], row_sum).then_inc(inv_made, 1)
                    if 1 <= n <= HEADS:
                        dve.wait_ge(s_made, HEADS * L + n)
                        if n >= 2:
                            dve.wait_ge(p_made, 2 * (HEADS * L + n - 1))
                        link(dve.scalar_tensor_tensor(out=s_buf[:, :], in0=bank[B_S][:, 0:3 * P], scalar=SCALE, in1=mask[:, :],
                                                      op0=ALU.mult, op1=ALU.add))
                        dve.reduce_max(neg_max[:, 0:1], s_buf[:, 0:P], AX, negate=True).then_inc(max_made, 1)
                        dve.reduce_max(neg_max[:, 1:2], s_buf[:, P:3 * P], AX, negate=True).then_inc(max_made, 1)
                    if n >= 3:
                        dve.wait_ge(o_made, HEADS * L + n - 2)
                        dve.wait_ge(inv_made, HEADS * L + n - 2)
                        for t in range(NT):
                            dve.tensor_scalar(xs[:, t, (n - 3) * VD:(n - 2) * VD], bank[B_O][:, t * VD:(t + 1) * VD],
                                              row_inv[(n - 1) % 2][:, t:t + 1], None, ALU.mult).then_inc(o_in, 1)
                    if n < HEADS and n % 4:
                        lo(B + BLK_GATE + n // 4 + 1, n % 4 - 1, SLAB_SIZES[n % 4 - 1])
                    elif n and n <= HEADS:
                        add_bias(n // 4 - 1)
                transposed_lo(4 * L + 1, aT_lo, aT_hi)
                los(L, BLK_ATT + 1)
                for t in range(NT):
                    dve.wait_ge(gate_made, NT * L + t + 1)
                    dve.wait_ge(act_out[t], (PAIR_UKV, PAIR_GATE)[t] * L + PAIR_CONV + 2)
                    link(dve.tensor_tensor(mixed[:, t, :], mixed[:, t, :], gates[:, t, 0:D], ALU.mult))
                for u in range(2):
                    for t in range(NT):
                        wait_out(dve, L, PAIR_ATT + u, t)
                        g_b, m = gates[:, t, D + u * NB:D + (u + 1) * NB], mixed[:, t, u * NB:(u + 1) * NB]
                        dve.tensor_tensor(g_b, g_b, bank[2 * ((PAIR_ATT + u) % 2) + t][:, :], ALU.mult).then_inc(dve_out[t], 1)
                        dve.wait_ge(dve_out[t], dve_value(L, PAIR_ATT + u, t))
                        dve.tensor_tensor(m, m, g_b, ALU.add).then_inc(m_made, 1)
                    if u == 0:
                        los(L, BLK_MIX)
                transposed_lo(4 * L + 2, bT_lo, bT_hi)
                los(L, BLK_MIX + 1)
                for u in range(2):
                    for t in range(NT):
                        wait_out(dve, L, PAIR_MIX + u, t)
                        part = h[:, t, u * NB:(u + 1) * NB]
                        dve.tensor_tensor(part, part, bank[2 * ((PAIR_MIX + u) % 2) + t][:, :], ALU.add).then_inc(dve_out[t], 1)
                    if u == 0 and L == 0:
                        los(L, MIXER)

            def hidden(fb):
                for t in range(NT):
                    dve.wait_ge(silu_made, 2 * fb + t + 1)
                    dve.tensor_tensor(hid[:, t, :], sg[:, t, :], bank[B_GU + t][:, HB:2 * HB], ALU.mult).then_inc(hid_made, 1)

            def hidden_lo(fb):
                dve.wait_ge(hT_hi_made, fb + 1)
                dve.tensor_tensor(hT_lo[:, :, :], bank[B_HT][:, :].rearrange("p (c s) -> p c s", s=S),
                                  hT_hi[:, :, :].bitcast(F32), ALU.subtract).then_inc(hT_lo_made, 1)

            def ffn_step(F, fb, ahead):
                lo(F - 1, 2, SLOT)
                hidden_lo(fb - 1)
                if ahead:
                    lo(F + 1, 0, SLOT)
                    hidden(fb)
                    lo(F + 1, 1, SLOT)

            mixer(0)
            dve.wait_ge(rw_hi_made, 1)
            dve.tensor_tensor(rw_lo[:, :], rwt[:, :], rw_hi[:, :].bitcast(F32), ALU.subtract).then_inc(rw_lo_made, 1)
            square_tile(1)
            scale_tokens(1)
            transposed_lo(3, aT_lo, aT_hi)
            F = FFN[0]
            lo(F + 1, 0, SLOT)
            hidden(0)
            lo(F + 1, 1, SLOT)
            with dve.Fori(1, DENSE - 1) as i:
                ffn_step(F + i, i, True)
            ffn_step(F + DENSE - 1, DENSE - 1, False)
            lo(MIX[1], 0, LAT_SIZES[0])
            hidden(DENSE - 1)
            lo(MIX[1], 1, LAT_SIZES[1])
            lo(F + DENSE - 1, 2, SLOT)
            hidden_lo(DENSE - 1)
            lo(MIX[1], 2, LAT_SIZES[2])
            dve.wait_ge(used[2], F + DENSE)
            for t in range(NT):
                for u in range(2):
                    part = h[:, t, u * NB:(u + 1) * NB]
                    dve.tensor_tensor(part, part, bank[2 * t + u][:, :], ALU.add).then_inc(h_new, 1)
            mixer(1)
            square_tile(3)
            scale_tokens(3)
            transposed_lo(7, aT_lo, aT_hi)
            for t in range(NT):
                dve.wait_ge(xn_hi_made, t + 1)
                dve.tensor_tensor(xn_lo[:, t, :], xs[:, t, :], xn_hi[:, t, :].bitcast(F32), ALU.subtract).then_inc(xn_lo_made, 1)
            lg, mx, ix, ixf, df, w1, w2, pick = (rt[:, :, n, :] for n in range(8))
            iota_e = rt[:, :, 8, :]
            dve.wait_ge(logits_made, 1)
            link(*[dve.tensor_copy(lg[:, t, :], bank[t][:, 0:EXPERTS]) for t in range(NT)])
            link(*[dve.memset(iota_e[:, :, n:n + 1], float(n)) for n in range(EXPERTS)])
            link(*[dve.max(mx[:, t, :], lg[:, t, :]) for t in range(NT)])
            link(*[dve.max_index(ix[:, t, :].bitcast(U32), mx[:, t, :], lg[:, t, :]) for t in range(NT)])
            link(dve.tensor_copy(ixf, ix.bitcast(U32)))
            dve.tensor_tensor(df[:, :, 0:1], mx[:, :, 1:2], mx[:, :, 0:1], ALU.subtract).then_inc(lmax_made, 1)
            dve.wait_ge(lexp_made, 1)
            link(dve.tensor_scalar(w1[:, :, 1:2], w1[:, :, 0:1], 1.0, None, ALU.add))
            link(dve.reciprocal(w1[:, :, 2:3], w1[:, :, 1:2]))
            link(dve.tensor_tensor(w1[:, :, 3:4], w1[:, :, 0:1], w1[:, :, 2:3], ALU.mult))
            for t in range(NT):
                link(dve.tensor_scalar(pick[:, t, :], iota_e[:, t, :], ixf[:, t, 0:1], w1[:, t, 2:3], ALU.is_equal, ALU.mult),
                     dve.tensor_scalar(w2[:, t, :], iota_e[:, t, :], ixf[:, t, 1:2], w1[:, t, 3:4], ALU.is_equal, ALU.mult))
                link(dve.tensor_tensor(expert_gate[:, t, :], pick[:, t, :], w2[:, t, :], ALU.add))
            for t in range(NT):
                dve.tensor_scalar(pick[:, t, :], iota_e[:, t, :], ixf[:, t, 0:1], None, ALU.is_equal).then_inc(dve_link, 1)
                dve.tensor_scalar(w2[:, t, :], iota_e[:, t, :], ixf[:, t, 1:2], None, ALU.is_equal).then_inc(dve_link, 1)
            links[0] += 2 * NT
            dve.wait_ge(dve_link, links[0])
            dve.tensor_tensor(chosen[:, :, :], pick, w2, ALU.add).then_inc(chosen_made, 1)
            dve.wait_ge(iota_made, 2)
            link(dve.tensor_copy(slot_no[:, :], iota_i[:, :]))
            dve.wait_ge(chosen_made, 1)
            dve.wait_ge(ranks_made, 1)
            for t in range(NT):
                link(dve.tensor_tensor(token_slot[:, t, :], chosen[:, t, :], bank[t][:, EXPERTS:2 * EXPERTS], ALU.mult))
            link(dve.tensor_scalar(token_slot[:, :, :], token_slot[:, :, :], -1.0, None, ALU.add))

            def expert_lo(b, j, x, i):
                dve.wait_ge(hi_made[j], b + 1)
                dve.tensor_tensor(w_lo[:, j, :], raw[:, (FFN[1] + x * EXPERT + i) % 2, j, :], w_hi[:, j, :].bitcast(F32),
                                  ALU.subtract).then_inc(lo_made[j], 1)

            def choose(r, e, E, x):
                for t in range(NT):
                    dve.tensor_scalar(sel[:, x, t, :], slot_no[:, r * P:(r + 1) * P], token_slot[:, t, ds(e, 1)], None,
                                      ALU.is_equal).then_inc(sel_made, 1)

            def gathered_lo(E, x):
                dve.wait_ge(x_lo_tr, E + 1)
                for n, b in enumerate(B_XLO):
                    dve.tensor_copy(aT_lo[:, 4 * n:4 * n + 4, x * P:(x + 1) * P],
                                    bank[b][:, :].rearrange("p (c s) -> p c s", s=P)).then_inc(x_lo_in, 1)

            def output_lo(E):
                for u in range(2):
                    dve.wait_ge(y_hi_made, 2 * E + u + 1)
                    dve.tensor_tensor(y_lo[:, u * NB:(u + 1) * NB], bank[u][:, :], y_hi[:, u * NB:(u + 1) * NB].bitcast(F32),
                                      ALU.subtract).then_inc(y_lo_made, 1)

            def add_outputs(e, E):
                for t in range(NT):
                    dve.wait_ge(back_made, 2 * E + t + 1)
                    for u in range(2):
                        part = h[:, t, u * NB:(u + 1) * NB]
                        dve.scalar_tensor_tensor(out=part, in0=bank[B_BACK[t][u]][:, :], scalar=expert_gate[:, t, ds(e, 1)],
                                                 in1=part, op0=ALU.mult, op1=ALU.add).then_inc(h_new, 1)

            def hidden_1(fb):
                dve.wait_ge(silu_made, fb + DENSE + 1)
                dve.tensor_tensor(hid[:, 0, :], sg[:, 0, :], bank[B_GU][:, HB:2 * HB], ALU.mult).then_inc(hid_made, 1)

            def hidden_lo_1(fb):
                dve.wait_ge(hT_hi_made, fb + 1)
                dve.tensor_tensor(hT_lo[:, :, 0:P], bank[B_HT][:, 0:HC * P].rearrange("p (c s) -> p c s", s=P),
                                  hT_hi[:, :, 0:P].bitcast(F32), ALU.subtract).then_inc(hT_lo_made, 1)

            def experts(r):
                F0, E0, fb0 = FFN[1] + EXPERT * EXPERTS * r, EXPERTS * r, DENSE + EXPERT * EXPERTS * r
                choose(r, 0, E0, 0)
                gathered_lo(E0, 0)
                for j in range(2):
                    expert_lo(F0, j, 0, 0)

                def step(e, i, x, gather, back, ahead):
                    b, fb = F0 + EXPERT * e + i, fb0 + EXPERT * e + i
                    if not (isinstance(e, int) and e == 0 and i == 0):
                        expert_lo(b - 1, 2, x, i - 1)
                        if back:
                            output_lo(E0 + e - 1)
                        hidden_lo_1(fb - 1)
                    if gather and i == 2:
                        choose(r, e + 1, E0 + e + 1, 1 - x)
                    if gather and i == 4:
                        gathered_lo(E0 + e + 1, 1 - x)
                    if ahead:
                        expert_lo(b + 1, 0, x, i + 1)
                    hidden_1(fb)
                    if ahead:
                        expert_lo(b + 1, 1, x, i + 1)
                        if back:
                            add_outputs(e - 1, E0 + e - 1)
                    else:
                        expert_lo(b, 2, x, i)
                        hidden_lo_1(fb)
                        output_lo(E0 + e)
                        add_outputs(e, E0 + e)

                expert_round(dve, r, step)

            link(dve.tensor_copy(counts[:, :], bank[0][:, 2 * EXPERTS:3 * EXPERTS]))
            link(dve.reduce_max(small[:, 40:41], counts[:, :], AX))
            link(dve.tensor_scalar(small[:, 41:42], small[:, 40:41], float(P), None, ALU.is_gt))
            dve.tensor_copy(flag[:, :], small[:, 41:42]).then_inc(flag_made, 1)
            experts(0)
            second_round(dve, experts, lambda: dve.wait_ge(h_new, 4 + 8 * EXPERTS))
            square_tile(4)
            scale_tokens(4)

        @block.tensor
        def _(pe):
            def product(dst, x_hi, x_lo, b_hi, b_lo, start, stop):
                pe.matmul(dst, x_hi, b_hi, start=start, stop=False)
                pe.matmul(dst, x_hi, b_lo, start=False, stop=False)
                return pe.matmul(dst, x_lo, b_hi, start=False, stop=stop)

            def tile(m, c, t):
                return m[:, c, t * P:(t + 1) * P]

            def w(j, c, n, width, m):
                return m[:, j, c * width:c * width + n]

            def slab(L, b, pair, x_hi, x_lo, before=None):
                for j, (c0, nc_) in enumerate(G_CHUNKS):
                    pe.wait_ge(lo_made[j], MIX[L] + b + 1)
                    for t in range(NT):
                        if j == 0:
                            wait_pair_free(pe, L, pair, t)
                        dst = bank[2 * (pair % 2) + t][:, :]
                        for c in range(nc_):
                            last = product(dst, tile(x_hi, c0 + c, t), tile(x_lo, c0 + c, t), w(j, c, NB, NB, w_hi),
                                           w(j, c, NB, NB, w_lo), c0 + c == 0, c0 + c == KC - 1)
                        if j == 2 and t == 0:
                            last.then_inc(out_made, 1)
                    last.then_inc(used[j], 1)

            def transpose_tokens(src, use, halves=(0, 1)):
                for u in halves:
                    for n in (2 * u, 2 * u + 1):
                        for c in (2 * n, 2 * n + 1):
                            for t in range(NT):
                                last = pe.transpose(bank[B_T + n][:, (c % 2) * S + t * P:(c % 2) * S + (t + 1) * P],
                                                    src(t)[:, c * P:(c + 1) * P], ident[:, :])
                        last.then_inc(use, 1)

            def mixer(L):
                pe.wait_ge(xs_made, 4 * L + 2)
                transpose_tokens(lambda t: xs[:, t, :], tr_made)
                pe.wait_ge(tr_lo, 16 * L + 4)
                for j, (c0, nc_) in enumerate(G_CHUNKS):
                    pe.wait_ge(lo_made[j], MIX[L] + BLK_LAT + 1)
                    for t in range(NT):
                        for c in range(nc_):
                            last = product(bank[B_LAT + t][:, 0:LAT], tile(aT_hi, c0 + c, t), tile(aT_lo, c0 + c, t),
                                           w(j, c, LAT, LAT, w_hi), w(j, c, LAT, LAT, w_lo), c0 + c == 0, c0 + c == KC - 1)
                        if j == 2 and t == 0:
                            last.then_inc(out_made, 1)
                    last.then_inc(used[j], 1)
                for p in range(6):
                    if p == 5:
                        pe.wait_ge(z_made, NT * (L + 1))
                        pe.wait_ge(lat_scaled, 6 * (L + 1))
                        pe.wait_ge(lat_lo, LC * (L + 1))
                        transpose_tokens(lambda t: proj[:, 0, t, :], z_tr)
                    slab(L, BLK_CU + p, PAIR_CU + p, aT_hi, aT_lo)
                    if p == 1:
                        pe.wait_ge(lat_scaled, 6 * (L + 1))
                        for c in range(LC):
                            for t in range(NT):
                                last = pe.transpose(bank[B_LT + c // 2][:, c % 2 * S + t * P:c % 2 * S + (t + 1) * P],
                                                    mixed[:, t, c * P:(c + 1) * P], ident[:, :])
                            if c:
                                last.then_inc(lat_tr, 1)
                for t in range(NT):
                    pe.wait_ge(act_out[t], (PAIR_UKV, PAIR_GATE)[t] * L + PAIR_CONV)
                pe.wait_ge(z_in, 4 * (L + 1))
                transpose_tokens(lambda t: proj[:, 2, t, :], b_tr)
                pe.wait_ge(prod_lo, 4 * (L + 1))
                for u in range(2):
                    slab(L, BLK_CONV + u, PAIR_CONV + u, bT_hi, bT_lo)
                for j in range(3):
                    pe.wait_ge(lo_made[j], MIX[L] + BLK_UQ + 1)
                    for t in range(NT):
                        wait_pair_free(pe, L, PAIR_UQ + j, t)
                        for c in range(2):
                            last = product(bank[2 * ((PAIR_UQ + j) % 2) + t][:, :], tile(lT_hi, c, t), tile(lT_lo, c, t),
                                           w(j, c, NB, NB, w_hi), w(j, c, NB, NB, w_lo), c == 0, c == 1)
                        if t == 0:
                            last.then_inc(out_made, 1)
                    last.then_inc(used[j], 1)
                for c, (j, n) in enumerate(((0, 0), (0, 1), (1, 0), (2, 0))):
                    pe.wait_ge(lo_made[j], MIX[L] + BLK_UKV + 1)
                    for t in range(NT):
                        wait_pair_free(pe, L, PAIR_UKV + c, t)
                        last = product(bank[2 * ((PAIR_UKV + c) % 2) + t][:, :], tile(lT_hi, 2, t), tile(lT_lo, 2, t),
                                       w(j, n, NB, NB, w_hi), w(j, n, NB, NB, w_lo), True, True)
                        if t == 0:
                            last.then_inc(out_made, 1)
                    if c:
                        last.then_inc(used[j], 1)
                for n in range(HEADS + 3):
                    if n < HEADS:
                        g, b = n // 4, BLK_GATE + n // 4
                        for c in (2 * (n % 4), 2 * (n % 4) + 1):
                            j = c // 3
                            if c % 3 == 0:
                                pe.wait_ge(lo_made[j], MIX[L] + b + 1)
                            for t in range(NT):
                                if c == 0:
                                    wait_pair_free(pe, L, PAIR_GATE + g, t)
                                last = product(bank[2 * ((PAIR_GATE + g) % 2) + t][:, :], tile(aT_hi, c, t), tile(aT_lo, c, t),
                                               w(j, c % 3, NB, NB, w_hi), w(j, c % 3, NB, NB, w_lo), c == 0, c == KC - 1)
                                if c == KC - 1 and t == 0:
                                    last.then_inc(out_made, 1)
                            if c in (2, 5, 7):
                                last.then_inc(used[j], 1)
                        if n == 0:
                            pe.wait_ge(heads_ready, 6 * (L + 1))
                            pe.wait_ge(kv_act, 4 * (L + 1))
                            for t in range(NT):
                                pe.wait_ge((dve_out, act_out)[t][t], dve_value(L, PAIR_UKV + 3, 0) if t == 0 else PAIR_GATE * (L + 1))
                        else:
                            pe.wait_ge(qk_in, HEADS * L + n)
                        for m, src in enumerate((q, k)):
                            for t in range(NT):
                                last = pe.transpose(bank[B_QK][0:QK, m * S + t * P:m * S + (t + 1) * P],
                                                    src[:, t, n * QK:(n + 1) * QK], ident[:, :])
                        last.then_inc(qk_tr, 1)
                    if 1 <= n <= HEADS:
                        pe.wait_ge(qk_in, HEADS * L + n)
                        if n >= 2:
                            pe.wait_ge(max_made, 2 * (HEADS * L + n - 1))
                        for t in range(NT):
                            last = pe.matmul(bank[B_S][:, t * P:(2 * t + 1) * P], qkT[0:QK, t * P:(t + 1) * P],
                                             qkT[0:QK, S:S + (t + 1) * P], start=True, stop=True)
                        last.then_inc(s_made, 1)
                    if 2 <= n <= HEADS + 1:
                        pe.wait_ge(p_made, 2 * (HEADS * L + n - 1))
                        if n >= 3:
                            pe.wait_ge(p_in, HEADS * L + n - 2)
                        for m in range(3):
                            last = pe.transpose(bank[B_PT][:, m * P:(m + 1) * P], p_buf[:, m * P:(m + 1) * P], ident[:, :])
                        last.then_inc(p_tr, 1)
                    if n >= 3:
                        pe.wait_ge(p_in, HEADS * L + n - 2)
                        if n >= 4:
                            pe.wait_ge(o_in, 2 * (HEADS * L + n - 3))
                        for t, (m, kt, start, stop) in zip((0, 1, 1), ((0, 0, True, True), (1, 0, True, False), (2, 1, False, True))):
                            last = pe.matmul(bank[B_O][:, t * VD:(t + 1) * VD], pT[:, m * P:(m + 1) * P],
                                             v[:, kt, (n - 3) * VD:(n - 2) * VD], start=start, stop=stop)
                        last.then_inc(o_made, 1)
                pe.wait_ge(o_in, 2 * HEADS * (L + 1))
                transpose_tokens(lambda t: xs[:, t, :], tr_made)
                pe.wait_ge(tr_lo, 16 * L + 8)
                for u in range(2):
                    slab(L, BLK_ATT + u, PAIR_ATT + u, aT_hi, aT_lo)
                pe.wait_ge(m_made, 4 * L + 4)
                transpose_tokens(lambda t: mixed[:, t, :], tr_made)
                pe.wait_ge(tr_lo, 16 * L + 12)
                for u in range(2):
                    slab(L, BLK_MIX + u, PAIR_MIX + u, bT_hi, bT_lo)

            def gate_up(F, fb, j):
                pe.wait_ge(lo_made[j], F + 1)
                for t in range(NT):
                    if j == 0 and not (isinstance(fb, int) and fb == 0):
                        pe.wait_ge(hid_made, 2 * fb - 1 + t)
                    for c in range(4):
                        last = product(bank[B_GU + t][:, :], tile(aT_hi, 4 * j + c, t), tile(aT_lo, 4 * j + c, t),
                                       w(j, c, NB, NB, w_hi), w(j, c, NB, NB, w_lo), j == 0 and c == 0, j == 1 and c == 3)
                    if j == 1 and t == 0:
                        last.then_inc(gu_made, 1)
                last.then_inc(used[j], 1)

            def hidden_transposes(fb):
                pe.wait_ge(hid_made, 2 * fb + 2)
                for c in range(HC):
                    for t in range(NT):
                        last = pe.transpose(bank[B_HT][:, c * S + t * P:c * S + (t + 1) * P], hid[:, t, c * P:(c + 1) * P], ident[:, :])
                last.then_inc(hid_tr, 1)

            def down(F, fb, start, stop):
                pe.wait_ge(hT_lo_made, fb + 1)
                pe.wait_ge(lo_made[2], F + 1)
                for t in range(NT):
                    for u in range(2):
                        for c in range(HC):
                            last = product(bank[2 * t + u][:, :], tile(hT_hi, c, t), tile(hT_lo, c, t),
                                           w_hi[:, 2, c * D + u * NB:c * D + (u + 1) * NB], w_lo[:, 2, c * D + u * NB:c * D + (u + 1) * NB],
                                           start and c == 0, stop and c == HC - 1)
                last.then_inc(used[2], 1)

            def ffn_step(F, fb, start):
                gate_up(F, fb, 0)
                hidden_transposes(fb - 1)
                gate_up(F, fb, 1)
                down(F - 1, fb - 1, start, False)

            pe.wait_ge(rows_in, 16 * 3 * DEPTH)
            pe.wait_ge(ident_made, 1)
            pe.transpose(bank[7][:, 0:NCOL], rowc[:, :], ident[0:NCOL, 0:NCOL]).then_inc(cols_tr, 1)
            pe.wait_ge(cols_made, 1)
            mixer(0)
            F = FFN[0]
            pe.wait_ge(xs_made, 4)
            transpose_tokens(lambda t: xs[:, t, :], tr_made)
            pe.wait_ge(tr_lo, 16)
            for j in range(2):
                gate_up(F, 0, j)
            ffn_step(F + 1, 1, True)
            with pe.Fori(2, DENSE) as i:
                ffn_step(F + i, i, False)
            hidden_transposes(DENSE - 1)
            down(F + DENSE - 1, DENSE - 1, False, True)
            pe.wait_ge(h_new, 4)
            mixer(1)
            pe.wait_ge(xs_made, 8)
            transpose_tokens(lambda t: xs[:, t, :], tr_made)
            pe.wait_ge(tr_lo, 32)
            pe.wait_ge(rw_lo_made, 1)
            for t in range(NT):
                for c in range(KC):
                    e8 = slice(c * EXPERTS, (c + 1) * EXPERTS)
                    last = product(bank[t][:, 0:EXPERTS], tile(aT_hi, c, t), tile(aT_lo, c, t), rw_hi[:, e8], rw_lo[:, e8],
                                   c == 0, c == KC - 1)
            last.then_inc(logits_made, 1)
            pe.wait_ge(chosen_made, 1)
            pe.wait_ge(iota_made, 2)
            ranks = slice(EXPERTS, 2 * EXPERTS)
            pe.matmul(bank[0][:, ranks], tri[:, :], chosen[:, 0, :], start=True, stop=True)
            pe.matmul(bank[1][:, ranks], ones[:, :], chosen[:, 0, :], start=True, stop=False)
            pe.matmul(bank[1][:, ranks], tri[:, :], chosen[:, 1, :], start=False, stop=True)
            for t in range(NT):
                last = pe.matmul(bank[0][:, 2 * EXPERTS:3 * EXPERTS], ones[:, :], chosen[:, t, :], start=t == 0, stop=t == 1)
            last.then_inc(ranks_made, 1)

            def gather(E, x, part, src, made):
                for n, b in enumerate(part):
                    for c in range(4):
                        for t in range(NT):
                            last = pe.matmul(bank[b][:, c * P:(c + 1) * P], src[:, t, (4 * n + c) * P:(4 * n + c + 1) * P],
                                             sel[:, x, t, :], start=t == 0, stop=t == 1)
                last.then_inc(made, 1)

            def transpose_sel(E, x):
                pe.wait_ge(x_hi_in, 2 * E + 2)
                for t in range(NT):
                    last = pe.transpose(bank[B_SELT][:, t * P:(t + 1) * P], sel[:, x, t, :].bitcast(F32), ident[:, :])
                last.then_inc(selT_tr, 1)

            def bring_back(E, x):
                pe.wait_ge(selT_in, E + 1)
                pe.wait_ge(y_lo_made, 2 * E + 2)
                for t in range(NT):
                    for u in range(2):
                        dst = bank[B_BACK[t][u]][:, :]
                        pe.matmul(dst, selT[:, x, t * P:(t + 1) * P], y_hi[:, u * NB:(u + 1) * NB], start=True, stop=False)
                        last = pe.matmul(dst, selT[:, x, t * P:(t + 1) * P], y_lo[:, u * NB:(u + 1) * NB], start=False, stop=True)
                    last.then_inc(back_made, 1)

            def expert_gate_up(b, fb, x, j):
                pe.wait_ge(lo_made[j], b + 1)
                if j == 0:
                    pe.wait_ge(hid_made, fb + DENSE)
                for c in range(4):
                    last = product(bank[B_GU][:, :], tile(aT_hi, 4 * j + c, x), tile(aT_lo, 4 * j + c, x),
                                   w(j, c, NB, NB, w_hi), w(j, c, NB, NB, w_lo), j == 0 and c == 0, j == 1 and c == 3)
                last.then_inc(used[j], 1)

            def expert_transposes(fb):
                pe.wait_ge(hid_made, fb + DENSE + 1)
                for c in range(HC):
                    last = pe.transpose(bank[B_HT][:, c * P:(c + 1) * P], hid[:, 0, c * P:(c + 1) * P], ident[:, :])
                last.then_inc(hid_tr, 1)

            def expert_down(b, fb, i):
                pe.wait_ge(hT_lo_made, fb + 1)
                pe.wait_ge(lo_made[2], b + 1)
                for u in range(2):
                    for c in range(HC):
                        last = product(bank[u][:, :], tile(hT_hi, c, 0), tile(hT_lo, c, 0),
                                       w_hi[:, 2, c * D + u * NB:c * D + (u + 1) * NB], w_lo[:, 2, c * D + u * NB:c * D + (u + 1) * NB],
                                       i == 0 and c == 0, i == EXPERT - 1 and c == HC - 1)
                last.then_inc(used[2], 1)

            def experts(r):
                F0, E0, fb0 = FFN[1] + EXPERT * EXPERTS * r, EXPERTS * r, DENSE + EXPERT * EXPERTS * r
                pe.wait_ge(sel_made, 2 * E0 + 2)
                pe.wait_ge(xn_lo_made, NT)
                if r:
                    pe.wait_ge(h_new, 4 + 4 * EXPERTS)
                gather(E0, 0, B_XHI, xn_hi, x_hi_tr)
                gather(E0, 0, B_XLO, xn_lo, x_lo_tr)
                transpose_sel(E0, 0)
                pe.wait_ge(x_lo_in, 2 * E0 + 2)

                def step(e, i, x, gather_next, back, ahead):
                    b, fb, E = F0 + EXPERT * e + i, fb0 + EXPERT * e + i, E0 + e
                    first = isinstance(e, int) and e == 0 and i == 0
                    if gather_next and i == 3:
                        pe.wait_ge(sel_made, 2 * (E + 1) + 2)
                        pe.wait_ge(h_new, 4 + 4 * E)
                    if i == 0 and not first:
                        pe.wait_ge(x_lo_in, 2 * E + 2)
                    expert_gate_up(b, fb, x, 0)
                    if gather_next and i == 3:
                        gather(E + 1, 1 - x, B_XHI, xn_hi, x_hi_tr)
                    if not first:
                        expert_transposes(fb - 1)
                    expert_gate_up(b, fb, x, 1)
                    if gather_next and i == 3:
                        gather(E + 1, 1 - x, B_XLO, xn_lo, x_lo_tr)
                    if gather_next and i == 4:
                        transpose_sel(E + 1, 1 - x)
                    if back:
                        bring_back(E - 1, 1 - x)
                    if not first:
                        expert_down(b - 1, fb - 1, (i - 1) % EXPERT)
                    if not ahead:
                        expert_transposes(fb)
                        expert_down(b, fb, i)
                        bring_back(E, x)

                expert_round(pe, r, lambda e, i, x, gather, back, ahead: step(e, i, x, gather, back, ahead))

            experts(0)
            second_round(pe, experts)


_INS = ["x", "positions", "norm_mix", "w_in", "b_gate", "conv_w", "w_conv_out", "norm_q", "norm_kv", "w_uq", "w_ukv",
        "w_attn_out", "w_mix_out", "norm_ffn", "dense_w_gate", "dense_w_up", "dense_w_down", "router_w",
        "moe_w_gate", "moe_w_up", "moe_w_down", "norm_final"]


def kernel(**inputs):
    import numpy as _np
    import concourse.bacc as _bacc
    from concourse import mybir as _mybir
    from concourse.bass_utils import run_bass_kernel_spmd as _run

    nc = _bacc.Bacc("TRN2", target_bir_lowering=False, num_devices=1)
    arrays, args = {}, []
    for name in _INS:
        a = _np.ascontiguousarray(inputs[name])
        arrays[f"in_{name}"] = a
        args.append(nc.dram_tensor(f"in_{name}", a.shape, _mybir.dt.from_np(a.dtype), kind="ExternalInput").ap())
    args.append(nc.dram_tensor("out_0", (1, S, D), F32, kind="ExternalOutput").ap())
    build_trunk(nc, *args)
    r = _run(nc, [arrays], core_ids=[0])
    return r.results[0]["out_0"]
```

```python
from contextlib import ExitStack

import concourse.bass as bass
import numpy as np
from concourse import mybir

F32 = mybir.dt.float32
F32R = mybir.dt.float32r
I32 = mybir.dt.int32
U32 = mybir.dt.uint32
ACT = mybir.ActivationFunctionType
ALU = mybir.AluOpType
AX = mybir.AxisListType.X
ds = bass.ds

P = 128
D = 1024
KC = D // P
S = 256
NT = S // P
DEPTH = 2
CHUNK = 64
CONV_K = 3
HEADS, NOPE, ROPE, VD = 16, 64, 32, 64
QK = NOPE + ROPE
RH = ROPE // 2
Q_LORA, KV_LORA = 256, 128
LAT = Q_LORA + KV_LORA + ROPE
LC = (Q_LORA + KV_LORA) // P
F_DENSE, F_EXPERT, EXPERTS = 2816, 1792, 8
EPS = 1e-6
THETA = 10000.0
SCALE = float(QK) ** -0.5
MASKED = -1e30
NB = 512
HB = 256
HC = HB // P
SLOT = 2048
G_CHUNKS = ((0, 3), (3, 3), (6, 2))
COL_B, COL_C, COL_U, COL_LAT, COL_G = 0, D, 2 * D, 3 * D, 3 * D + LAT

BLK_LAT, BLK_CU, BLK_B, BLK_GATE0, BLK_UQ, BLK_UKV, BLK_CONV, BLK_GATE, BLK_ATT, BLK_MIX, MIXER = (
    0, 1, 5, 7, 8, 9, 10, 12, 15, 17, 19)
DENSE, EXPERT = F_DENSE // HB, F_EXPERT // HB
MIX = (0, MIXER + DENSE)
FFN = (MIXER, 2 * MIXER + DENSE)

SLAB_SIZES = tuple(n * NB for _, n in G_CHUNKS)
LAT_SIZES = tuple(n * LAT for _, n in G_CHUNKS)
UQ_SIZES = (2 * NB,) * 3
UKV_SIZES = (2 * NB, NB, NB)
FFN_SIZES = (SLOT,) * 3


def mixer_sizes(b):
    return {BLK_LAT: LAT_SIZES, BLK_UQ: UQ_SIZES, BLK_UKV: UKV_SIZES, MIXER: FFN_SIZES}.get(b, SLAB_SIZES)


def raw_value(block, j, first):
    if j == 2:
        return 16 * (block + 1)
    doubled = {MIX[0]: 0, FFN[0]: 0, MIX[1]: DENSE, FFN[1]: DENSE}[first]
    return 16 * (first + doubled) + (32 if first in FFN else 16) * (block - first + 1)


GRANULE_AHEAD = {6 * g + s: (BLK_GATE + g + 1, j) for g in range(3) for s, j in ((2, 0), (4, 1), (6, 2))}

PAIR_CU, PAIR_B, PAIR_GATE0, PAIR_UQ, PAIR_UKV, PAIR_CONV, PAIR_GATE, PAIR_ATT, PAIR_MIX, PAIRS = (
    0, 4, 6, 7, 10, 14, 16, 19, 21, 23)
GATE_BLK = (BLK_GATE0, BLK_GATE, BLK_GATE + 1, BLK_GATE + 2)
GATE_PAIR = (PAIR_GATE0, PAIR_GATE, PAIR_GATE + 1, PAIR_GATE + 2)
GATE_SLOTS = 6


def build_trunk(nc, x, positions, norm_mix, w_in, b_gate, conv_w, w_conv_out, norm_q, norm_kv, w_uq, w_ukv,
                w_attn_out, w_mix_out, norm_ffn, dense_w_gate, dense_w_up, dense_w_down, router_w,
                moe_w_gate, moe_w_up, moe_w_down, norm_final, out):
    ctx = ExitStack()
    with ctx:
        sizeof = 4
        at = [(nc.sbuf_base + 31) // 32 * 32]

        def place(name, shape, dt=F32):
            t = nc.alloc_sbuf_tensor_at(name, shape, dt, offset=at[0])
            at[0] += (int(np.prod(shape[1:])) * sizeof + 31) // 32 * 32
            return t

        def regions(*groups):
            start, end, got = at[0], at[0], []
            for group in groups:
                at[0] = start
                got += [place(*t) for t in group]
                end = max(end, at[0])
            at[0] = end
            return got

        def sem(name):
            return ctx.enter_context(nc.semaphore(name))

        raw = place("raw", [P, 2, 3, SLOT])
        w_hi = place("w_hi", [P, 3, SLOT], F32R)
        w_lo = place("w_lo", [P, 3, SLOT], F32R)
        h = place("h", [P, NT, D])
        aT_hi = place("aT_hi", [P, KC, S], F32R)
        aT_lo = place("aT_lo", [P, KC, S], F32R)
        ident = place("ident", [P, P])
        mask = place("mask", [P, 3 * P])
        cos = place("cos", [P, NT, RH])
        sin = place("sin", [P, NT, RH])
        NCOL = DEPTH * (CONV_K * KC + LC)
        cols = place("cols", [P, NCOL])
        rwt = place("rwt", [P, KC * EXPERTS])
        rw_hi = place("rw_hi", [P, KC * EXPERTS], F32R)
        rw_lo = place("rw_lo", [P, KC * EXPERTS], F32R)
        expert_gate = place("expert_gate", [P, NT, EXPERTS])
        rope_k = place("rope_k", [P, 4, NT, RH])
        k_rope = place("k_rope", [P, NT, ROPE])
        small = place("small", [P, 64])
        sq_sum, var, rstd = small[:, 0:2], small[:, 2:4], small[:, 4:6]
        lat_sq, lat_var, lat_rstd = small[:, 6:10], small[:, 10:14], small[:, 14:18]
        minus_half = small[:, 18:22]
        neg_max = small[:, 22:24]
        row_sum = small[:, 24:26]
        row_inv = (small[:, 26:28], small[:, 32:34])
        lat_scale = small[:, 28:32]
        mixed, y_hi, y_lo = regions(
            [("mixed", [P, NT, D])],
            [("y_hi", [P, D], F32R), ("y_lo", [P, D], F32R)])
        gates, xn_hi, xn_lo = regions(
            [("gates", [P, NT, 2 * D])],
            [("xn_hi", [P, NT, D], F32R), ("xn_lo", [P, NT, D], F32R)])
        xs, lT_hi, lT_lo = regions(
            [("xs", [P, NT, D])],
            [("lT_hi", [P, LC, S], F32R), ("lT_lo", [P, LC, S], F32R)])
        (proj, zT, q, k, v, sg, hid, hT_hi, hT_lo, rt, gain, sel, selT, slot_no, token_slot, chosen, tri, ones, counts, flag, iota_i, ang, turns, rowc, pos_i, posf, freq) = regions(
            [("proj", [P, 3, NT, D]), ("zT", [P, KC, S])],
            [("q", [P, NT, HEADS * QK]), ("k", [P, NT, HEADS * QK]), ("v", [P, NT, HEADS * VD])],
            [("sg", [P, NT, HB]), ("hid", [P, NT, HB]),
             ("hT_hi", [P, HC, S], F32R), ("hT_lo", [P, HC, S], F32R),
             ("rt", [P, NT, 11, EXPERTS]),
             ("gain", [P, D]),
             ("sel", [P, 2, NT, P], F32R),
             ("selT", [P, 2, S], F32R),
             ("slot_no", [P, S]), ("token_slot", [P, NT, EXPERTS]), ("chosen", [P, NT, EXPERTS]),
             ("tri", [P, P]), ("ones", [P, P]), ("counts", [P, 8]), ("flag", [P, 1], I32), ("iota_i", [P, S], I32)],
            [("ang", [P, 4, NT, RH]), ("turns", [P, 4, NT, RH]), ("rowc", [NCOL, P]),
             ("pos_i", [P, NT], I32), ("posf", [P, NT]), ("freq", [P, RH])])
        acc = proj[:, 1, :, :].rearrange("p t (c s) -> p (t c) s", s=S)
        bT_hi, bT_lo, qkT, s_buf, p_buf, pT = regions(
            [("bT_hi", [P, KC, S], F32R), ("bT_lo", [P, KC, S], F32R)],
            [("qkT", [P, 2 * S]), ("s_buf", [P, 3 * P]), ("p_buf", [P, 3 * P]), ("pT", [P, 3 * P])])
        rope_t = mixed[:, 0, :].rearrange("p (n h d) -> p n h d", n=4, h=HEADS)
        assert at[0] <= nc.sbuf_usable_end, at[0] - nc.sbuf_usable_end

        bank = [ctx.enter_context(nc.psum_tensor(f"bank{i}", [P, NB], F32)) for i in range(8)]
        B_QK, B_S, B_PT, B_O = 4, 5, 6, 7
        B_T = 4
        B_LAT, B_LT = 4, 6

        raw_in = [sem(f"raw_in{j}") for j in range(3)]
        hi_made = [sem(f"hi_made{j}") for j in range(3)]
        lo_made = [sem(f"lo_made{j}") for j in range(3)]
        used = [sem(f"used{j}") for j in range(3)]
        h_in, rows_in, gain_in, bias_in, router_in, pos_in = (sem(n) for n in (
            "h_in", "rows_in", "gain_in", "bias_in", "router_in", "pos_in"))
        ident_made, consts_made, cols_tr, cols_made = (sem(n) for n in ("ident_made", "consts_made", "cols_tr", "cols_made"))
        sq_act, sq_dve, rstd_made, xs_made = (sem(n) for n in ("sq_act", "sq_dve", "rstd_made", "xs_made"))
        tr_made, tr_hi, tr_lo = (sem(n) for n in ("tr_made", "tr_hi", "tr_lo"))
        out_made, act_out, dve_out = sem("out_made"), [sem("act_out0"), sem("act_out1")], [sem("dve_out0"), sem("dve_out1")]
        lat_squared, lat_rstd_made, lat_scaled, lat_tr, lat_hi, lat_lo = (sem(n) for n in (
            "lat_squared", "lat_rstd_made", "lat_scaled", "lat_tr", "lat_hi", "lat_lo"))
        z_made, z_tr, z_in, b_tr, prod_made, prod_hi, prod_lo = (sem(n) for n in (
            "z_made", "z_tr", "z_in", "b_tr", "prod_made", "prod_hi", "prod_lo"))
        heads_ready, kv_act, qk_tr, qk_in, s_made, max_made, p_made, p_tr, p_in, o_made, o_in = (sem(n) for n in (
            "heads_ready", "kv_act", "qk_tr", "qk_in", "s_made", "max_made", "p_made", "p_tr", "p_in", "o_made", "o_in"))
        inv_made, gate_made, m_made = (sem(n) for n in ("inv_made", "gate_made", "m_made"))
        gu_made, silu_made, hid_made, hid_tr, hT_hi_made, hT_lo_made, h_new = (sem(n) for n in (
            "gu_made", "silu_made", "hid_made", "hid_tr", "hT_hi_made", "hT_lo_made", "h_new"))
        xn_hi_made, xn_lo_made, chosen_made, ranks_made, iota_made, flag_made, sel_made, x_hi_tr, x_lo_tr, x_hi_in, x_lo_in, selT_tr, selT_in, y_hi_made, y_lo_made, back_made = (
            sem(n) for n in ("xn_hi_made", "xn_lo_made", "chosen_made", "ranks_made", "iota_made", "flag_made", "sel_made", "x_hi_tr", "x_lo_tr",
                             "x_hi_in", "x_lo_in", "selT_tr", "selT_in", "y_hi_made", "y_lo_made", "back_made"))
        logitsT_made, logitsT_in, logits_made, lmax_made, lexp_made, rw_hi_made, rw_lo_made, angle_made, sines_made = (sem(n) for n in (
            "logitsT_made", "logitsT_in", "logits_made", "lmax_made", "lexp_made", "rw_hi_made", "rw_lo_made", "angle_made", "sines_made"))
        down_made, dve_link, pool_link, stored = (sem(n) for n in ("down_made", "dve_link", "pool_link", "stored"))

        B_GU, B_HT = 4, 6
        B_XHI, B_XLO, B_SELT = (2, 3), (5, 7), 2
        B_BACK = ((2, 3), (5, 7))
        OUTS = 1 + PAIRS

        def by_dve(pair, t):
            return pair == PAIR_GATE0 or pair >= PAIR_GATE or (t == 0 and PAIR_UKV <= pair < PAIR_CONV)

        def wait_read(eng, L, pair, t):
            mine = [by_dve(p, t) == by_dve(pair, t) for p in range(PAIRS)]
            eng.wait_ge((dve_out if by_dve(pair, t) else act_out)[t], sum(mine) * L + sum(mine[:pair + 1]))

        def wait_residual(eng, N):
            if N == 0:
                eng.wait_ge(h_in, 16)
            elif N % 2:
                for t in range(NT):
                    wait_read(eng, N // 2, PAIRS - 1, t)
            else:
                eng.wait_ge(h_new, (4, 4 + 4 * EXPERTS)[N // 2 - 1])

        def wait_out(eng, L, pair, t):
            if pair == PAIR_UKV and t == 1:
                pair, t = pair + 1, 0
            if t == 0:
                eng.wait_ge(out_made, OUTS * L + 1 + pair + 1)
            else:
                b, j = ((BLK_CU + pair, 2) if pair < PAIR_UQ else (BLK_UQ, pair - PAIR_UQ) if pair < PAIR_UKV else
                        (BLK_UKV, pair - PAIR_UKV - 1) if pair < PAIR_CONV else (BLK_CONV + pair - PAIR_CONV, 2))
                eng.wait_ge(used[j], MIX[L] + b + 1)

        def wait_pair_free(eng, L, pair, t):
            if pair >= 2:
                wait_read(eng, L, pair - 2, t)

        def expert_round(eng, r, step):
            def turn(p, last):
                for x in range(2):
                    final = last and x == 1
                    for i in range(2, EXPERT):
                        step(2 * p + x, i, x, gather=not final, back=False, ahead=not (final and i == EXPERT - 1))
                    if not final:
                        for i in range(2):
                            step(2 * p + x + 1, i, 1 - x, gather=False, back=i == 1, ahead=True)

            for i in range(2):
                step(0, i, 0, gather=False, back=False, ahead=True)
            with eng.Fori(0, EXPERTS // 2 - 1) as p:
                turn(p, False)
            turn(EXPERTS // 2 - 1, True)

        def second_round(eng, round_of, after=None):
            eng.wait_ge(flag_made, 1)
            over = eng.value_load(flag[0:1, 0:1], min_val=0, max_val=1)
            with eng.If(over > 0):
                round_of(1)
                if after is not None:
                    after()

        block = ctx.enter_context(nc.Block())

        @block.sync
        def _(sp):
            loaded_reg = sp.alloc_register("loaded")

            def load(b, j, first, parts, settled=False):
                at_span_start = isinstance(b, int) and b == first
                before = {FFN[0]: MIX[0], MIX[1]: FFN[0], FFN[1]: MIX[1]}.get(first) if at_span_start else first
                loaded = raw_value(b - 1, j, before) if settled or b >= 1 else None
                if not isinstance(b, int):
                    sp.reg_mov(loaded_reg, loaded)
                    loaded = sp.snap(loaded_reg)
                if settled or b >= 2:
                    sp.wait_ge(lo_made[j], b - 1)
                if settled or b >= 1:
                    sp.wait_ge(raw_in[j], loaded)
                for dst, src in parts:
                    sp.dma_start(dst, src).then_inc(raw_in[j], 16)

            def slot(b, j, n, width):
                return raw[:, b % 2, j, 0:n * width].rearrange("p (c n) -> p c n", n=width)

            def slab(b, first, w, col, width=NB):
                for j, (c0, n) in enumerate(G_CHUNKS):
                    load(b, j, first, [(slot(b, j, n, width), w[:, c0:c0 + n, col:col + width])])

            def chunks(w):
                return w.rearrange("(c p) n -> p c n", p=P)

            def gate_up(b, i, first, w_gate, w_up, settled):
                for j in range(2):
                    dst = raw[:, b % 2, j, :].rearrange("p (c w n) -> p c w n", w=2, n=HB)
                    load(b, j, first, [(dst[:, :, n, :], w[:, 4 * j:4 * j + 4, ds(i * HB, HB)])
                                       for n, w in enumerate((w_gate, w_up))], settled)

            def down(b, i, first, w_down):
                load(b, 2, first, [(slot(b, 2, HC, D), w_down[:, ds(i * HC, HC), :])], True)

            def ffn(F, first, n, w_gate, w_up, w_down):
                gate_up(F, 0, first, w_gate, w_up, True)
                with sp.Fori(1, n) as i:
                    gate_up(F + i, i, first, w_gate, w_up, True)
                    down(F + i - 1, i - 1, first, w_down)
                down(F + n - 1, n - 1, first, w_down)

            sp.dma_start(h[:, :, :], x[0].rearrange("(t p) d -> p t d", p=P)).then_inc(h_in, 16)
            for L in range(DEPTH):
                B = MIX[L]
                w_in_c = chunks(w_in[L])
                slab(B + BLK_LAT, B, w_in_c, COL_LAT, LAT)
                for s, col in enumerate((COL_C, COL_C + NB, COL_U, COL_U + NB, COL_B, COL_B + NB)):
                    slab(B + BLK_CU + s, B, w_in_c, col)
                slab(B + BLK_GATE0, B, w_in_c, COL_G)
                for j in range(3):
                    b = B + BLK_UQ
                    load(b, j, B, [(slot(b, j, 2, NB), chunks(w_uq[L])[:, :, j * NB:(j + 1) * NB])])
                for j, (c0, n) in enumerate(((0, 2), (2, 1), (3, 1))):
                    b = B + BLK_UKV
                    load(b, j, B, [(raw[:, b % 2, j, 0:n * NB], w_ukv[L][:, c0 * NB:(c0 + n) * NB])])
                for u in range(2):
                    slab(B + BLK_CONV + u, B, chunks(w_conv_out[L]), u * NB)
                for g in range(1, 4):
                    slab(B + GATE_BLK[g], B, w_in_c, COL_G + g * NB)
                for u in range(2):
                    slab(B + BLK_ATT + u, B, chunks(w_attn_out[L]), u * NB)
                for u in range(2):
                    slab(B + BLK_MIX + u, B, chunks(w_mix_out[L]), u * NB)
                if L == 0:
                    ffn(FFN[0], FFN[0], DENSE, chunks(dense_w_gate[0]), chunks(dense_w_up[0]), chunks(dense_w_down[0]))
                else:
                    eg = moe_w_gate[0].rearrange("e (c p) n -> p (e c) n", p=P)
                    eu = moe_w_up[0].rearrange("e (c p) n -> p (e c) n", p=P)
                    ed = moe_w_down[0].rearrange("e (c p) n -> p (e c) n", p=P)

                    def expert_loads(r):
                        def step(e, i, x, gather, back, ahead):
                            b = FFN[1] + EXPERT * (EXPERTS * r + e) + i
                            parity = (FFN[1] + x * EXPERT + i) % 2
                            for j in range(2):
                                dst = raw[:, parity, j, :].rearrange("p (c w n) -> p c w n", w=2, n=HB)
                                load(b, j, FFN[1], [(dst[:, :, n, :], w[:, ds(e * KC + 4 * j, 4), i * HB:(i + 1) * HB])
                                                    for n, w in enumerate((eg, eu))], True)
                            if isinstance(e, int) and e == 0 and i == 0:
                                return
                            expert_down(b - 1, e, i - 1, 1 - parity)
                            if not ahead:
                                expert_down(b, e, i, parity)

                        def expert_down(b, e, i, parity):
                            load(b, 2, FFN[1], [(raw[:, parity, 2, :].rearrange("p (c n) -> p c n", n=D),
                                                 ed[:, ds(e * HC * EXPERT + HC * i, HC), :])], True)

                        expert_round(sp, r, step)

                    expert_loads(0)
                    second_round(sp, expert_loads)
            for t in range(NT):
                sp.wait_ge(xs_made, 4 * NT + t + 1)
                sp.dma_start(out[0, t * P:(t + 1) * P, :], xs[:, t, :]).then_inc(stored, 16)
            sp.wait_ge(stored, 16 * NT)

        @block.gpsimd
        def _(pool):
            links = [0]

            def link(ins):
                links[0] += 1
                ins.then_inc(pool_link, 1)
                pool.wait_ge(pool_link, links[0])

            pool.dma_start(gain[:, :], norm_mix[0].partition_broadcast(P)).then_inc(gain_in, 16)
            for t in range(NT):
                pool.dma_start(pos_i[:, t:t + 1], positions[0, t * P:(t + 1) * P].rearrange("(p o) -> p o", o=1)).then_inc(pos_in, 16)
            link(pool.memset(ident[:, :], 0.0))
            pool.affine_select(out=ident[:, :], in_=ident[:, :], compare_op=ALU.not_equal, fill=1.0, base=0,
                               pattern=[[-1, P]], channel_multiplier=1).then_inc(ident_made, 1)
            pool.memset(minus_half, -0.5)
            link(pool.memset(mask[:, :], 0.0))
            pool.memset(mask[0:CHUNK, CHUNK:P], MASKED)
            pool.memset(mask[0:CHUNK, 2 * P + CHUNK:3 * P], MASKED)
            pool.memset(lat_scale[:, 0:2], 1.0 / Q_LORA)
            pool.memset(lat_scale[:, 2:4], 1.0 / KV_LORA)
            inv_freq = np.float32(THETA) ** (-np.arange(0, ROPE, 2, dtype=np.float32) / np.float32(ROPE))
            for n in range(RH):
                last = pool.memset(freq[:, n:n + 1], float(inv_freq[n]))
            last.then_inc(consts_made, 1)

            def norm_root(N, next_gain):
                pool.wait_ge(sq_act, N + 1)
                pool.wait_ge(sq_dve, N + 1)
                link(pool.tensor_scalar(var, sq_sum, 1.0 / D, EPS, ALU.mult, ALU.add))
                pool.tensor_tensor(rstd, var, minus_half[:, 0:2], ALU.pow).then_inc(rstd_made, 1)
                if next_gain is not None:
                    pool.wait_ge(xs_made, 2 * N + 2)
                    pool.dma_start(gain[:, :], next_gain.partition_broadcast(P)).then_inc(gain_in, 16)

            norm_root(0, None)
            for L in range(DEPTH):
                taps = CONV_K * KC
                pool.dma_start(rowc[L * taps:(L + 1) * taps, :], conv_w[L].rearrange("k o (c p) -> (k o c) p", p=P)).then_inc(rows_in, 16)
                r = DEPTH * taps + L * LC
                pool.dma_start(rowc[r:r + 2, :], norm_q[L].rearrange("(c p) -> c p", p=P)).then_inc(rows_in, 16)
                pool.dma_start(rowc[r + 2:r + 3, :], norm_kv[L].rearrange("(c p) -> c p", p=P)).then_inc(rows_in, 16)
            pool.dma_start(rwt[:, :].rearrange("p (c e) -> p c e", e=EXPERTS),
                           router_w[0].rearrange("(c p) e -> p c e", p=P)).then_inc(router_in, 16)
            pool.dma_start(gates[:, 0, :], b_gate[0].partition_broadcast(P)).then_inc(bias_in, 16)
            pool.dma_start(gates[:, 1, :], b_gate[0].partition_broadcast(P)).then_inc(bias_in, 16)
            for L in range(DEPTH):
                if L:
                    norm_root(2 * L, None)
                pool.wait_ge(lat_squared, 4 * (L + 1))
                link(pool.tensor_tensor(lat_var, lat_sq, lat_scale, ALU.mult))
                link(pool.tensor_scalar(lat_var, lat_var, EPS, None, ALU.add))
                pool.tensor_tensor(lat_rstd, lat_var, minus_half, ALU.pow).then_inc(lat_rstd_made, 1)
                pool.wait_ge(o_made, HEADS * (L + 1))
                pool.dma_start(gain[:, :], norm_ffn[L].partition_broadcast(P)).then_inc(gain_in, 16)
                if L == 1:
                    pool.iota(iota_i[:, :], pattern=[[1, S]], base=0, channel_multiplier=0).then_inc(iota_made, 1)
                    link(pool.memset(ones[:, :], 1.0))
                    pool.affine_select(out=tri[:, :], in_=ones[:, :], compare_op=ALU.is_ge, fill=0.0, base=0,
                                       pattern=[[1, P]], channel_multiplier=-1).then_inc(iota_made, 1)
                norm_root(2 * L + 1, norm_mix[1] if L == 0 else norm_final)
                if L == 0:
                    pool.wait_ge(m_made, 4)
                    for t in range(NT):
                        pool.dma_start(gates[:, t, :], b_gate[1].partition_broadcast(P)).then_inc(bias_in, 16)
            norm_root(4, None)

        @block.scalar
        def _(act):
            def hi(b, j, n, first, settled=False):
                act.wait_ge(raw_in[j], raw_value(b, j, first))
                if settled or b >= 1:
                    act.wait_ge(used[j], b)
                act.activation(w_hi[:, j, 0:n], raw[:, b % 2, j, 0:n], ACT.Copy).then_inc(hi_made[j], 1)

            def his(L, b):
                first = MIX[L] if b < MIXER else FFN[L]
                for j in range(3 if b < MIXER else 2):
                    hi(MIX[L] + b, j, mixer_sizes(b)[j], first)

            def square_tile(N):
                wait_residual(act, N)
                act.activation(xs[:, 0, :], h[:, 0, :], ACT.Square, accum_out=sq_sum[:, 0:1]).then_inc(sq_act, 1)

            def transposed_hi(use, dst, banks=range(4)):
                for n in banks:
                    act.wait_ge(tr_made, 4 * use + n + 1)
                    act.activation(dst[:, 2 * n:2 * n + 2, :], bank[B_T + n][:, :].rearrange("p (c s) -> p c s", s=S),
                                   ACT.Copy).then_inc(tr_hi, 1)

            def out_copy(L, pair, dst):
                for t in range(NT):
                    wait_out(act, L, pair, t)
                    act.activation(dst(t), bank[2 * (pair % 2) + t][:, :], ACT.Copy).then_inc(act_out[t], 1)

            def mixer(L):
                B = MIX[L]
                square_tile(2 * L)
                if L == 0:
                    his(0, BLK_LAT)
                else:
                    hi(B, 2, LAT_SIZES[2], B)
                transposed_hi(4 * L, aT_hi)
                if L == 0:
                    act.wait_ge(angle_made, 1)
                    act.activation(ang[:, 2:4, :, :], ang[:, 0:2, :, :], ACT.Sin).then_inc(sines_made, 1)
                his(L, BLK_CU)
                for t in range(NT):
                    act.wait_ge((out_made, used[2])[t], (OUTS * L + 1, MIX[L] + BLK_LAT + 1)[t])
                    for n, (a, b) in enumerate(((0, Q_LORA), (Q_LORA, Q_LORA + KV_LORA))):
                        act.activation(mixed[:, t, a:b], bank[B_LAT + t][:, a:b], ACT.Square,
                                       accum_out=lat_sq[:, 2 * n + t:2 * n + t + 1]).then_inc(lat_squared, 1)
                for t in range(NT):
                    act.activation(mixed[:, t, LAT - ROPE:LAT], bank[B_LAT + t][:, LAT - ROPE:LAT], ACT.Copy).then_inc(lat_scaled, 1)
                act.wait_ge(lat_rstd_made, L + 1)
                for t in range(NT):
                    for n, (a, b) in enumerate(((0, Q_LORA), (Q_LORA, Q_LORA + KV_LORA))):
                        act.activation(mixed[:, t, a:b], bank[B_LAT + t][:, a:b], ACT.Copy,
                                       scale=lat_rstd[:, 2 * n + t:2 * n + t + 1]).then_inc(lat_scaled, 1)
                for p in range(6):
                    if p < 5:
                        his(L, BLK_CU + p + 1)
                    else:
                        for j in range(2):
                            hi(B + BLK_GATE0, j, SLAB_SIZES[j], B)
                    out_copy(L, PAIR_CU + p, lambda t: proj[:, p // 2, t, p % 2 * NB:(p % 2 + 1) * NB])
                    if p == 1:
                        for c in range(LC):
                            act.wait_ge(lat_tr, 2 * L + (1 if c < 2 else 2))
                            act.activation(lT_hi[:, c, :], bank[B_LT + c // 2][:, c % 2 * S:(c % 2 + 1) * S], ACT.Copy,
                                           scale=cols[:, DEPTH * CONV_K * KC + L * LC + c:][:, 0:1]).then_inc(lat_hi, 1)
                    if p == 4:
                        for n in range(4):
                            act.wait_ge(z_tr, 4 * L + n + 1)
                            act.activation(zT[:, 2 * n:2 * n + 2, :], bank[B_T + n][:, :].rearrange("p (c s) -> p c s", s=S),
                                           ACT.Copy).then_inc(z_in, 1)
                hi(B + BLK_GATE0, 2, SLAB_SIZES[2], B)
                hi(B + BLK_UQ, 0, UQ_SIZES[0], B)
                for n in range(4):
                    act.wait_ge(prod_made, 4 * L + n + 1)
                    act.activation(bT_hi[:, 2 * n:2 * n + 2, :], acc[:, 2 * n:2 * n + 2, :], ACT.Copy).then_inc(prod_hi, 1)
                for j in (1, 2):
                    hi(B + BLK_UQ, j, UQ_SIZES[j], B)
                act.wait_ge(prod_lo, 4 * (L + 1))
                for j in range(3):
                    hi(B + BLK_UKV, j, UKV_SIZES[j], B)
                    out_copy(L, PAIR_UQ + j, lambda t: q[:, t, j * NB:(j + 1) * NB])
                for c in range(4):
                    wait_out(act, L, PAIR_UKV + c, 1)
                    src = bank[2 * ((PAIR_UKV + c) % 2) + 1][:, :].rearrange("p (h d) -> p h d", d=NOPE + VD)
                    act.activation(k[:, 1, :].rearrange("p (h d) -> p h d", d=QK)[:, 4 * c:4 * c + 4, 0:NOPE],
                                   src[:, :, 0:NOPE], ACT.Copy).then_inc(kv_act, 1)
                    act.activation(v[:, 1, :].rearrange("p (h d) -> p h d", d=VD)[:, 4 * c:4 * c + 4, :],
                                   src[:, :, NOPE:], ACT.Copy).then_inc(act_out[1], 1)
                    if c:
                        j = c - 1
                        hi(B + BLK_CONV, j, SLAB_SIZES[j], B)
                for u in range(2):
                    his(L, BLK_CONV + u + 1)
                    if u == 0:
                        act.wait_ge(heads_ready, 6 * (L + 1))
                    out_copy(L, PAIR_CONV + u, lambda t: mixed[:, t, u * NB:(u + 1) * NB])
                for n in range(HEADS + 3):
                    if n < HEADS:
                        act.wait_ge(qk_tr, HEADS * L + n + 1)
                        if n:
                            act.wait_ge(s_made, HEADS * L + n)
                        act.activation(qkT[0:QK, :], bank[B_QK][0:QK, :], ACT.Copy).then_inc(qk_in, 1)
                    if 1 <= n <= HEADS:
                        act.wait_ge(max_made, 2 * (HEADS * L + n))
                        if n >= 2:
                            act.wait_ge(p_tr, HEADS * L + n - 1)
                            act.wait_ge(inv_made, HEADS * L + n - 1)
                        act.activation(p_buf[:, 0:P], s_buf[:, 0:P], ACT.Exp, bias=neg_max[:, 0:1],
                                       accum_out=row_sum[:, 0:1]).then_inc(p_made, 1)
                        act.activation(p_buf[:, P:3 * P], s_buf[:, P:3 * P], ACT.Exp, bias=neg_max[:, 1:2],
                                       accum_out=row_sum[:, 1:2]).then_inc(p_made, 1)
                    if 2 <= n <= HEADS + 1:
                        act.wait_ge(p_tr, HEADS * L + n - 1)
                        if n >= 3:
                            act.wait_ge(o_made, HEADS * L + n - 2)
                        act.activation(pT[:, :], bank[B_PT][:, 0:3 * P], ACT.Copy).then_inc(p_in, 1)
                    if n == HEADS + 2:
                        transposed_hi(4 * L + 1, aT_hi, (0, 1))
                    if n in GRANULE_AHEAD:
                        b, j = GRANULE_AHEAD[n]
                        hi(B + b, j, SLAB_SIZES[j], B)
                transposed_hi(4 * L + 1, aT_hi, (2, 3))
                for t in range(NT):
                    wait_read(act, L, GATE_PAIR[3], t)
                    act.activation(gates[:, t, :], gates[:, t, :], ACT.Sigmoid).then_inc(gate_made, 1)
                his(L, BLK_ATT + 1)
                hi(B + BLK_MIX, 0, SLAB_SIZES[0], B)
                transposed_hi(4 * L + 2, bT_hi, (0, 1))
                for j in (1, 2):
                    hi(B + BLK_MIX, j, SLAB_SIZES[j], B)
                transposed_hi(4 * L + 2, bT_hi, (2, 3))
                his(L, BLK_MIX + 1)
                his(L, MIXER)

            def silu(F, fb):
                for t in range(NT):
                    act.wait_ge((gu_made, used[1])[t], (fb + 1, F + 1)[t])
                    act.activation(sg[:, t, :], bank[B_GU + t][:, 0:HB], ACT.Silu).then_inc(silu_made, 1)

            def hidden_hi(fb):
                act.wait_ge(hid_tr, fb + 1)
                act.activation(hT_hi[:, :, :], bank[B_HT][:, :].rearrange("p (c s) -> p c s", s=S), ACT.Copy).then_inc(hT_hi_made, 1)

            def ffn_step(F, fb, first, ahead):
                hi(F - 1, 2, SLOT, first, True)
                hidden_hi(fb - 1)
                if ahead:
                    hi(F + 1, 0, SLOT, first, True)
                    silu(F, fb)
                    hi(F + 1, 1, SLOT, first, True)

            mixer(0)
            act.wait_ge(router_in, 16)
            act.activation(rw_hi[:, :], rwt[:, :], ACT.Copy).then_inc(rw_hi_made, 1)
            square_tile(1)
            transposed_hi(3, aT_hi)
            F = FFN[0]
            hi(F + 1, 0, SLOT, F, True)
            silu(F, 0)
            hi(F + 1, 1, SLOT, F, True)
            with act.Fori(1, DENSE - 1) as i:
                ffn_step(F + i, i, F, True)
            ffn_step(F + DENSE - 1, DENSE - 1, F, False)
            hi(MIX[1], 0, LAT_SIZES[0], MIX[1])
            silu(F + DENSE - 1, DENSE - 1)
            hi(MIX[1], 1, LAT_SIZES[1], MIX[1])
            hi(F + DENSE - 1, 2, SLOT, F, True)
            hidden_hi(DENSE - 1)
            mixer(1)
            square_tile(3)
            transposed_hi(7, aT_hi)
            for t in range(NT):
                act.activation(xn_hi[:, t, :], xs[:, t, :], ACT.Copy).then_inc(xn_hi_made, 1)
            act.wait_ge(lmax_made, 1)
            act.activation(rt[:, :, 5, 0:1], rt[:, :, 4, 0:1], ACT.Exp).then_inc(lexp_made, 1)

            def gathered_hi(E, x):
                act.wait_ge(x_hi_tr, E + 1)
                for n, b in enumerate(B_XHI):
                    act.activation(aT_hi[:, 4 * n:4 * n + 4, x * P:(x + 1) * P], bank[b][:, :].rearrange("p (c s) -> p c s", s=P),
                                   ACT.Copy).then_inc(x_hi_in, 1)

            def sel_transposed(E, x):
                act.wait_ge(selT_tr, E + 1)
                act.activation(selT[:, x, :], bank[B_SELT][:, 0:S], ACT.Copy).then_inc(selT_in, 1)

            def output_hi(F, E):
                act.wait_ge(used[2], F + EXPERT)
                for u in range(2):
                    act.activation(y_hi[:, u * NB:(u + 1) * NB], bank[u][:, :], ACT.Copy).then_inc(y_hi_made, 1)

            def experts(r):
                F0, E0, fb0 = FFN[1] + EXPERT * EXPERTS * r, EXPERTS * r, DENSE + EXPERT * EXPERTS * r
                gathered_hi(E0, 0)
                sel_transposed(E0, 0)
                for j in range(2 if r else 0):
                    expert_hi(F0, j, 0, 0)

                def step(e, i, x, gather, back, ahead):
                    b, fb = F0 + EXPERT * e + i, fb0 + EXPERT * e + i
                    if not (isinstance(e, int) and e == 0 and i == 0):
                        expert_hi(b - 1, 2, x, i - 1)
                        if back:
                            output_hi(F0 + EXPERT * (e - 1), E0 + e - 1)
                        hidden_hi_1(fb - 1)
                    if gather and i == 4:
                        gathered_hi(E0 + e + 1, 1 - x)
                    if gather and i == 5:
                        sel_transposed(E0 + e + 1, 1 - x)
                    if ahead:
                        expert_hi(b + 1, 0, x, i + 1)
                    expert_silu(b)
                    if ahead:
                        expert_hi(b + 1, 1, x, i + 1)
                    else:
                        expert_hi(b, 2, x, i)
                        hidden_hi_1(fb)
                        output_hi(F0 + EXPERT * e, E0 + e)

                expert_round(act, r, step)

            def expert_hi(b, j, x, i):
                act.wait_ge(raw_in[j], raw_value(b, j, FFN[1]))
                act.wait_ge(used[j], b)
                act.activation(w_hi[:, j, :], raw[:, (FFN[1] + x * EXPERT + i) % 2, j, :], ACT.Copy).then_inc(hi_made[j], 1)

            def expert_silu(b):
                act.wait_ge(used[1], b + 1)
                act.activation(sg[:, 0, :], bank[B_GU][:, 0:HB], ACT.Silu).then_inc(silu_made, 1)

            def hidden_hi_1(fb):
                act.wait_ge(hid_tr, fb + 1)
                act.activation(hT_hi[:, :, 0:P], bank[B_HT][:, 0:HC * P].rearrange("p (c s) -> p c s", s=P), ACT.Copy).then_inc(hT_hi_made, 1)

            experts(0)
            second_round(act, experts, lambda: act.wait_ge(h_new, 4 + 8 * EXPERTS))
            square_tile(4)

        @block.vector
        def _(dve):
            links = [0]

            def link(*ins):
                for i in ins:
                    links[0] += 1
                    i.then_inc(dve_link, 1)
                dve.wait_ge(dve_link, links[0])

            def lo(b, j, n):
                dve.wait_ge(hi_made[j], b + 1)
                dve.tensor_tensor(w_lo[:, j, 0:n], raw[:, b % 2, j, 0:n], w_hi[:, j, 0:n].bitcast(F32),
                                  ALU.subtract).then_inc(lo_made[j], 1)

            def los(L, b):
                for j in range(3 if b < MIXER else 2):
                    lo(MIX[L] + b, j, mixer_sizes(b)[j])

            def square_tile(N):
                wait_residual(dve, N)
                dve.tensor_tensor_reduce(out=xs[:, 1, :], in0=h[:, 1, :], in1=h[:, 1, :], scale=1.0, scalar=0.0,
                                         op0=ALU.mult, op1=ALU.add, accum_out=sq_sum[:, 1:2]).then_inc(sq_dve, 1)

            def scale_tokens(N):
                dve.wait_ge(rstd_made, N + 1)
                dve.wait_ge(gain_in, 16 * (N + 1))
                for t in range(NT):
                    dve.scalar_tensor_tensor(out=xs[:, t, :], in0=h[:, t, :], scalar=rstd[:, t:t + 1], in1=gain[:, :],
                                             op0=ALU.mult, op1=ALU.mult).then_inc(xs_made, 1)

            def transposed_lo(use, dst, dst_hi, banks=range(4)):
                for n in banks:
                    dve.wait_ge(tr_hi, 4 * use + n + 1)
                    dve.tensor_tensor(dst[:, 2 * n:2 * n + 2, :], bank[B_T + n][:, :].rearrange("p (c s) -> p c s", s=S),
                                      dst_hi[:, 2 * n:2 * n + 2, :].bitcast(F32), ALU.subtract).then_inc(tr_lo, 1)

            def heads_of(t, d):
                return t.rearrange("p (h d) -> p h d", d=d)

            def rotary_table():
                dve.wait_ge(pos_in, 16 * NT)
                dve.wait_ge(consts_made, 1)
                link(dve.tensor_copy(posf[:, :], pos_i[:, :]))
                link(*[dve.tensor_scalar(turns[:, 0, t, :], freq[:, :], posf[:, t:t + 1], None, ALU.mult) for t in range(NT)])
                magic = 1.5 * 2.0 ** 23
                two_pi = 2.0 * np.pi
                part1 = float(np.float32(6.28125))
                part2 = float(np.floor((two_pi - part1) * 2.0 ** 20) / 2.0 ** 20)
                part3 = float(np.float32(two_pi - part1 - part2))
                link(dve.tensor_scalar(turns[:, 1], turns[:, 0], 1.0 / two_pi, magic, ALU.mult, ALU.add))
                link(dve.tensor_scalar(turns[:, 2], turns[:, 1], magic, None, ALU.subtract))
                for part in (part1, part2, part3):
                    link(dve.scalar_tensor_tensor(out=turns[:, 0], in0=turns[:, 2], scalar=-part, in1=turns[:, 0],
                                                  op0=ALU.mult, op1=ALU.add))
                link(dve.tensor_scalar(ang[:, 0], turns[:, 0], 3.1415925, -3.1415925, ALU.min, ALU.max))
                dve.tensor_scalar(ang[:, 1], ang[:, 0], 0.5, None, ALU.mult).then_inc(angle_made, 1)
                dve.wait_ge(sines_made, 1)
                dve.tensor_copy(sin[:, :, :], ang[:, 2])
                link(dve.tensor_tensor(turns[:, 3], ang[:, 3], ang[:, 3], ALU.mult))
                link(dve.tensor_scalar(cos[:, :, :], turns[:, 3], -2.0, 1.0, ALU.mult, ALU.add))

            def channel_constants():
                dve.wait_ge(cols_tr, 1)
                dve.tensor_copy(cols[:, :], bank[7][:, 0:NCOL]).then_inc(cols_made, 1)

            def mixer(L):
                B = MIX[L]

                def add_bias(g):
                    for t in range(NT):
                        wait_out(dve, L, GATE_PAIR[g], t)
                        part = gates[:, t, g * NB:(g + 1) * NB]
                        dve.tensor_tensor(part, part, bank[2 * (GATE_PAIR[g] % 2) + t][:, :], ALU.add).then_inc(dve_out[t], 1)

                square_tile(2 * L)
                if L == 0:
                    los(0, BLK_LAT)
                else:
                    lo(B, 2, LAT_SIZES[2])
                scale_tokens(2 * L)
                transposed_lo(4 * L, aT_lo, aT_hi)
                if L == 0:
                    rotary_table()
                los(L, BLK_CU)
                if L == 0:
                    channel_constants()
                dve.wait_ge(lat_scaled, 6 * L + 2)
                k1, k2 = mixed[:, :, LAT - ROPE:LAT - RH], mixed[:, :, LAT - RH:LAT]
                kt = [rope_k[:, n, :, :] for n in range(4)]
                link(dve.tensor_tensor(kt[0], k1, cos[:, :, :], ALU.mult), dve.tensor_tensor(kt[1], k2, sin[:, :, :], ALU.mult),
                     dve.tensor_tensor(kt[2], k1, sin[:, :, :], ALU.mult), dve.tensor_tensor(kt[3], k2, cos[:, :, :], ALU.mult))
                link(dve.tensor_tensor(k_rope[:, :, 0:RH], kt[0], kt[1], ALU.subtract),
                     dve.tensor_tensor(k_rope[:, :, RH:], kt[2], kt[3], ALU.add))
                for p in range(6):
                    los(L, BLK_CU + p + 1)
                    if p == 1:
                        for c in range(LC):
                            dve.wait_ge(lat_hi, LC * L + (2 if c < 2 else 3))
                            dve.scalar_tensor_tensor(out=lT_lo[:, c, :], in0=bank[B_LT + c // 2][:, c % 2 * S:(c % 2 + 1) * S],
                                                     scalar=cols[:, DEPTH * CONV_K * KC + L * LC + c:][:, 0:1],
                                                     in1=lT_hi[:, c, :].bitcast(F32), op0=ALU.mult,
                                                     op1=ALU.subtract).then_inc(lat_lo, 1)
                    if p == 3:
                        for t in range(NT):
                            wait_read(dve, L, PAIR_B - 1, t)
                            dve.tensor_tensor(proj[:, 0, t, :], proj[:, 0, t, :], proj[:, 1, t, :], ALU.mult).then_inc(z_made, 1)
                    if p == 4:
                        dve.wait_ge(z_in, 4 * L + 4)
                        tap = [[cols[:, (L * CONV_K + n) * KC + c:][:, 0:1] for c in range(KC)] for n in range(CONV_K)]
                        link(*[dve.tensor_scalar(acc[:, c, :], zT[:, c, :], tap[2][c], None, ALU.mult) for c in range(KC)])
                        for back in (1, 2):
                            link(*[dve.scalar_tensor_tensor(out=acc[:, c, back:], in0=zT[:, c, 0:S - back], scalar=tap[2 - back][c],
                                                            in1=acc[:, c, back:], op0=ALU.mult, op1=ALU.add) for c in range(KC)])
                lo(B + BLK_UQ, 0, UQ_SIZES[0])
                for n in range(4):
                    part = acc[:, 2 * n:2 * n + 2, :]
                    dve.wait_ge(b_tr, 4 * L + n + 1)
                    dve.tensor_tensor(part, part, bank[B_T + n][:, :].rearrange("p (c s) -> p c s", s=S), ALU.mult).then_inc(prod_made, 1)
                for n in range(4):
                    part = acc[:, 2 * n:2 * n + 2, :]
                    dve.wait_ge(prod_hi, 4 * L + n + 1)
                    dve.tensor_tensor(bT_lo[:, 2 * n:2 * n + 2, :], part, bT_hi[:, 2 * n:2 * n + 2, :].bitcast(F32),
                                      ALU.subtract).then_inc(prod_lo, 1)
                lo(B + BLK_UQ, 1, UQ_SIZES[1])
                dve.wait_ge(bias_in, 32 * (L + 1))
                add_bias(0)
                lo(B + BLK_UQ, 2, UQ_SIZES[2])
                for j in range(3):
                    lo(B + BLK_UKV, j, UKV_SIZES[j])
                for c in range(4):
                    wait_out(dve, L, PAIR_UKV + c, 0)
                    src = heads_of(bank[2 * ((PAIR_UKV + c) % 2)][:, :], NOPE + VD)
                    link(dve.tensor_copy(heads_of(k[:, 0, :], QK)[:, 4 * c:4 * c + 4, 0:NOPE], src[:, :, 0:NOPE]))
                    dve.tensor_copy(heads_of(v[:, 0, :], VD)[:, 4 * c:4 * c + 4, :], src[:, :, NOPE:]).then_inc(dve_out[0], 1)
                    if c:
                        lo(B + BLK_CONV, c - 1, SLAB_SIZES[c - 1])
                for t in range(NT):
                    dve.tensor_copy(heads_of(k[:, t, :], QK)[:, :, NOPE:],
                                    k_rope[:, t, :].unsqueeze(1).to_broadcast([P, HEADS, ROPE])).then_inc(heads_ready, 1)
                    wait_read(dve, L, PAIR_UKV - 1, t)
                    q1, q2 = heads_of(q[:, t, :], QK)[:, :, NOPE:NOPE + RH], heads_of(q[:, t, :], QK)[:, :, NOPE + RH:]
                    c_b, s_b = (m[:, t, :].unsqueeze(1).to_broadcast([P, HEADS, RH]) for m in (cos, sin))
                    r = [rope_t[:, n, :, :] for n in range(4)]
                    if t:
                        dve.wait_ge(heads_ready, 6 * L + 3)
                    link(dve.tensor_tensor(r[0], q1, c_b, ALU.mult), dve.tensor_tensor(r[1], q2, s_b, ALU.mult),
                         dve.tensor_tensor(r[2], q1, s_b, ALU.mult), dve.tensor_tensor(r[3], q2, c_b, ALU.mult))
                    dve.tensor_tensor(q1, r[0], r[1], ALU.subtract).then_inc(heads_ready, 1)
                    dve.tensor_tensor(q2, r[2], r[3], ALU.add).then_inc(heads_ready, 1)
                los(L, BLK_CONV + 1)
                los(L, BLK_GATE)
                for n in range(HEADS + 3):
                    if 2 <= n <= HEADS + 1:
                        dve.wait_ge(p_made, 2 * (HEADS * L + n - 1))
                        if n >= 4:
                            dve.wait_ge(o_in, 2 * (HEADS * L + n - 3))
                        dve.reciprocal(row_inv[n % 2], row_sum).then_inc(inv_made, 1)
                    if 1 <= n <= HEADS:
                        dve.wait_ge(s_made, HEADS * L + n)
                        if n >= 2:
                            dve.wait_ge(p_made, 2 * (HEADS * L + n - 1))
                        link(dve.scalar_tensor_tensor(out=s_buf[:, :], in0=bank[B_S][:, 0:3 * P], scalar=SCALE, in1=mask[:, :],
                                                      op0=ALU.mult, op1=ALU.add))
                        dve.reduce_max(neg_max[:, 0:1], s_buf[:, 0:P], AX, negate=True).then_inc(max_made, 1)
                        dve.reduce_max(neg_max[:, 1:2], s_buf[:, P:3 * P], AX, negate=True).then_inc(max_made, 1)
                    if n >= 3:
                        dve.wait_ge(o_made, HEADS * L + n - 2)
                        dve.wait_ge(inv_made, HEADS * L + n - 2)
                        for t in range(NT):
                            dve.tensor_scalar(xs[:, t, (n - 3) * VD:(n - 2) * VD], bank[B_O][:, t * VD:(t + 1) * VD],
                                              row_inv[(n - 1) % 2][:, t:t + 1], None, ALU.mult).then_inc(o_in, 1)
                    if n == HEADS + 2:
                        transposed_lo(4 * L + 1, aT_lo, aT_hi, (0, 1))
                    if n and n % GATE_SLOTS == 0:
                        add_bias(n // GATE_SLOTS)
                    if n in GRANULE_AHEAD:
                        b, j = GRANULE_AHEAD[n]
                        lo(B + b, j, SLAB_SIZES[j])
                transposed_lo(4 * L + 1, aT_lo, aT_hi, (2, 3))
                for t in range(NT):
                    dve.wait_ge(gate_made, NT * L + t + 1)
                    wait_read(dve, L, PAIR_CONV + 1, t)
                    link(dve.tensor_tensor(mixed[:, t, :], mixed[:, t, :], gates[:, t, 0:D], ALU.mult))
                los(L, BLK_ATT + 1)
                for u in range(2):
                    for t in range(NT):
                        wait_out(dve, L, PAIR_ATT + u, t)
                        g_b, m = gates[:, t, D + u * NB:D + (u + 1) * NB], mixed[:, t, u * NB:(u + 1) * NB]
                        dve.tensor_tensor(g_b, g_b, bank[2 * ((PAIR_ATT + u) % 2) + t][:, :], ALU.mult).then_inc(dve_out[t], 1)
                        wait_read(dve, L, PAIR_ATT + u, t)
                        dve.tensor_tensor(m, m, g_b, ALU.add).then_inc(m_made, 1)
                    if u == 0:
                        lo(B + BLK_MIX, 0, SLAB_SIZES[0])
                        transposed_lo(4 * L + 2, bT_lo, bT_hi, (0, 1))
                        lo(B + BLK_MIX, 1, SLAB_SIZES[1])
                lo(B + BLK_MIX, 2, SLAB_SIZES[2])
                transposed_lo(4 * L + 2, bT_lo, bT_hi, (2, 3))
                los(L, BLK_MIX + 1)
                for u in range(2):
                    for t in range(NT):
                        wait_out(dve, L, PAIR_MIX + u, t)
                        part = h[:, t, u * NB:(u + 1) * NB]
                        dve.tensor_tensor(part, part, bank[2 * ((PAIR_MIX + u) % 2) + t][:, :], ALU.add).then_inc(dve_out[t], 1)
                    if u == 0:
                        lo(B + MIXER, 0, SLOT)

            def hidden(fb):
                for t in range(NT):
                    dve.wait_ge(silu_made, 2 * fb + t + 1)
                    dve.tensor_tensor(hid[:, t, :], sg[:, t, :], bank[B_GU + t][:, HB:2 * HB], ALU.mult).then_inc(hid_made, 1)

            def hidden_lo(fb):
                dve.wait_ge(hT_hi_made, fb + 1)
                dve.tensor_tensor(hT_lo[:, :, :], bank[B_HT][:, :].rearrange("p (c s) -> p c s", s=S),
                                  hT_hi[:, :, :].bitcast(F32), ALU.subtract).then_inc(hT_lo_made, 1)

            def ffn_step(F, fb, ahead):
                lo(F - 1, 2, SLOT)
                hidden_lo(fb - 1)
                if ahead:
                    lo(F + 1, 0, SLOT)
                    hidden(fb)
                    lo(F + 1, 1, SLOT)

            mixer(0)
            dve.wait_ge(rw_hi_made, 1)
            dve.tensor_tensor(rw_lo[:, :], rwt[:, :], rw_hi[:, :].bitcast(F32), ALU.subtract).then_inc(rw_lo_made, 1)
            square_tile(1)
            scale_tokens(1)
            transposed_lo(3, aT_lo, aT_hi)
            F = FFN[0]
            lo(F, 1, SLOT)
            lo(F + 1, 0, SLOT)
            hidden(0)
            lo(F + 1, 1, SLOT)
            with dve.Fori(1, DENSE - 1) as i:
                ffn_step(F + i, i, True)
            ffn_step(F + DENSE - 1, DENSE - 1, False)
            lo(MIX[1], 0, LAT_SIZES[0])
            hidden(DENSE - 1)
            lo(MIX[1], 1, LAT_SIZES[1])
            lo(F + DENSE - 1, 2, SLOT)
            hidden_lo(DENSE - 1)
            for t in range(NT):
                dve.wait_ge((down_made, used[2])[t], (1, F + DENSE)[t])
                for u in range(2):
                    part = h[:, t, u * NB:(u + 1) * NB]
                    dve.tensor_tensor(part, part, bank[2 * t + u][:, :], ALU.add).then_inc(h_new, 1)
            mixer(1)
            square_tile(3)
            scale_tokens(3)
            transposed_lo(7, aT_lo, aT_hi)
            lg, mx, ix, ixf, df, w1, w2, pick = (rt[:, :, n, :] for n in range(8))
            iota_e, chose1, chose2 = (rt[:, :, n, :] for n in (8, 9, 10))
            dve.wait_ge(logitsT_made, 1)
            dve.tensor_copy(hid[0:EXPERTS, 0, :], bank[2][0:EXPERTS, 0:S]).then_inc(logitsT_in, 1)
            dve.wait_ge(logits_made, 1)
            link(*[dve.tensor_copy(lg[:, t, :], bank[t][:, 0:EXPERTS]) for t in range(NT)])
            link(*[dve.memset(iota_e[:, :, n:n + 1], float(n)) for n in range(EXPERTS)])
            link(*[dve.max(mx[:, t, :], lg[:, t, :]) for t in range(NT)])
            link(*[dve.max_index(ix[:, t, :].bitcast(U32), mx[:, t, :], lg[:, t, :]) for t in range(NT)])
            link(dve.tensor_copy(ixf, ix.bitcast(U32)))
            dve.tensor_tensor(df[:, :, 0:1], mx[:, :, 1:2], mx[:, :, 0:1], ALU.subtract).then_inc(lmax_made, 1)
            for t in range(NT):
                dve.tensor_scalar(chose1[:, t, :], iota_e[:, t, :], ixf[:, t, 0:1], None, ALU.is_equal).then_inc(dve_link, 1)
                dve.tensor_scalar(chose2[:, t, :], iota_e[:, t, :], ixf[:, t, 1:2], None, ALU.is_equal).then_inc(dve_link, 1)
            links[0] += 2 * NT
            dve.wait_ge(dve_link, links[0])
            dve.tensor_tensor(chosen[:, :, :], chose1, chose2, ALU.add).then_inc(chosen_made, 1)
            dve.wait_ge(lexp_made, 1)
            link(dve.tensor_scalar(w1[:, :, 1:2], w1[:, :, 0:1], 1.0, None, ALU.add))
            link(dve.reciprocal(w1[:, :, 2:3], w1[:, :, 1:2]))
            link(dve.tensor_tensor(w1[:, :, 3:4], w1[:, :, 0:1], w1[:, :, 2:3], ALU.mult))
            for t in range(NT):
                link(dve.tensor_scalar(pick[:, t, :], iota_e[:, t, :], ixf[:, t, 0:1], w1[:, t, 2:3], ALU.is_equal, ALU.mult),
                     dve.tensor_scalar(w2[:, t, :], iota_e[:, t, :], ixf[:, t, 1:2], w1[:, t, 3:4], ALU.is_equal, ALU.mult))
                link(dve.tensor_tensor(expert_gate[:, t, :], pick[:, t, :], w2[:, t, :], ALU.add))
            dve.wait_ge(iota_made, 2)
            link(dve.tensor_copy(slot_no[:, :], iota_i[:, :]))
            dve.wait_ge(chosen_made, 1)
            dve.wait_ge(ranks_made, 1)
            for t in range(NT):
                link(dve.tensor_tensor(token_slot[:, t, :], chosen[:, t, :], bank[t][:, EXPERTS:2 * EXPERTS], ALU.mult))
            link(dve.tensor_scalar(token_slot[:, :, :], token_slot[:, :, :], -1.0, None, ALU.add))

            def expert_lo(b, j, x, i):
                dve.wait_ge(hi_made[j], b + 1)
                dve.tensor_tensor(w_lo[:, j, :], raw[:, (FFN[1] + x * EXPERT + i) % 2, j, :], w_hi[:, j, :].bitcast(F32),
                                  ALU.subtract).then_inc(lo_made[j], 1)

            def choose(r, e, E, x):
                for t in range(NT):
                    dve.tensor_scalar(sel[:, x, t, :], slot_no[:, r * P:(r + 1) * P], token_slot[:, t, ds(e, 1)], None,
                                      ALU.is_equal).then_inc(sel_made, 1)

            def split_tokens():
                for t in range(NT):
                    dve.wait_ge(xn_hi_made, t + 1)
                    dve.tensor_tensor(xn_lo[:, t, :], xs[:, t, :], xn_hi[:, t, :].bitcast(F32), ALU.subtract).then_inc(xn_lo_made, 1)
                link(dve.tensor_copy(counts[:, :], bank[0][:, 2 * EXPERTS:3 * EXPERTS]))
                link(dve.reduce_max(small[:, 40:41], counts[:, :], AX))
                link(dve.tensor_scalar(small[:, 41:42], small[:, 40:41], float(P), None, ALU.is_gt))
                dve.tensor_copy(flag[:, :], small[:, 41:42]).then_inc(flag_made, 1)

            def gathered_lo(E, x):
                dve.wait_ge(x_lo_tr, E + 1)
                for n, b in enumerate(B_XLO):
                    dve.tensor_copy(aT_lo[:, 4 * n:4 * n + 4, x * P:(x + 1) * P],
                                    bank[b][:, :].rearrange("p (c s) -> p c s", s=P)).then_inc(x_lo_in, 1)

            def output_lo(E):
                for u in range(2):
                    dve.wait_ge(y_hi_made, 2 * E + u + 1)
                    dve.tensor_tensor(y_lo[:, u * NB:(u + 1) * NB], bank[u][:, :], y_hi[:, u * NB:(u + 1) * NB].bitcast(F32),
                                      ALU.subtract).then_inc(y_lo_made, 1)

            def add_outputs(e, E):
                for t in range(NT):
                    dve.wait_ge(back_made, 2 * E + t + 1)
                    for u in range(2):
                        part = h[:, t, u * NB:(u + 1) * NB]
                        dve.scalar_tensor_tensor(out=part, in0=bank[B_BACK[t][u]][:, :], scalar=expert_gate[:, t, ds(e, 1)],
                                                 in1=part, op0=ALU.mult, op1=ALU.add).then_inc(h_new, 1)

            def hidden_1(fb):
                dve.wait_ge(silu_made, fb + DENSE + 1)
                dve.tensor_tensor(hid[:, 0, :], sg[:, 0, :], bank[B_GU][:, HB:2 * HB], ALU.mult).then_inc(hid_made, 1)

            def hidden_lo_1(fb):
                dve.wait_ge(hT_hi_made, fb + 1)
                dve.tensor_tensor(hT_lo[:, :, 0:P], bank[B_HT][:, 0:HC * P].rearrange("p (c s) -> p c s", s=P),
                                  hT_hi[:, :, 0:P].bitcast(F32), ALU.subtract).then_inc(hT_lo_made, 1)

            def experts(r):
                F0, E0, fb0 = FFN[1] + EXPERT * EXPERTS * r, EXPERTS * r, DENSE + EXPERT * EXPERTS * r
                choose(r, 0, E0, 0)
                if r == 0:
                    split_tokens()
                    expert_lo(F0, 1, 0, 0)
                gathered_lo(E0, 0)
                for j in range(2 if r else 0):
                    expert_lo(F0, j, 0, 0)

                def step(e, i, x, gather, back, ahead):
                    b, fb = F0 + EXPERT * e + i, fb0 + EXPERT * e + i
                    if not (isinstance(e, int) and e == 0 and i == 0):
                        expert_lo(b - 1, 2, x, i - 1)
                        if back:
                            output_lo(E0 + e - 1)
                        hidden_lo_1(fb - 1)
                    if gather and i == 2:
                        choose(r, e + 1, E0 + e + 1, 1 - x)
                    if gather and i == 4:
                        gathered_lo(E0 + e + 1, 1 - x)
                    if ahead:
                        expert_lo(b + 1, 0, x, i + 1)
                    hidden_1(fb)
                    if ahead:
                        expert_lo(b + 1, 1, x, i + 1)
                        if back:
                            add_outputs(e - 1, E0 + e - 1)
                    else:
                        expert_lo(b, 2, x, i)
                        hidden_lo_1(fb)
                        output_lo(E0 + e)
                        add_outputs(e, E0 + e)

                expert_round(dve, r, step)

            experts(0)
            second_round(dve, experts, lambda: dve.wait_ge(h_new, 4 + 8 * EXPERTS))
            square_tile(4)
            scale_tokens(4)

        @block.tensor
        def _(pe):
            def product(dst, x_hi, x_lo, b_hi, b_lo, start, stop):
                pe.matmul(dst, x_hi, b_hi, start=start, stop=False)
                pe.matmul(dst, x_hi, b_lo, start=False, stop=False)
                return pe.matmul(dst, x_lo, b_hi, start=False, stop=stop)

            def tile(m, c, t):
                return m[:, c, t * P:(t + 1) * P]

            def w(j, c, n, width, m):
                return m[:, j, c * width:c * width + n]

            def slab(L, b, pair, x_hi, x_lo, use=None, after_granule_0=None):
                for j, (c0, nc_) in enumerate(G_CHUNKS):
                    if use is not None:
                        pe.wait_ge(tr_lo, 4 * use + (c0 + nc_ + 1) // 2)
                    pe.wait_ge(lo_made[j], MIX[L] + b + 1)
                    for t in range(NT):
                        if j == 0:
                            wait_pair_free(pe, L, pair, t)
                        dst = bank[2 * (pair % 2) + t][:, :]
                        for c in range(nc_):
                            last = product(dst, tile(x_hi, c0 + c, t), tile(x_lo, c0 + c, t), w(j, c, NB, NB, w_hi),
                                           w(j, c, NB, NB, w_lo), c0 + c == 0, c0 + c == KC - 1)
                        if j == 2 and t == 0:
                            last.then_inc(out_made, 1)
                    last.then_inc(used[j], 1)
                    if j == 0 and after_granule_0 is not None:
                        after_granule_0()

            def transpose_tokens(src, use, halves=(0, 1)):
                for u in halves:
                    for n in (2 * u, 2 * u + 1):
                        for c in (2 * n, 2 * n + 1):
                            for t in range(NT):
                                last = pe.transpose(bank[B_T + n][:, (c % 2) * S + t * P:(c % 2) * S + (t + 1) * P],
                                                    src(t)[:, c * P:(c + 1) * P], ident[:, :])
                        last.then_inc(use, 1)

            def transpose_normed(N):
                for t in range(NT):
                    pe.wait_ge(xs_made, NT * N + t + 1)
                    for n in range(4):
                        for c in (2 * n, 2 * n + 1):
                            last = pe.transpose(bank[B_T + n][:, (c % 2) * S + t * P:(c % 2) * S + (t + 1) * P],
                                                xs[:, t, c * P:(c + 1) * P], ident[:, :])
                        if t == NT - 1:
                            last.then_inc(tr_made, 1)

            def mixer(L):
                transpose_normed(2 * L)
                for j, (c0, nc_) in enumerate(G_CHUNKS):
                    pe.wait_ge(tr_lo, 16 * L + (c0 + nc_ + 1) // 2)
                    pe.wait_ge(lo_made[j], MIX[L] + BLK_LAT + 1)
                    for t in range(NT):
                        for c in range(nc_):
                            last = product(bank[B_LAT + t][:, 0:LAT], tile(aT_hi, c0 + c, t), tile(aT_lo, c0 + c, t),
                                           w(j, c, LAT, LAT, w_hi), w(j, c, LAT, LAT, w_lo), c0 + c == 0, c0 + c == KC - 1)
                        if j == 2 and t == 0:
                            last.then_inc(out_made, 1)
                    last.then_inc(used[j], 1)
                if L == 0:
                    pe.wait_ge(rows_in, 16 * 3 * DEPTH)
                    pe.transpose(bank[7][:, 0:NCOL], rowc[:, :], ident[0:NCOL, 0:NCOL]).then_inc(cols_tr, 1)
                for p in range(6):
                    if p == 5:
                        pe.wait_ge(z_made, NT * (L + 1))
                        pe.wait_ge(lat_scaled, 6 * (L + 1))
                        pe.wait_ge(lat_lo, LC * (L + 1))
                        transpose_tokens(lambda t: proj[:, 0, t, :], z_tr)
                    slab(L, BLK_CU + p, PAIR_CU + p, aT_hi, aT_lo)
                    if p == 1:
                        pe.wait_ge(lat_scaled, 6 * (L + 1))
                        if L == 0:
                            pe.wait_ge(cols_made, 1)
                        for c in range(LC):
                            for t in range(NT):
                                last = pe.transpose(bank[B_LT + c // 2][:, c % 2 * S + t * P:c % 2 * S + (t + 1) * P],
                                                    mixed[:, t, c * P:(c + 1) * P], ident[:, :])
                            if c:
                                last.then_inc(lat_tr, 1)

                def transpose_b():
                    for t in range(NT):
                        wait_read(pe, L, PAIR_B + 1, t)
                    pe.wait_ge(z_in, 4 * (L + 1))
                    transpose_tokens(lambda t: proj[:, 2, t, :], b_tr)

                slab(L, BLK_GATE0, PAIR_GATE0, aT_hi, aT_lo, after_granule_0=transpose_b)
                for j in range(3):
                    pe.wait_ge(lo_made[j], MIX[L] + BLK_UQ + 1)
                    for t in range(NT):
                        wait_pair_free(pe, L, PAIR_UQ + j, t)
                        for c in range(2):
                            last = product(bank[2 * ((PAIR_UQ + j) % 2) + t][:, :], tile(lT_hi, c, t), tile(lT_lo, c, t),
                                           w(j, c, NB, NB, w_hi), w(j, c, NB, NB, w_lo), c == 0, c == 1)
                        if t == 0:
                            last.then_inc(out_made, 1)
                    last.then_inc(used[j], 1)
                for c, (j, n) in enumerate(((0, 0), (0, 1), (1, 0), (2, 0))):
                    pe.wait_ge(lo_made[j], MIX[L] + BLK_UKV + 1)
                    for t in range(NT):
                        wait_pair_free(pe, L, PAIR_UKV + c, t)
                        last = product(bank[2 * ((PAIR_UKV + c) % 2) + t][:, :], tile(lT_hi, 2, t), tile(lT_lo, 2, t),
                                       w(j, n, NB, NB, w_hi), w(j, n, NB, NB, w_lo), True, True)
                        if t == 0:
                            last.then_inc(out_made, 1)
                    if c:
                        last.then_inc(used[j], 1)
                pe.wait_ge(prod_lo, 4 * (L + 1))
                for u in range(2):
                    slab(L, BLK_CONV + u, PAIR_CONV + u, bT_hi, bT_lo)
                for n in range(HEADS + 3):
                    if n < 3 * GATE_SLOTS:
                        g = n // GATE_SLOTS
                        b, s = BLK_GATE + g, n % GATE_SLOTS
                        for c in range((4 * s + 2) // 3, (4 * s + 6) // 3):
                            j = c // 3
                            if c % 3 == 0:
                                pe.wait_ge(lo_made[j], MIX[L] + b + 1)
                            for t in range(NT):
                                if c == 0:
                                    wait_pair_free(pe, L, PAIR_GATE + g, t)
                                last = product(bank[2 * ((PAIR_GATE + g) % 2) + t][:, :], tile(aT_hi, c, t), tile(aT_lo, c, t),
                                               w(j, c % 3, NB, NB, w_hi), w(j, c % 3, NB, NB, w_lo), c == 0, c == KC - 1)
                                if c == KC - 1 and t == 0:
                                    last.then_inc(out_made, 1)
                            if c in (2, 5, 7):
                                last.then_inc(used[j], 1)
                    if n < HEADS:
                        if n == 0:
                            pe.wait_ge(heads_ready, 6 * (L + 1))
                            pe.wait_ge(kv_act, 4 * (L + 1))
                            for t in range(NT):
                                wait_read(pe, L, PAIR_UKV + 3, t)
                        else:
                            pe.wait_ge(qk_in, HEADS * L + n)
                        for m, src in enumerate((q, k)):
                            for t in range(NT):
                                last = pe.transpose(bank[B_QK][0:QK, m * S + t * P:m * S + (t + 1) * P],
                                                    src[:, t, n * QK:(n + 1) * QK], ident[:, :])
                        last.then_inc(qk_tr, 1)
                    if 1 <= n <= HEADS:
                        pe.wait_ge(qk_in, HEADS * L + n)
                        if n >= 2:
                            pe.wait_ge(max_made, 2 * (HEADS * L + n - 1))
                        for t in range(NT):
                            last = pe.matmul(bank[B_S][:, t * P:(2 * t + 1) * P], qkT[0:QK, t * P:(t + 1) * P],
                                             qkT[0:QK, S:S + (t + 1) * P], start=True, stop=True)
                        last.then_inc(s_made, 1)
                    if 2 <= n <= HEADS + 1:
                        pe.wait_ge(p_made, 2 * (HEADS * L + n - 1))
                        if n >= 3:
                            pe.wait_ge(p_in, HEADS * L + n - 2)
                        for m in range(3):
                            last = pe.transpose(bank[B_PT][:, m * P:(m + 1) * P], p_buf[:, m * P:(m + 1) * P], ident[:, :])
                        last.then_inc(p_tr, 1)
                    if n == HEADS + 2:
                        pe.wait_ge(qk_in, HEADS * (L + 1))
                        pe.wait_ge(max_made, 2 * HEADS * (L + 1))
                        pe.wait_ge(o_in, 2 * (HEADS * L + HEADS // 2))
                        transpose_tokens(lambda t: xs[:, t, :], tr_made, (0,))
                    if n >= 3:
                        pe.wait_ge(p_in, HEADS * L + n - 2)
                        if n >= 4:
                            pe.wait_ge(o_in, 2 * (HEADS * L + n - 3))
                        for t, (m, kt, start, stop) in zip((0, 1, 1), ((0, 0, True, True), (1, 0, True, False), (2, 1, False, True))):
                            last = pe.matmul(bank[B_O][:, t * VD:(t + 1) * VD], pT[:, m * P:(m + 1) * P],
                                             v[:, kt, (n - 3) * VD:(n - 2) * VD], start=start, stop=stop)
                        last.then_inc(o_made, 1)

                def half(src, u, sem_ready, value):
                    def transposes():
                        pe.wait_ge(sem_ready, value)
                        transpose_tokens(src, tr_made, (u,))
                    return transposes

                slab(L, BLK_ATT, PAIR_ATT, aT_hi, aT_lo, 4 * L + 1, half(lambda t: xs[:, t, :], 1, o_in, 2 * HEADS * (L + 1)))
                slab(L, BLK_ATT + 1, PAIR_ATT + 1, aT_hi, aT_lo, None, half(lambda t: mixed[:, t, :], 0, m_made, 4 * L + 2))
                slab(L, BLK_MIX, PAIR_MIX, bT_hi, bT_lo, 4 * L + 2, half(lambda t: mixed[:, t, :], 1, m_made, 4 * L + 4))
                slab(L, BLK_MIX + 1, PAIR_MIX + 1, bT_hi, bT_lo)

            def gate_up(F, fb, j):
                pe.wait_ge(lo_made[j], F + 1)
                for t in range(NT):
                    if j == 0 and not (isinstance(fb, int) and fb == 0):
                        pe.wait_ge(hid_made, 2 * fb - 1 + t)
                    for c in range(4):
                        last = product(bank[B_GU + t][:, :], tile(aT_hi, 4 * j + c, t), tile(aT_lo, 4 * j + c, t),
                                       w(j, c, NB, NB, w_hi), w(j, c, NB, NB, w_lo), j == 0 and c == 0, j == 1 and c == 3)
                    if j == 1 and t == 0:
                        last.then_inc(gu_made, 1)
                last.then_inc(used[j], 1)

            def hidden_transposes(fb):
                pe.wait_ge(hid_made, 2 * fb + 2)
                for c in range(HC):
                    for t in range(NT):
                        last = pe.transpose(bank[B_HT][:, c * S + t * P:c * S + (t + 1) * P], hid[:, t, c * P:(c + 1) * P], ident[:, :])
                last.then_inc(hid_tr, 1)

            def down(F, fb, start, stop):
                pe.wait_ge(hT_lo_made, fb + 1)
                pe.wait_ge(lo_made[2], F + 1)
                for t in range(NT):
                    for u in range(2):
                        for c in range(HC):
                            last = product(bank[2 * t + u][:, :], tile(hT_hi, c, t), tile(hT_lo, c, t),
                                           w_hi[:, 2, c * D + u * NB:c * D + (u + 1) * NB], w_lo[:, 2, c * D + u * NB:c * D + (u + 1) * NB],
                                           start and c == 0, stop and c == HC - 1)
                    if stop and t == 0:
                        last.then_inc(down_made, 1)
                last.then_inc(used[2], 1)

            def ffn_step(F, fb, start):
                gate_up(F, fb, 0)
                hidden_transposes(fb - 1)
                gate_up(F, fb, 1)
                down(F - 1, fb - 1, start, False)

            pe.wait_ge(ident_made, 1)
            mixer(0)
            F = FFN[0]
            transpose_normed(1)
            for j in range(2):
                pe.wait_ge(tr_lo, 12 + 2 * j + 2)
                gate_up(F, 0, j)
            ffn_step(F + 1, 1, True)
            with pe.Fori(2, DENSE) as i:
                ffn_step(F + i, i, False)
            hidden_transposes(DENSE - 1)
            down(F + DENSE - 1, DENSE - 1, False, True)
            pe.wait_ge(h_new, 4)
            mixer(1)
            transpose_normed(3)
            pe.wait_ge(rw_lo_made, 1)
            for c in range(KC):
                pe.wait_ge(tr_lo, 28 + c // 2 + 1)
                e8 = slice(c * EXPERTS, (c + 1) * EXPERTS)
                last = product(bank[2][0:EXPERTS, 0:S], rw_hi[:, e8], rw_lo[:, e8], aT_hi[:, c, :], aT_lo[:, c, :],
                               c == 0, c == KC - 1)
            last.then_inc(logitsT_made, 1)
            pe.wait_ge(logitsT_in, 1)
            for t in range(NT):
                last = pe.transpose(bank[t][:, 0:EXPERTS], hid[0:EXPERTS, 0, t * P:(t + 1) * P], ident[0:EXPERTS, 0:EXPERTS])
            last.then_inc(logits_made, 1)
            pe.wait_ge(chosen_made, 1)
            pe.wait_ge(iota_made, 2)
            ranks = slice(EXPERTS, 2 * EXPERTS)
            pe.matmul(bank[0][:, ranks], tri[:, :], chosen[:, 0, :], start=True, stop=True)
            pe.matmul(bank[1][:, ranks], ones[:, :], chosen[:, 0, :], start=True, stop=False)
            pe.matmul(bank[1][:, ranks], tri[:, :], chosen[:, 1, :], start=False, stop=True)
            for t in range(NT):
                last = pe.matmul(bank[0][:, 2 * EXPERTS:3 * EXPERTS], ones[:, :], chosen[:, t, :], start=t == 0, stop=t == 1)
            last.then_inc(ranks_made, 1)

            def gather(E, x, part, src, made):
                for n, b in enumerate(part):
                    for c in range(4):
                        for t in range(NT):
                            last = pe.matmul(bank[b][:, c * P:(c + 1) * P], src[:, t, (4 * n + c) * P:(4 * n + c + 1) * P],
                                             sel[:, x, t, :], start=t == 0, stop=t == 1)
                last.then_inc(made, 1)

            def transpose_sel(E, x):
                pe.wait_ge(x_hi_in, 2 * E + 2)
                for t in range(NT):
                    last = pe.transpose(bank[B_SELT][:, t * P:(t + 1) * P], sel[:, x, t, :].bitcast(F32), ident[:, :])
                last.then_inc(selT_tr, 1)

            def bring_back(E, x):
                pe.wait_ge(selT_in, E + 1)
                pe.wait_ge(y_lo_made, 2 * E + 2)
                for t in range(NT):
                    for u in range(2):
                        dst = bank[B_BACK[t][u]][:, :]
                        pe.matmul(dst, selT[:, x, t * P:(t + 1) * P], y_hi[:, u * NB:(u + 1) * NB], start=True, stop=False)
                        last = pe.matmul(dst, selT[:, x, t * P:(t + 1) * P], y_lo[:, u * NB:(u + 1) * NB], start=False, stop=True)
                    last.then_inc(back_made, 1)

            def expert_gate_up(b, fb, x, j):
                pe.wait_ge(lo_made[j], b + 1)
                if j == 0:
                    pe.wait_ge(hid_made, fb + DENSE)
                for c in range(4):
                    last = product(bank[B_GU][:, :], tile(aT_hi, 4 * j + c, x), tile(aT_lo, 4 * j + c, x),
                                   w(j, c, NB, NB, w_hi), w(j, c, NB, NB, w_lo), j == 0 and c == 0, j == 1 and c == 3)
                last.then_inc(used[j], 1)

            def expert_transposes(fb):
                pe.wait_ge(hid_made, fb + DENSE + 1)
                for c in range(HC):
                    last = pe.transpose(bank[B_HT][:, c * P:(c + 1) * P], hid[:, 0, c * P:(c + 1) * P], ident[:, :])
                last.then_inc(hid_tr, 1)

            def expert_down(b, fb, i):
                pe.wait_ge(hT_lo_made, fb + 1)
                pe.wait_ge(lo_made[2], b + 1)
                for u in range(2):
                    for c in range(HC):
                        last = product(bank[u][:, :], tile(hT_hi, c, 0), tile(hT_lo, c, 0),
                                       w_hi[:, 2, c * D + u * NB:c * D + (u + 1) * NB], w_lo[:, 2, c * D + u * NB:c * D + (u + 1) * NB],
                                       i == 0 and c == 0, i == EXPERT - 1 and c == HC - 1)
                last.then_inc(used[2], 1)

            def experts(r):
                F0, E0, fb0 = FFN[1] + EXPERT * EXPERTS * r, EXPERTS * r, DENSE + EXPERT * EXPERTS * r
                pe.wait_ge(sel_made, 2 * E0 + 2)
                pe.wait_ge(xn_hi_made, NT)
                if r:
                    pe.wait_ge(h_new, 4 + 4 * EXPERTS)
                gather(E0, 0, B_XHI, xn_hi, x_hi_tr)
                pe.wait_ge(xn_lo_made, NT)
                gather(E0, 0, B_XLO, xn_lo, x_lo_tr)
                transpose_sel(E0, 0)
                pe.wait_ge(x_lo_in, 2 * E0 + 2)

                def step(e, i, x, gather_next, back, ahead):
                    b, fb, E = F0 + EXPERT * e + i, fb0 + EXPERT * e + i, E0 + e
                    first = isinstance(e, int) and e == 0 and i == 0
                    if gather_next and i == 3:
                        pe.wait_ge(sel_made, 2 * (E + 1) + 2)
                        pe.wait_ge(h_new, 4 + 4 * E)
                    if i == 0 and not first:
                        pe.wait_ge(x_lo_in, 2 * E + 2)
                    expert_gate_up(b, fb, x, 0)
                    if gather_next and i == 3:
                        gather(E + 1, 1 - x, B_XHI, xn_hi, x_hi_tr)
                    if not first:
                        expert_transposes(fb - 1)
                    expert_gate_up(b, fb, x, 1)
                    if gather_next and i == 3:
                        gather(E + 1, 1 - x, B_XLO, xn_lo, x_lo_tr)
                    if gather_next and i == 4:
                        transpose_sel(E + 1, 1 - x)
                    if back:
                        bring_back(E - 1, 1 - x)
                    if not first:
                        expert_down(b - 1, fb - 1, (i - 1) % EXPERT)
                    if not ahead:
                        expert_transposes(fb)
                        expert_down(b, fb, i)
                        bring_back(E, x)

                expert_round(pe, r, lambda e, i, x, gather, back, ahead: step(e, i, x, gather, back, ahead))

            experts(0)
            second_round(pe, experts)


_INS = ["x", "positions", "norm_mix", "w_in", "b_gate", "conv_w", "w_conv_out", "norm_q", "norm_kv", "w_uq", "w_ukv",
        "w_attn_out", "w_mix_out", "norm_ffn", "dense_w_gate", "dense_w_up", "dense_w_down", "router_w",
        "moe_w_gate", "moe_w_up", "moe_w_down", "norm_final"]


def kernel(**inputs):
    import numpy as _np
    import concourse.bacc as _bacc
    from concourse import mybir as _mybir
    from concourse.bass_utils import run_bass_kernel_spmd as _run

    nc = _bacc.Bacc("TRN2", target_bir_lowering=False, num_devices=1)
    arrays, args = {}, []
    for name in _INS:
        a = _np.ascontiguousarray(inputs[name])
        arrays[f"in_{name}"] = a
        args.append(nc.dram_tensor(f"in_{name}", a.shape, _mybir.dt.from_np(a.dtype), kind="ExternalInput").ap())
    args.append(nc.dram_tensor("out_0", (1, S, D), F32, kind="ExternalOutput").ap())
    build_trunk(nc, *args)
    r = _run(nc, [arrays], core_ids=[0])
    return r.results[0]["out_0"]
```
